# Optimizing a Trainium2 kernel written in Bass

```python
import jax, jax.numpy as jnp
from jax import lax
import numpy as np
import math

D_MODEL = 1024
BATCH = 1
SEQ = 1024
DEPTH = 1

MIX_WIDTH = D_MODEL
RWKV_WIDTH = MIX_WIDTH // 2
RWKV_HEAD_DIM = 64
RWKV_HEADS = RWKV_WIDTH // RWKV_HEAD_DIM
RWKV_DECAY_LORA = 64
RWKV_AAA_LORA = 64
RWKV_GATE_LORA = 128
RWKV_GN_EPS = 64e-5
GLA_WIDTH = MIX_WIDTH - RWKV_WIDTH
GLA_HEADS = 4
GLA_DV = GLA_WIDTH // GLA_HEADS
GLA_DK = GLA_DV // 2
GLA_KEY_WIDTH = GLA_HEADS * GLA_DK
GLA_GATE_LORA = 16
GLA_GATE_TEMP = 16.0
GLA_CHUNK = 64
CONV_WIDTH = 3
PLE_DIM = 256
D_FF = -(-8 * D_MODEL // (3 * 256)) * 256
NORM_EPS = 1e-6

RWKV_SPLITS = (RWKV_WIDTH, 2 * RWKV_WIDTH, 3 * RWKV_WIDTH,
               3 * RWKV_WIDTH + 2 * RWKV_DECAY_LORA,
               3 * RWKV_WIDTH + 2 * RWKV_DECAY_LORA + RWKV_AAA_LORA)
RWKV_IN_WIDTH = RWKV_SPLITS[-1] + RWKV_GATE_LORA
GLA_SPLITS = (2 * GLA_KEY_WIDTH + GLA_WIDTH, 2 * GLA_KEY_WIDTH + 2 * GLA_WIDTH)
GLA_IN_WIDTH = GLA_SPLITS[-1] + 2 * GLA_GATE_LORA
IN_WIDTH = RWKV_IN_WIDTH + GLA_IN_WIDTH


def rms_norm(x, w, eps=NORM_EPS):
    xf = x.astype(jnp.float32)
    y = xf * lax.rsqrt(jnp.mean(xf * xf, axis=-1, keepdims=True) + eps)
    return (y * w.astype(jnp.float32)).astype(x.dtype)

def centred_shift(z):
    zp = jnp.pad(z, ((0, 0), (1, 1), (0, 0)))
    return 0.5 * (zp[:, :-2] + zp[:, 2:])

def centred_dwconv(z, w):
    pad = (w.shape[0] - 1) // 2
    return lax.conv_general_dilated(z, w.astype(z.dtype), window_strides=(1,),
                                    padding=[(pad, pad)],
                                    dimension_numbers=('NWC', 'WIO', 'NWC'),
                                    feature_group_count=z.shape[-1])

def rwkv7_scan(r, decay, k, v, kk, b, reverse):
    B, T, H, N = r.shape
    xs = tuple(jnp.moveaxis(t, 1, 0) for t in (r, decay, k, v, kk, b))

    def step(S, inp):
        r_t, w_t, k_t, v_t, kk_t, b_t = inp
        sa = jnp.einsum('bhij,bhj->bhi', S, -kk_t)
        S = (S * w_t[:, :, None, :] + sa[..., None] * b_t[:, :, None, :]
             + v_t[..., None] * k_t[:, :, None, :])
        return S, jnp.einsum('bhij,bhj->bhi', S, r_t)

    S0 = jnp.zeros((B, H, N, N), r.dtype)
    _, y = lax.scan(step, S0, xs, reverse=reverse)
    return jnp.moveaxis(y, 0, 1)

def rwkv7_mixer(z, w0, w_up, a0, a_up, g_up, k_k, k_a, r_k, ln_w, ln_b, out_dtype):
    B, T, _ = z.shape
    z = z.astype(jnp.float32)
    r, k, v, w_lo, a_lo, g_lo = jnp.split(z, RWKV_SPLITS, axis=-1)
    w_lo = w_lo.reshape(B, T, 2, RWKV_DECAY_LORA)
    w_log = -jax.nn.softplus(-(w0 + jnp.einsum('btdr,drc->btdc', jnp.tanh(w_lo), w_up))) - 0.5
    decay = jnp.exp(-jnp.exp(w_log))
    a = jax.nn.sigmoid(a0 + a_lo @ a_up)
    g = jax.nn.sigmoid(g_lo) @ g_up

    def heads(t):
        return t.reshape(B, T, RWKV_HEADS, RWKV_HEAD_DIM)

    kk = heads(k * k_k)
    kk = kk * lax.rsqrt(jnp.maximum(jnp.sum(kk * kk, axis=-1, keepdims=True), 1e-24))
    k = k * (1.0 + (a - 1.0) * k_a)
    r_h, k_h, v_h, a_h = heads(r), heads(k), heads(v), heads(a)
    b_h = kk * a_h
    y = (rwkv7_scan(r_h, heads(decay[:, :, 0]), k_h, v_h, kk, b_h, False)
         + rwkv7_scan(r_h, heads(decay[:, :, 1]), k_h, v_h, kk, b_h, True))
    mu = jnp.mean(y, axis=-1, keepdims=True)
    var = jnp.mean(jnp.square(y - mu), axis=-1, keepdims=True)
    y = heads(((y - mu) * lax.rsqrt(var + RWKV_GN_EPS)).reshape(B, T, RWKV_WIDTH) * ln_w + ln_b)
    bonus = jnp.sum(r_h * k_h * r_k, axis=-1, keepdims=True) * v_h
    y = (y + bonus).reshape(B, T, RWKV_WIDTH)
    return (y * g).astype(out_dtype)

def gla_chunked(q, k, v, log_a):
    B, H, T, DK = q.shape
    DV = v.shape[-1]
    nc = T // GLA_CHUNK

    def to_chunks(t):
        return t.reshape(B, H, nc, GLA_CHUNK, t.shape[-1]).transpose(2, 0, 1, 3, 4)

    qc, kc, vc = to_chunks(q), to_chunks(k), to_chunks(v)
    bc = jnp.cumsum(to_chunks(log_a), axis=-2)
    mask = jnp.tril(jnp.ones((GLA_CHUNK, GLA_CHUNK), dtype=bool))[:, :, None]

    def step(S, inp):
        q_c, k_c, v_c, b_c = inp
        o_inter = jnp.einsum('bhcd,bhde->bhce', q_c * jnp.exp(b_c), S)
        diff = b_c[:, :, :, None, :] - b_c[:, :, None, :, :]
        dmat = jnp.exp(jnp.where(mask, diff, -jnp.inf))
        scores = jnp.einsum('bhid,bhjd,bhijd->bhij', q_c, k_c, dmat)
        o_intra = jnp.einsum('bhij,bhje->bhie', scores, v_c)
        b_last = b_c[:, :, -1:, :]
        S = (S * jnp.exp(b_last[:, :, 0, :])[..., None]
             + jnp.einsum('bhcd,bhce->bhde', k_c * jnp.exp(b_last - b_c), v_c))
        return S, o_inter + o_intra

    S0 = jnp.zeros((B, H, DK, DV), q.dtype)
    _, o = lax.scan(step, S0, (qc, kc, vc, bc))
    return o.transpose(1, 2, 0, 3, 4).reshape(B, H, T, DV)

def gla_mixer(z, conv_w, a_up, a_b, norm_w, out_dtype):
    B, T, _ = z.shape
    z = z.astype(jnp.float32)
    qkv, g, a_lo = jnp.split(z, GLA_SPLITS, axis=-1)
    qkv = jax.nn.silu(centred_dwconv(qkv, conv_w))
    q, k, v = jnp.split(qkv, (GLA_KEY_WIDTH, 2 * GLA_KEY_WIDTH), axis=-1)
    a_lo = a_lo.reshape(B, T, 2, GLA_GATE_LORA)
    log_a = jax.nn.log_sigmoid(jnp.einsum('btdr,drc->btdc', a_lo, a_up) + a_b) / GLA_GATE_TEMP

    def heads(t, d):
        return t.reshape(B, T, GLA_HEADS, d).transpose(0, 2, 1, 3)

    def flip(t):
        return jnp.flip(t, axis=2)

    q_h = heads(q, GLA_DK) * GLA_DK ** -0.5
    k_h = heads(k, GLA_DK)
    v_h = heads(v, GLA_DV)
    o_f = gla_chunked(q_h, k_h, v_h, heads(log_a[:, :, 0], GLA_DK))
    o_b = flip(gla_chunked(flip(q_h), flip(k_h), flip(v_h), flip(heads(log_a[:, :, 1], GLA_DK))))
    o = (o_f + o_b).transpose(0, 2, 1, 3)
    o = rms_norm(o, norm_w) * jax.nn.silu(g.reshape(B, T, GLA_HEADS, GLA_DV))
    return o.reshape(B, T, GLA_WIDTH).astype(out_dtype)

def first_inputs(seed: int = 0) -> dict:
    key = jax.random.key(seed)
    ks = jax.random.split(key, 32)
    L = DEPTH
    f32 = jnp.float32

    def nrm(k, shape, scale):
        return jax.random.normal(k, shape, f32) * scale

    def gain(k, shape):
        return 1.0 + 0.05 * jax.random.normal(k, shape, f32)

    return {
        'x': jax.random.normal(ks[0], (BATCH, SEQ, D_MODEL), f32),
        'p': jax.random.normal(ks[1], (DEPTH, BATCH, SEQ, PLE_DIM), f32),
        'norm_mix_pre': gain(ks[2], (L, D_MODEL)),
        'norm_mix_post': gain(ks[3], (L, D_MODEL)),
        'norm_ffn_pre': gain(ks[4], (L, D_MODEL)),
        'norm_ffn_post': gain(ks[5], (L, D_MODEL)),
        'norm_ple': gain(ks[6], (L, D_MODEL)),
        'w_in': nrm(ks[7], (L, D_MODEL, IN_WIDTH), D_MODEL ** -0.5),
        'rwkv_mu': jax.random.uniform(ks[8], (L, RWKV_IN_WIDTH), f32),
        'rwkv_w0': jax.random.uniform(ks[9], (L, 2, RWKV_WIDTH), f32, -6.0, -1.0),
        'rwkv_w_up': nrm(ks[10], (L, 2, RWKV_DECAY_LORA, RWKV_WIDTH), RWKV_DECAY_LORA ** -0.5),
        'rwkv_a0': nrm(ks[11], (L, RWKV_WIDTH), 0.3),
        'rwkv_a_up': nrm(ks[12], (L, RWKV_AAA_LORA, RWKV_WIDTH), 0.5 * RWKV_AAA_LORA ** -0.5),
        'rwkv_g_up': nrm(ks[13], (L, RWKV_GATE_LORA, RWKV_WIDTH), RWKV_GATE_LORA ** -0.5),
        'rwkv_k_k': 0.85 + 0.05 * jax.random.normal(ks[14], (L, RWKV_WIDTH), f32),
        'rwkv_k_a': gain(ks[15], (L, RWKV_WIDTH)),
        'rwkv_r_k': nrm(ks[16], (L, RWKV_HEADS, RWKV_HEAD_DIM), 0.1),
        'rwkv_ln_w': gain(ks[17], (L, RWKV_WIDTH)),
        'rwkv_ln_b': nrm(ks[18], (L, RWKV_WIDTH), 0.02),
        'gla_conv': nrm(ks[19], (L, CONV_WIDTH, 1, 2 * GLA_KEY_WIDTH + GLA_WIDTH), CONV_WIDTH ** -0.5),
        'gla_a_up': nrm(ks[20], (L, 2, GLA_GATE_LORA, GLA_KEY_WIDTH), GLA_GATE_LORA ** -0.5),
        'gla_a_b': 2.0 + 0.5 * jax.random.normal(ks[21], (L, 2, GLA_KEY_WIDTH), f32),
        'gla_norm': gain(ks[22], (L, GLA_DV)),
        'w_out': nrm(ks[23], (L, MIX_WIDTH, D_MODEL), MIX_WIDTH ** -0.5),
        'ffn_gate': nrm(ks[24], (L, D_MODEL, D_FF), D_MODEL ** -0.5),
        'ffn_up': nrm(ks[25], (L, D_MODEL, D_FF), D_MODEL ** -0.5),
        'ffn_down': nrm(ks[26], (L, D_FF, D_MODEL), D_FF ** -0.5),
        'ple_proj': nrm(ks[27], (L, PLE_DIM, D_MODEL), PLE_DIM ** -0.5),
        'ple_gate': nrm(ks[28], (L, D_MODEL, D_MODEL), D_MODEL ** -0.5),
        'ple_gate_b': nrm(ks[29], (L, D_MODEL), 0.02),
    }

def first_block(x, p, norm_mix_pre, norm_mix_post, norm_ffn_pre, norm_ffn_post, norm_ple,
              w_in, rwkv_mu, rwkv_w0, rwkv_w_up, rwkv_a0, rwkv_a_up, rwkv_g_up,
              rwkv_k_k, rwkv_k_a, rwkv_r_k, rwkv_ln_w, rwkv_ln_b,
              gla_conv, gla_a_up, gla_a_b, gla_norm, w_out,
              ffn_gate, ffn_up, ffn_down, ple_proj, ple_gate, ple_gate_b):
    h = x
    for i in range(DEPTH):
        xn = rms_norm(h, norm_mix_pre[i])
        z = xn @ w_in[i]
        z_rwkv, z_gla = z[..., :RWKV_IN_WIDTH], z[..., RWKV_IN_WIDTH:]
        z_rwkv = z_rwkv + rwkv_mu[i] * (centred_shift(z_rwkv) - z_rwkv)
        y_rwkv = rwkv7_mixer(z_rwkv, rwkv_w0[i], rwkv_w_up[i], rwkv_a0[i], rwkv_a_up[i],
                             rwkv_g_up[i], rwkv_k_k[i], rwkv_k_a[i], rwkv_r_k[i],
                             rwkv_ln_w[i], rwkv_ln_b[i], h.dtype)
        y_gla = gla_mixer(z_gla, gla_conv[i], gla_a_up[i], gla_a_b[i], gla_norm[i], h.dtype)
        y = jnp.concatenate([y_rwkv, y_gla], axis=-1) @ w_out[i]
        h = h + rms_norm(y, norm_mix_post[i])
        hn = rms_norm(h, norm_ffn_pre[i])
        f = (jax.nn.silu(hn @ ffn_gate[i]) * (hn @ ffn_up[i])) @ ffn_down[i]
        h = h + rms_norm(f, norm_ffn_post[i])
        e = p[i] @ ple_proj[i]
        gate = jax.nn.sigmoid(h @ ple_gate[i] + ple_gate_b[i])
        h = h + rms_norm(gate * e, norm_ple[i])
    return h


GRID_W = 64
CTX_LEN = 256
MIX_DIM = D_MODEL
ATT_DIM = MIX_DIM // 2
CONV_DIM = MIX_DIM - ATT_DIM
HEAD_DIM = 64
N_HEADS = ATT_DIM // HEAD_DIM
NA_ROWS = 8
NA_COLS = 16
CONV_WIDTH_2 = 31
D_FF_2 = 4 * D_MODEL
IN_PROJ_DIM = 3 * ATT_DIM + 2 * CONV_DIM
N_MOD = 6
ROPE_BASE = 10000.0
EPS = 1e-6


def rms_norm_2(x, g):
    xf = x.astype(jnp.float32)
    y = xf * lax.rsqrt(jnp.mean(xf * xf, axis=-1, keepdims=True) + EPS)
    return (y * g.astype(jnp.float32)).astype(x.dtype)

def modulate(h, shift, scale):
    return h * (1 + scale) + shift

def split_heads(t):
    b, l, _ = t.shape
    return t.reshape(b, l, N_HEADS, HEAD_DIM)

def split_proj(p):
    q = split_heads(p[..., :ATT_DIM])
    k = split_heads(p[..., ATT_DIM:2 * ATT_DIM])
    v = split_heads(p[..., 2 * ATT_DIM:3 * ATT_DIM])
    u = p[..., 3 * ATT_DIM:]
    return q, k, v, u

def rope_half(xh, pos):
    n_pairs = xh.shape[-1] // 2
    inv_freq = ROPE_BASE ** (-jnp.arange(n_pairs, dtype=jnp.float32) / n_pairs)
    ang = pos.astype(jnp.float32)[:, None] * inv_freq[None, :]
    cos = jnp.cos(ang)[None, :, None, :]
    sin = jnp.sin(ang)[None, :, None, :]
    x1 = xh[..., :n_pairs].astype(jnp.float32)
    x2 = xh[..., n_pairs:].astype(jnp.float32)
    return jnp.concatenate([x1 * cos - x2 * sin, x2 * cos + x1 * sin], axis=-1).astype(xh.dtype)

def axial_rope(x, row_pos, col_pos):
    half = HEAD_DIM // 2
    return jnp.concatenate([rope_half(x[..., :half], row_pos),
                            rope_half(x[..., half:], col_pos)], axis=-1)

def conformer_conv(u, kernel, bias, ln_g, ln_b):
    a, b = jnp.split(u, 2, axis=-1)
    h = a * jax.nn.sigmoid(b)
    pad = CONV_WIDTH_2 // 2
    h = lax.conv_general_dilated(h, kernel[:, None, :].astype(h.dtype), window_strides=(1,),
                                 padding=[(pad, pad)], dimension_numbers=('NWC', 'WIO', 'NWC'),
                                 feature_group_count=CONV_DIM) + bias
    hf = h.astype(jnp.float32)
    mu = jnp.mean(hf, axis=-1, keepdims=True)
    var = jnp.mean(jnp.square(hf - mu), axis=-1, keepdims=True)
    hn = (hf - mu) * lax.rsqrt(var + EPS) * ln_g + ln_b
    return jax.nn.silu(hn).astype(u.dtype)

def sq_relu_mlp(h, w1, w2):
    return jnp.square(jax.nn.relu(h @ w1)) @ w2

def context_attention(q, k, v):
    b, lc = q.shape[0], q.shape[1]
    s = jnp.einsum('bqhd,bkhd->bhqk', q, k).astype(jnp.float32) * HEAD_DIM ** -0.5
    p = jax.nn.softmax(s, axis=-1).astype(v.dtype)
    o = jnp.einsum('bhqk,bkhd->bqhd', p, v)
    return o.reshape(b, lc, ATT_DIM)

def neighbourhood_attention(q_rot, q, k_rot, v, k_ctx, v_ctx, rpb):
    b, l, h, dh = q.shape
    rows = l // GRID_W
    kr = min(NA_ROWS, rows)
    scale = dh ** -0.5
    q_rot_g = q_rot.reshape(b, rows, GRID_W, h, dh).transpose(1, 0, 2, 3, 4)
    q_g = q.reshape(b, rows, GRID_W, h, dh).transpose(1, 0, 2, 3, 4)
    k_g = k_rot.reshape(b, rows, GRID_W, h, dh)
    v_g = v.reshape(b, rows, GRID_W, h, dh)
    row_start = np.clip(np.arange(rows) - kr // 2, 0, rows - kr).astype(np.int32)
    col_start = np.clip(np.arange(GRID_W) - NA_COLS // 2, 0, GRID_W - NA_COLS)
    col_idx = (col_start[:, None] + np.arange(NA_COLS)[None, :]).astype(np.int32)
    col_off = (col_idx - np.arange(GRID_W)[:, None] + (NA_COLS - 1)).astype(np.int32)
    rpb_cols = rpb[:, :, col_off]

    def one_row(args):
        qr_rot, qr, r, rs = args
        k_rows = lax.dynamic_slice_in_dim(k_g, rs, kr, axis=1)
        v_rows = lax.dynamic_slice_in_dim(v_g, rs, kr, axis=1)
        kw = k_rows[:, :, col_idx]
        vw = v_rows[:, :, col_idx]
        row_off = rs + jnp.arange(kr) - r + (NA_ROWS - 1)
        bias = rpb_cols[:, row_off].transpose(0, 2, 1, 3)
        s_win = jnp.einsum('bqhd,biqjhd->bhqij', qr_rot, kw).astype(jnp.float32) * scale
        s_win = (s_win + bias.astype(jnp.float32)[None]).reshape(b, h, GRID_W, kr * NA_COLS)
        s_ctx = jnp.einsum('bqhd,bchd->bhqc', qr, k_ctx).astype(jnp.float32) * scale
        p = jax.nn.softmax(jnp.concatenate([s_win, s_ctx], axis=-1), axis=-1).astype(v.dtype)
        p_win = p[..., :kr * NA_COLS].reshape(b, h, GRID_W, kr, NA_COLS)
        p_ctx = p[..., kr * NA_COLS:]
        return (jnp.einsum('bhqij,biqjhd->bqhd', p_win, vw)
                + jnp.einsum('bhqc,bchd->bqhd', p_ctx, v_ctx))

    out = lax.map(one_row, (q_rot_g, q_g, jnp.arange(rows, dtype=jnp.int32), jnp.asarray(row_start)))
    return out.transpose(1, 0, 2, 3, 4).reshape(b, l, h * dh)

def second_inputs(seed: int = 0) -> dict:
    key = jax.random.key(seed)
    ks = jax.random.split(key, 18)
    n = jax.random.normal
    return {
        'x': n(ks[0], (BATCH, SEQ, D_MODEL), jnp.float32),
        'c': n(ks[1], (BATCH, D_MODEL), jnp.float32),
        'ctx': n(ks[2], (BATCH, CTX_LEN, D_MODEL), jnp.float32),
        'c_ctx': n(ks[3], (D_MODEL,), jnp.float32),
        'w_ada': n(ks[4], (DEPTH, D_MODEL, N_MOD * D_MODEL), jnp.float32) * (0.5 * D_MODEL ** -0.5),
        'b_ada': 0.02 * n(ks[5], (DEPTH, N_MOD * D_MODEL), jnp.float32),
        'norm1_g': 1.0 + 0.02 * n(ks[6], (DEPTH, D_MODEL), jnp.float32),
        'norm2_g': 1.0 + 0.02 * n(ks[7], (DEPTH, D_MODEL), jnp.float32),
        'w_in': n(ks[8], (DEPTH, D_MODEL, IN_PROJ_DIM), jnp.float32) * D_MODEL ** -0.5,
        'dw_kernel': n(ks[9], (DEPTH, CONV_WIDTH_2, CONV_DIM), jnp.float32) * CONV_WIDTH_2 ** -0.5,
        'dw_bias': 0.02 * n(ks[10], (DEPTH, CONV_DIM), jnp.float32),
        'conv_ln_g': 1.0 + 0.02 * n(ks[11], (DEPTH, CONV_DIM), jnp.float32),
        'conv_ln_b': 0.02 * n(ks[12], (DEPTH, CONV_DIM), jnp.float32),
        'rpb': 0.5 * n(ks[13], (DEPTH, N_HEADS, 2 * NA_ROWS - 1, 2 * NA_COLS - 1), jnp.float32),
        'w_out': n(ks[14], (DEPTH, MIX_DIM, D_MODEL), jnp.float32) * MIX_DIM ** -0.5,
        'w_mlp1': n(ks[15], (DEPTH, D_MODEL, D_FF_2), jnp.float32) * D_MODEL ** -0.5,
        'w_mlp2': n(ks[16], (DEPTH, D_FF_2, D_MODEL), jnp.float32) * D_FF_2 ** -0.5,
        'final_g': 1.0 + 0.02 * n(ks[17], (D_MODEL,), jnp.float32),
    }

def second_block(x, c, ctx, c_ctx, w_ada, b_ada, norm1_g, norm2_g, w_in, dw_kernel, dw_bias,
              conv_ln_g, conv_ln_b, rpb, w_out, w_mlp1, w_mlp2, final_g):
    l = x.shape[1]
    t = jnp.arange(l, dtype=jnp.int32)
    row_pos = t // GRID_W
    col_pos = t % GRID_W
    silu_c = jax.nn.silu(c)
    silu_cc = jax.nn.silu(c_ctx)[None]
    for i in range(DEPTH):
        last = i == DEPTH - 1
        mod_x = (silu_c @ w_ada[i] + b_ada[i])[:, None, :]
        mod_c = (silu_cc @ w_ada[i] + b_ada[i])[:, None, :]
        sh1, sc1, g1, sh2, sc2, g2 = jnp.split(mod_x, N_MOD, axis=-1)
        csh1, csc1, cg1, csh2, csc2, cg2 = jnp.split(mod_c, N_MOD, axis=-1)

        hx = modulate(rms_norm_2(x, norm1_g[i]), sh1, sc1)
        hc = modulate(rms_norm_2(ctx, norm1_g[i]), csh1, csc1)
        qx, kx, vx, ux = split_proj(hx @ w_in[i])
        if last:
            kvc = hc @ w_in[i][:, ATT_DIM:3 * ATT_DIM]
            kc, vc = split_heads(kvc[..., :ATT_DIM]), split_heads(kvc[..., ATT_DIM:])
        else:
            qc, kc, vc, uc = split_proj(hc @ w_in[i])

        qx_rot = axial_rope(qx, row_pos, col_pos)
        kx_rot = axial_rope(kx, row_pos, col_pos)
        attn_x = neighbourhood_attention(qx_rot, qx, kx_rot, vx, kc, vc, rpb[i])
        conv_x = conformer_conv(ux, dw_kernel[i], dw_bias[i], conv_ln_g[i], conv_ln_b[i])
        x_new = x + g1 * (jnp.concatenate([attn_x, conv_x], axis=-1) @ w_out[i])

        hx2 = modulate(rms_norm_2(x_new, norm2_g[i]), sh2, sc2)
        x_new = x_new + g2 * sq_relu_mlp(hx2, w_mlp1[i], w_mlp2[i])

        if not last:
            attn_c = context_attention(qc, kc, vc)
            conv_c = conformer_conv(uc, dw_kernel[i], dw_bias[i], conv_ln_g[i], conv_ln_b[i])
            ctx = ctx + cg1 * (jnp.concatenate([attn_c, conv_c], axis=-1) @ w_out[i])
            hc2 = modulate(rms_norm_2(ctx, norm2_g[i]), csh2, csc2)
            ctx = ctx + cg2 * sq_relu_mlp(hc2, w_mlp1[i], w_mlp2[i])
        x = x_new
    return rms_norm_2(x, final_g)


def setup_inputs(seed=0):
    out = dict(first_inputs(seed))
    for name, value in second_inputs(seed + 1).items():
        if name != "x":
            out[name + "_2"] = value
    return out


def reference(
    x, p, norm_mix_pre, norm_mix_post, norm_ffn_pre, norm_ffn_post, norm_ple, w_in, rwkv_mu,
    rwkv_w0, rwkv_w_up, rwkv_a0, rwkv_a_up, rwkv_g_up, rwkv_k_k, rwkv_k_a, rwkv_r_k, rwkv_ln_w,
    rwkv_ln_b, gla_conv, gla_a_up, gla_a_b, gla_norm, w_out, ffn_gate, ffn_up, ffn_down,
    ple_proj, ple_gate, ple_gate_b, c_2, ctx_2, c_ctx_2, w_ada_2, b_ada_2, norm1_g_2, norm2_g_2,
    w_in_2, dw_kernel_2, dw_bias_2, conv_ln_g_2, conv_ln_b_2, rpb_2, w_out_2, w_mlp1_2,
    w_mlp2_2, final_g_2,
):
    x = first_block(
        x, p, norm_mix_pre, norm_mix_post, norm_ffn_pre, norm_ffn_post, norm_ple, w_in, rwkv_mu,
        rwkv_w0, rwkv_w_up, rwkv_a0, rwkv_a_up, rwkv_g_up, rwkv_k_k, rwkv_k_a, rwkv_r_k,
        rwkv_ln_w, rwkv_ln_b, gla_conv, gla_a_up, gla_a_b, gla_norm, w_out, ffn_gate, ffn_up,
        ffn_down, ple_proj, ple_gate, ple_gate_b,
    )
    return second_block(
        x, c_2, ctx_2, c_ctx_2, w_ada_2, b_ada_2, norm1_g_2, norm2_g_2, w_in_2, dw_kernel_2,
        dw_bias_2, conv_ln_g_2, conv_ln_b_2, rpb_2, w_out_2, w_mlp1_2, w_mlp2_2, final_g_2,
    )


_drawn_inputs = setup_inputs


def setup_inputs(seed=0):
    import zlib

    import numpy as np

    out = dict(_drawn_inputs(seed))
    spreads = {}
    factors = {'rwkv_ln_b': 5.857,
     'gla_a_up': 3.0,
     'ple_gate_b': 8.0,
     'ctx_2': 6.264,
     'c_ctx_2': 3.003,
     'b_ada_2': 3.407,
     'norm1_g_2': 8.0,
     'norm2_g_2': 22.074,
     'dw_bias_2': 36.919,
     'conv_ln_g_2': 51.803,
     'conv_ln_b_2': 47.371,
     'rpb_2': 25.1,
     'final_g_2': 21.769}
    for name, (base, spread) in spreads.items():
        noise = np.random.default_rng([zlib.crc32(name.encode()), seed]).standard_normal(out[name].shape)
        drawn = base * np.exp(spread * noise) if base else spread * noise
        out[name] = __import__('jax').numpy.asarray(drawn.astype(out[name].dtype))
    for name, factor in factors.items():
        out[name] = (out[name] * factor).astype(out[name].dtype)
    return out
```

```python
import math
from contextlib import ExitStack

import numpy as np

import concourse.bass as bass
from concourse import mybir

F32 = mybir.dt.float32
ALU = mybir.AluOpType
ACTF = mybir.ActivationFunctionType
AX = mybir.AxisListType

PART = 128
TOK = 1024
HALF = 512
D = 1024
DC = D // PART
CH = 64
NBLK = TOK // PART
RW = 512
RPAIR = 4
LANES = 2 * RPAIR
LEVELS = 6
GPAIR = 2
GLEV = LEVELS + 1
GSLOT = GLEV + 2
DFF = 2816
DFF2 = 4096
CTX = 256
HEADS = 8
GRID = 64
ROWS = TOK // GRID
WIN_R, WIN_C = 8, 16
RPB_R, RPB_C = 2 * WIN_R - 1, 2 * WIN_C - 1
TAPS = 31
NEG = -1.0e30
DECAY = -math.exp(-0.5)


def constants():
    c = {}
    f = np.float32
    c["ident"] = np.eye(PART, dtype=f)
    t = np.arange(PART)
    same = (t[:, None] // CH) == (t[None, :] // CH)
    tri = np.zeros((2, PART, 2, PART), f)
    s, q = t[:, None], t[None, :]
    for d, (inc, exc) in enumerate((((s <= q), (s < q)), ((s >= q), (s > q)))):
        tri[d, :, 0] = DECAY * np.where(same, inc.astype(f) - 0.5, 0)
        tri[d, :, 1] = DECAY * np.where(same, exc.astype(f) - 0.5, 0)
    c["tri"] = np.ascontiguousarray(tri.transpose(1, 0, 2, 3)).reshape(PART, -1)
    g = np.zeros((2, PART, GSLOT, PART), f)
    for d in range(2):
        pos = (t % CH) if d == 0 else (CH - 1 - t % CH)
        ps, pq = pos[:, None], pos[None, :]
        for lev in range(1, GLEV):
            w = 2 ** (lev - 1)
            mid = (pq // (2 * w)) * 2 * w + w
            m = np.where(pq >= mid, (ps >= mid) & (ps <= pq), (ps > pq) & (ps < mid))
            g[d, :, lev] = m & same
        g[d, :, GLEV] = (ps <= pq) & same
        g[d, :, GLEV + 1] = (ps > pq) & same
    g /= 16.0
    c["gsum"] = np.ascontiguousarray(g.transpose(1, 0, 2, 3)).reshape(PART, -1)
    tt = np.arange(CH)
    m = np.zeros((CH, 2, 2, CH), f)
    m[:, 0, 0] = tt[:, None] < tt[None, :]
    m[:, 0, 1] = tt[:, None] <= tt[None, :]
    m[:, 1, 0] = tt[:, None] > tt[None, :]
    m[:, 1, 1] = tt[:, None] >= tt[None, :]
    c["gram_mask"] = np.tile(m.reshape(CH, -1), (2, 1))
    lm = np.zeros((CH, LEVELS, 2, CH), f)
    gm = np.zeros((CH, 2, GLEV, CH), f)
    for d in range(2):
        pos = tt if d == 0 else CH - 1 - tt
        gm[:, d, 0] = np.eye(CH)
        for lev in range(LEVELS):
            w = 2 ** lev
            blk = pos // (2 * w)
            late = (pos % (2 * w)) >= w
            lm[:, lev, d] = (blk[:, None] == blk[None, :]) & late[:, None] & ~late[None, :]
            gm[:, d, lev + 1] = (blk[:, None] == blk[None, :]) & ~late[:, None] & late[None, :]
    c["lev_mask"] = np.tile(lm.reshape(CH, -1), (2, 1))
    c["gla_mask"] = np.tile(gm.reshape(CH, -1), (2, 1))
    c["stack_eye"] = np.tile(np.eye(CH, dtype=f), (2, 1))
    hb = (t[:, None] // CH) == (t[None, :] // CH)
    c["head_ones"] = hb.astype(f)
    n = 16
    inv = (np.float32(10000.0) ** (-np.arange(n, dtype=f) / n)).astype(f)
    tok = np.arange(TOK)
    ch = np.arange(64)
    p = np.where((ch < 32)[:, None], (tok // GRID)[None, :], (tok % GRID)[None, :]).astype(f)
    ang = (p * inv[ch % n][:, None]).astype(f)
    sign = np.where((ch % 32) < 16, -1.0, 1.0).astype(f)[:, None]
    c["rope_cos"] = np.tile(np.cos(ang), (2, 1)).astype(f)
    c["rope_sin"] = np.tile(np.sin(ang) * sign, (2, 1)).astype(f)
    c["swap"] = (s == (q ^ 16)).astype(f)
    cs = np.clip(np.arange(GRID) - WIN_C // 2, 0, GRID - WIN_C)
    inside = (np.arange(GRID)[None, :] >= cs[:, None]) & (np.arange(GRID)[None, :] < cs[:, None] + WIN_C)
    c["col_mask"] = np.tile(np.where(inside, 0.0, NEG).astype(f), (2, 1))
    return c


class Done:

    def __init__(self, counter, count, per, turn):
        self.counter, self.count, self.per, self.turn = counter, count, per, turn

    def before(self):
        assert self.count >= self.per
        return Done(self.counter, self.count - self.per, self.per, self.turn)


class Counter:
    def __init__(self, prog, name, step):
        self.sem, self.step = prog.nc.alloc_semaphore(name), step
        self.prog, self.count, self.per = prog, 0, 0
        prog.counters.append(self)

    def here(self):
        return Done(self, self.count, self.per, self.prog.turn)


class Queue:

    def __init__(self, prog, name, eng, chained):
        self.prog, self.eng, self.chained = prog, eng, chained
        self.counter = Counter(prog, name, 1)
        self.seen = {}

    def wait(self, done):
        if self.prog.dry or done is None:
            return
        if isinstance(done, (list, tuple)):
            for d in done:
                self.wait(d)
            return
        key = (done.counter, done.per)
        if done.count <= self.seen.get(key, 0) or (done.count == 0 and not done.per):
            return
        self.seen[key] = done.count
        step = done.counter.step
        value = done.count * step
        if done.per:
            assert done.count > 0
            value = done.turn * (done.per * step) + value
        self.eng.wait_ge(done.counter.sem, value)

    def __call__(self, make, after=None, mark=None, chain=None):
        self.wait(after)
        if self.chained if chain is None else chain:
            self.wait(self.counter.here())
        if self.chained if mark is None else mark:
            self.counter.count += 1
            if not self.prog.dry:
                make(self.eng).then_inc(self.counter.sem, 1)
        elif not self.prog.dry:
            make(self.eng)
        return self.counter.here()


class Transfer:

    def __init__(self, prog, name):
        self.prog, self.counter = prog, Counter(prog, name, 16)

    def start(self, queue, out, in_, after=None):
        queue.wait(after)
        self.counter.count += 1
        if not self.prog.dry:
            queue.eng.dma_start(out, in_).then_inc(self.counter.sem, 16)
        return self.counter.here()

    def here(self):
        return self.counter.here()


class Prog:
    def __init__(self, nc):
        self.nc, self.counters, self.dry, self.turn = nc, [], False, None
        self.pe = Queue(self, "pe", nc.tensor, False)
        self.act = Queue(self, "act", nc.scalar, True)
        self.dve = Queue(self, "dve", nc.vector, True)
        self.pool = Queue(self, "pool", nc.gpsimd, True)
        self.sp = Queue(self, "sp", nc.sync, False)
        self.engines = (self.pe, self.act, self.dve, self.pool)

    def loop(self, turns, body):
        if turns <= 0:
            return
        start = [c.count for c in self.counters]
        self.dry = True
        left = body(0, None)
        self.dry = False
        for c, s in zip(self.counters, start):
            c.per, c.count = c.count - s, s
        seen = [dict(q.seen) for q in (*self.engines, self.sp)]
        with self.nc.Fori(0, turns) as turn:
            self.turn = turn
            last = None
            if left is not None:
                last = {k: [Done(d.counter, d.count, d.counter.per, turn).before() for d in v]
                        for k, v in left.items()}
            body(turn, last)
        self.turn = None
        for c, s in zip(self.counters, start):
            assert c.count == s + c.per
            c.count, c.per = s + c.per * turns, 0
        for q, s in zip((*self.engines, self.sp), seen):
            q.seen = s

    def all_done(self):
        return [q.counter.here() for q in self.engines]

    def meet(self, *more):
        done = [*self.all_done(), *more]
        for q in (*self.engines, self.sp):
            q.wait(done)


class Columns:

    def __init__(self):
        self.rows, self.at = [], {}
        self.n = 0

    def add(self, name, ap2d):
        self.at[name] = self.n
        r = 0
        n = ap2d.shape[0]
        while r < n:
            k = min(n - r, PART - self.n % PART)
            self.rows.append((self.n, k, ap2d[r:r + k, :]))
            self.n += k
            r += k


def blocks(ap):
    return ap.rearrange("(n p) -> n p", p=PART)


class Kernel:
    def __init__(self, nc, ins, out, only=None, dumps=None):
        self.nc, self.i, self.out = nc, ins, out
        self.p = Prog(nc)
        self.only, self.dumps, self.made = only, dumps or {}, 0
        self.ps = nc.alloc_psum_tensor("ps", [PART, 8, HALF], F32)
        self.t_misc = Transfer(self.p, "t_misc")
        self.t_w = [Transfer(self.p, "t_w0"), Transfer(self.p, "t_w1")]
        self.t_h = Transfer(self.p, "t_h")
        self.t_st = Transfer(self.p, "t_st")
        self.t_in = Transfer(self.p, "t_in")
        self.h_dram = ins.get("h_dram")
        if self.h_dram is None:
            self.h_dram = nc.dram_tensor("h_dram", (PART, DC, TOK), F32, kind="Internal").ap()

    def sb(self, stack, name, shape):
        self.made = self.made + 1
        return stack.enter_context(self.nc.sbuf_tensor(f"{name}_{self.made}", shape, F32))

    def dump(self, name, ap):
        if name in self.dumps:
            self.p.meet()
            self.t_misc.start(self.p.sp, self.dumps[name], ap)
            self.p.meet(self.t_misc.here())

    def col(self, name, k=0, rows=PART):
        at = self.cols_at[name]
        if isinstance(k, int):
            return self.cols[0:rows, at + k:at + k + 1]
        return self.cols[0:rows, bass.ds(k + at, 1)]

    def setup(self, stack):
        p, i = self.p, self.i
        c = Columns()
        for n in ("norm_mix_pre", "norm_mix_post", "norm_ffn_pre", "norm_ffn_post", "norm_ple", "ple_gate_b",
                  "rwkv_a0", "rwkv_k_k", "rwkv_k_a", "rwkv_ln_w", "rwkv_ln_b", "norm1_g_2", "norm2_g_2",
                  "b_ada_2", "dw_bias_2", "conv_ln_g_2", "conv_ln_b_2"):
            c.add(n, i[n].rearrange("a (n p) -> (a n) p", p=PART))
        c.add("rwkv_r_k", i["rwkv_r_k"].rearrange("a (n two) p -> (a n) (two p)", two=2))
        mu = i["rwkv_mu"]
        c.add("mu", mu[:, 0:3 * RW + PART].rearrange("a (n p) -> (a n) p", p=PART))
        c.add("mu_g", mu[:, 1728:1856])
        c.add("mu_a", mu[:, 1664:1728])
        c.add("gla_norm", i["gla_norm"])
        c.add("conv", i["gla_conv"].rearrange("a w b (n p) -> (a w b n) p", p=PART))
        c.add("dw", i["dw_kernel_2"].rearrange("a w (n p) -> (a w n) p", p=PART))
        c.add("final_g", blocks(i["final_g_2"]))
        c.add("c_2", i["c_2"].rearrange("a (n p) -> (a n) p", p=PART))
        c.add("c_ctx", blocks(i["c_ctx_2"]))
        self.cols_at = c.at
        nt = -(-c.n // PART)
        self.cols = self.sb(stack, "cols", [PART, nt * PART])
        self.ident = self.sb(stack, "ident", [PART, PART])
        self.ones = self.sb(stack, "ones", [PART, PART])
        self.t_misc.start(p.sp, self.ident[:], i["k_ident"])
        p.dve(lambda e: e.memset(self.ones[:], 1.0))
        with ExitStack() as tmp:
            rows = self.sb(tmp, "rows", [PART, nt, PART])
            zeroed = p.dve(lambda e: e.memset(rows[:], 0.0))
            for at, k, src in c.rows:
                w = src.shape[1]
                self.t_misc.start(p.sp, rows[at % PART:at % PART + k, at // PART, 0:w], src, after=zeroed)
            for t in range(nt):
                done = p.pe(lambda e: e.transpose(self.ps[:, 0, t * PART:(t + 1) * PART], rows[:, t, :],
                                                  self.ident[:]), after=self.t_misc.here(), mark=True)
            p.dve(lambda e: e.tensor_copy(self.cols[:], self.ps[:, 0, 0:nt * PART]), after=done)
            p.meet()

    def weight_slots(self, stack, cols=2048):
        self.w = [self.sb(stack, f"w{s}", [PART, cols]) for s in range(2)]

    def gemm(self, weights, kc, groups, nb, rhs, evac, after=None, tokens=TOK, m=PART, split=False):
        p = self.p
        nh = -(-tokens // HALF)
        tw = min(tokens, HALF)
        slot = [w[:, 0:kc * nb * m].rearrange("p (c n) -> p c n", c=kc) for w in self.w]
        free = {0: list(p.all_done()), 1: list(p.all_done())}

        def load(g, s, freed):
            parts = weights(g) if split else [weights(g)]
            for b, w in enumerate(parts):
                wide = w.shape[1]
                self.t_w[s].start(p.sp, slot[s][:, :, b * wide:(b + 1) * wide], w.rearrange("(c p) n -> p c n", p=PART),
                                  after=freed)

        def compute(g, s):
            loaded = self.t_w[s].here()
            for b in range(nb):
                pair = (s * nb + b) % 2
                bank = self.ps[:, 2 * pair:2 * pair + 2, :]
                p.pe.wait(loaded)
                p.pe.wait(free[pair])
                for h in range(nh):
                    for k in range(kc):
                        done = p.pe(lambda e: e.matmul(bank[0:m, h, 0:tw], slot[s][:, k, b * m:(b + 1) * m],
                                                       rhs(k, h), start=(k == 0), stop=(k == kc - 1)),
                                    mark=(h == nh - 1 and k == kc - 1))
                free[pair] = evac(g, b, bank, done) if split else evac(g * nb + b, bank, done)
            return done

        p.pe.wait(after)
        start = p.all_done()
        load(0, 0, start)
        if groups > 1:
            load(1, 1, start)
        turns = groups // 2 - 1
        if turns < 2:
            turns = 0

        def turn(t, last):
            if last is not None:
                free[0], free[1] = last["f0"], last["f1"]
            for s in range(2):
                used = compute(t * 2 + s, s)
                load(t * 2 + s + 2, s, used)
            return {"f0": free[0], "f1": free[1]}

        if turns:
            p.pe.wait([free[0], free[1]])
            p.loop(turns, turn)
            free[0] = free[1] = p.all_done()
        for g in range(2 * turns, groups):
            used = compute(g, g % 2)
            if g + 2 < groups:
                load(g + 2, g % 2, used)
        return p.all_done()

    def rsqrt(self, v, y, t, after=None):
        p = self.p
        done = p.act(lambda e: e.activation(y, v, ACTF.Sqrt), after=[after, p.dve.counter.here()])
        p.dve(lambda e: e.reciprocal(y, y), after=done)
        p.dve(lambda e: e.tensor_tensor(t, y, y, ALU.mult))
        p.dve(lambda e: e.tensor_tensor(t, t, v, ALU.mult))
        p.dve(lambda e: e.tensor_scalar(t, t, -0.5, 1.5, ALU.mult, ALU.add))
        return p.dve(lambda e: e.tensor_tensor(y, y, t, ALU.mult))

    def rms_inverse(self, x, nblk, width, inv, tmp, tokens=TOK, eps=1e-6):
        p = self.p
        nh = -(-tokens // HALF)
        tw = min(tokens, HALF)
        start = p.all_done()
        added = start
        for c in range(nblk):
            dst = inv if c == 0 else tmp[:, 0, :]
            sq = p.act(lambda e: e.activation(dst, x(c), ACTF.Square), after=added)
            if c:
                added = p.dve(lambda e: e.tensor_tensor(inv, inv, tmp[:, 0, :], ALU.add), after=[sq, start])
        last = added if nblk > 1 else sq
        for h in range(nh):
            done = p.pe(lambda e: e.matmul(self.ps[:, 4 + h, 0:tw], self.ones[:], inv[:, h * tw:(h + 1) * tw],
                                           start=True, stop=True), after=[last, start], mark=True)
        v = tmp[:, 0, :]
        p.dve(lambda e: e.tensor_scalar(v.rearrange("p (h t) -> p h t", h=nh), self.ps[:, 4:4 + nh, 0:tw],
                                        1.0 / width, eps, ALU.mult, ALU.add), after=done)
        return self.rsqrt(v, inv, tmp[:, 1, :])

    def normed(self, dst, x, inv, name, nblk=DC):
        p = self.p
        for c in range(nblk):
            p.dve(lambda e: e.scalar_tensor_tensor(out=dst(c), in0=x(c), scalar=self.col(name, c), in1=inv,
                                                   op0=ALU.mult, op1=ALU.mult))

    def add_normed(self, y, name, h, stack):
        p = self.p
        inv = self.sb(stack, "an_inv", [PART, TOK])
        tmp = self.sb(stack, "an_tmp", [PART, 2, TOK])
        self.rms_inverse(lambda c: y[:, c, :], DC, D, inv[:], tmp)
        self.normed(lambda c: y[:, c, :], lambda c: y[:, c, :], inv[:], name)
        for c in range(DC):
            p.dve(lambda e: e.tensor_tensor(h[:, c, :], h[:, c, :], y[:, c, :], ALU.add))
        p.meet()

    def load_x(self, xn, stack):
        p = self.p
        x = self.i["x"].rearrange("b (n p) c -> n p (b c)", p=PART)
        row = self.sb(stack, "x_row", [PART, D])
        p.meet()

        def turn(t, last):
            got = self.t_in.start(p.sp, row[:], x[t], after=p.pe.counter.here())
            p.pe.wait([got, p.dve.counter.here()])
            for c in range(DC):
                done = p.pe(lambda e: e.transpose(self.ps[:, c // 4, (c % 4) * PART:(c % 4 + 1) * PART],
                                                  row[:, c * PART:(c + 1) * PART], self.ident[:]), mark=(c == DC - 1))
            p.dve(lambda e: e.tensor_copy(
                xn[:, :, bass.ts(t, PART)].rearrange("p (a b) t -> p a b t", b=4),
                self.ps[:, 0:2, :].rearrange("p a (b t) -> p a b t", t=PART)), after=done)

        p.loop(NBLK, turn)
        kept = self.t_h.start(p.sp, self.h_dram, xn[:], after=p.dve.counter.here())
        inv = self.sb(stack, "x_inv", [PART, TOK])
        tmp = self.sb(stack, "x_tmp", [PART, 2, TOK])
        self.rms_inverse(lambda c: xn[:, c, :], DC, D, inv[:], tmp)
        p.dve.wait(kept)
        self.normed(lambda c: xn[:, c, :], lambda c: xn[:, c, :], inv[:], "norm_mix_pre")
        p.meet()

    def gla(self, xn, ycat):
        p, i, nc = self.p, self.i, self.nc
        w_in = i["w_in"].rearrange("a k n -> (a k) n")
        st = ExitStack()
        qkv = self.sb(st, "g_qkv", [PART, 8, TOK])
        gate = self.sb(st, "g_gate", [PART, 4, TOK])
        la_dram = nc.dram_tensor("la_dram", (NBLK, PART, 512), F32, kind="Internal").ap()
        p.meet()
        with ExitStack() as gs:
            self.weight_slots(gs)
            zp = [self.sb(gs, f"g_zp{s}", [PART, TOK + 2]) for s in range(2)]
            cv = [self.sb(gs, f"g_cv{s}", [PART, TOK]) for s in range(2)]
            alo = self.sb(gs, "g_alo", [32, TOK])
            aup = self.sb(gs, "g_aup", [32, 512])
            ab = self.sb(gs, "g_ab", [PART, 512])
            la = self.sb(gs, "g_la", [PART, NBLK, 512])
            lb = self.sb(gs, "g_lb", [PART, NBLK, 512])
            for z in zp:
                p.dve(lambda e: e.memset(z[:, 0:1], 0.0))
                p.dve(lambda e: e.memset(z[:, TOK + 1:TOK + 2], 0.0))
            zeroed = p.dve(lambda e: e.memset(aup[:], 0.0))
            for d in range(2):
                self.t_misc.start(p.sp, aup[16 * d:16 * d + 16, 256 * d:256 * d + 256], i["gla_a_up"][0, d], after=zeroed)
                self.t_misc.start(p.sp, ab[:, 256 * d:256 * d + 256], i["gla_a_b"][0, d:d + 1, :].to_broadcast([PART, 256]))

            parity = [0]

            def conv_evac(n, bank, done):
                parity[0] ^= 1
                z, o = zp[parity[0]], cv[parity[0]]
                free = p.act(lambda e: e.activation(z[:, 1:TOK + 1].rearrange("p (h t) -> p h t", h=2), bank, ACTF.Copy),
                             after=done)
                p.dve(lambda e: e.tensor_scalar(o[:], z[:, 0:TOK], self.col("conv", n), None, ALU.mult), after=free)
                p.dve(lambda e: e.scalar_tensor_tensor(out=o[:], in0=z[:, 1:TOK + 1], scalar=self.col("conv", n + 8),
                                                       in1=o[:], op0=ALU.mult, op1=ALU.add))
                c = p.dve(lambda e: e.scalar_tensor_tensor(out=o[:], in0=z[:, 2:TOK + 2], scalar=self.col("conv", n + 16),
                                                           in1=o[:], op0=ALU.mult, op1=ALU.add))
                p.act(lambda e: e.activation(qkv[:, n, :], o[:], ACTF.Silu), after=c)
                return [free]

            self.gemm(lambda g: w_in[:, bass.ds(g * 256 + 1856, 256)], DC, 4, 2, lambda k, h: xn[:, k, h * HALF:(h + 1) * HALF],
                      conv_evac, None)

            def gate_evac(n, bank, done):
                return [p.act(lambda e: e.activation(gate[:, n, :].rearrange("p (h t) -> p h t", h=2), bank, ACTF.Silu),
                              after=done)]

            self.gemm(lambda g: w_in[:, bass.ds(g * 256 + 2880, 256)], DC, 2, 2, lambda k, h: xn[:, k, h * HALF:(h + 1) * HALF],
                      gate_evac, None)

            def alo_evac(n, bank, done):
                return [p.act(lambda e: e.activation(alo[:].rearrange("p (h t) -> p h t", h=2), bank[0:32], ACTF.Copy), after=done)]

            self.gemm(lambda g: w_in[:, 3392:3424], DC, 1, 1, lambda k, h: xn[:, k, h * HALF:(h + 1) * HALF], alo_evac, None, m=32)
            p.act(lambda e: e.activation(qkv[:, 0:2, :], qkv[:, 0:2, :], ACTF.Copy, scale=CH ** -0.5))
            p.meet(self.t_misc.here())
            for n in range(NBLK):
                done = p.pe(lambda e: e.matmul(self.ps[:, n, :], alo[:, n * PART:(n + 1) * PART], aup[:], start=True, stop=True),
                            mark=True)
            abb = bass_rep(ab[:], NBLK)
            p.dve(lambda e: e.tensor_tensor(la[:], self.ps[:], abb, ALU.add), after=done)
            m = p.dve(lambda e: e.scalar_tensor_tensor(out=lb[:], in0=la[:], scalar=-1.0, in1=la[:], op0=ALU.mult, op1=ALU.min))
            a = p.act(lambda e: e.activation(lb[:], lb[:], ACTF.Exp), after=m)
            a = p.act(lambda e: e.activation(lb[:], lb[:], ACTF.Ln, bias=1.0))
            p.dve(lambda e: e.tensor_scalar(la[:], la[:], 0.0, None, ALU.min))
            m = p.dve(lambda e: e.tensor_tensor(la[:], la[:], lb[:], ALU.subtract), after=a)
            kept = self.t_misc.start(p.sp, la_dram.rearrange("n p c -> p n c"), la[:], after=m)
            p.meet(kept)
        self.dump("d_qkv", qkv[:])
        with ExitStack() as ls:
            gsum = self.sb(ls, "gsum", [PART, 2, GSLOT, PART])
            mask = self.sb(ls, "gmask", [PART, 2, GLEV, CH])
            lat = self.sb(ls, "g_lat", [PART, 2, 256])
            E = self.sb(ls, "g_E", [PART, 4, GSLOT, PART])
            Qs = self.sb(ls, "g_Qs", [PART, 4, GLEV, CH])
            Qe = self.sb(ls, "g_Qe", [PART, 4, PART])
            Kb = self.sb(ls, "g_Kb", [PART, 4, GLEV + 1, PART])
            VT = self.sb(ls, "g_VT", [PART, 4, PART])
            KeT = self.sb(ls, "g_KeT", [PART, 4, PART])
            VP = self.sb(ls, "g_VP", [PART, 4, PART])
            SM = self.sb(ls, "g_SM", [PART, 4, GLEV, CH])
            Pc = self.sb(ls, "g_Pc", [PART, 4, CH])
            Pb = self.sb(ls, "g_Pb", [PART, 4, PART])
            S = self.sb(ls, "g_S", [PART, 4, PART])
            self.t_misc.start(p.sp, gsum[:].rearrange("p a b c -> p (a b c)"), i["k_gsum"])
            self.t_misc.start(p.sp, mask[:].rearrange("p a b c -> p (a b c)"), i["k_gla_mask"])
            for t in (Qe, Kb, Pb, S):
                p.dve(lambda e: e.memset(t[:], 0.0))
            p.dve(lambda e: e.memset(ycat[:, 4:8, :], 0.0))
            p.dve(lambda e: e.memset(E[:, :, 0, :], 1.0))
            p.meet(self.t_misc.here())

            def turn(t, last):
                self.t_in.start(p.sp, lat[:, 0, :], la_dram[t, :, 0:256], after=p.pe.counter.here())
                got = self.t_in.start(p.sp, lat[:, 1, :], la_dram[7 - t, :, 256:512])
                p.pe.wait([got, p.act.counter.here(), p.dve.counter.here()])
                for d in range(2):
                    for pr in range(2):
                        for s in range(2):
                            done = p.pe(lambda e: e.matmul(self.ps[:, 4 * d + 2 * pr + s, :], lat[:, d, pr * PART:(pr + 1) * PART],
                                                           gsum[:, d, 1 + 4 * s:5 + 4 * s, :], start=True, stop=True),
                                        mark=True)
                for l in range(4):
                    made = p.act(lambda e: e.activation(E[:, l, 1:GSLOT, :].rearrange("p a b -> p (a b)"),
                                                        self.ps[:, 2 * l:2 * l + 2, :].rearrange("p a b -> p (a b)"), ACTF.Exp),
                                 after=[done, p.dve.counter.here()])
                p.pool.wait(made)
                for sub in range(2):
                    for d in range(2):
                        u = sub if d == 0 else 1 - sub
                        tok = (t * PART + u * CH) if d == 0 else ((7 - t) * PART + u * CH)
                        eu = E[:, 2 * d:2 * d + 2, :, u * CH:(u + 1) * CH]
                        L = slice(2 * d, 2 * d + 2)
                        p.dve.wait([made, p.pe.counter.here()])
                        q = qkv[:, 0:2, bass.ds(tok, CH)]
                        p.dve(lambda e: e.tensor_tensor(Qs[:, L], rep_mid(q, GLEV), eu[:, :, 0:GLEV], ALU.mult), chain=False)
                        for h in range(2):
                            H = slice(64 * h, 64 * h + 64)
                            qh, kh = qkv[H, 0:2, bass.ds(tok, CH)], qkv[H, 2:4, bass.ds(tok, CH)]
                            p.dve(lambda e: e.tensor_tensor(Qe[H, L, H], qh, eu[H, :, GLEV], ALU.mult), chain=False)
                            p.dve(lambda e: e.tensor_tensor(Kb[H, L, 0:GLEV, H], rep_mid(kh, GLEV), eu[H, :, 0:GLEV], ALU.mult),
                                  chain=False)
                            ready = p.dve(lambda e: e.tensor_tensor(Kb[H, L, GLEV, H], kh, eu[H, :, GLEV + 1], ALU.mult), chain=False)
                        vsrc = qkv[:, 4:8, bass.ds(tok, CH)]
                        vready = p.act(lambda e: e.activation(VT[:, L].rearrange("p l (h t) -> p (l h) t", h=2), vsrc, ACTF.Copy),
                                       after=p.pe.counter.here(), chain=False)
                    p.pe.wait([ready, vready])
                    for l in range(4):
                        p.pe(lambda e: e.transpose(self.ps[:, 0, l * PART:(l + 1) * PART], Kb[:, l, GLEV, :], self.ident[:]))
                    for l in range(4):
                        tr = p.pe(lambda e: e.transpose(self.ps[:, 1, l * PART:(l + 1) * PART], VT[:, l, :], self.ident[:]), mark=(l == 3))
                    for l in range(4):
                        for v in range(GLEV):
                            sc = p.pe(lambda e: e.matmul(self.ps[:, 2 + l, v * CH:(v + 1) * CH], Kb[:, l, v, :], Qs[:, l, v, :],
                                                         start=True, stop=True), mark=(l == 3 and v == GLEV - 1))
                    p.act(lambda e: e.activation(KeT[:].rearrange("p a b -> p (a b)"), self.ps[:, 0, :], ACTF.Copy), after=tr, chain=False)
                    tv = p.act(lambda e: e.activation(VP[:].rearrange("p a b -> p (a b)"), self.ps[:, 1, :], ACTF.Copy), chain=False)
                    for d in range(2):
                        L = slice(2 * d, 2 * d + 2)
                        p.dve(lambda e: e.tensor_tensor(SM[:, L].rearrange("p l v t -> p l (v t)"), self.ps[:, 2 + 2 * d:4 + 2 * d, 0:GLEV * CH],
                                                        bass_rep(mask[:, d].rearrange("p v t -> p (v t)"), 2), ALU.mult), after=sc, chain=False)
                    p.dve(lambda e: e.tensor_reduce(Pc[:], SM[:].rearrange("p l v t -> p l t v"), AX.X, ALU.add))
                    for h in range(2):
                        H = slice(64 * h, 64 * h + 64)
                        pb = p.dve(lambda e: e.tensor_copy(Pb[H, :, H], Pc[H]), chain=(h == 0))
                    p.pe.wait([pb, tv])
                    for l in range(4):
                        p.pe(lambda e: e.matmul(self.ps[:, 6, l * PART:(l + 1) * PART], VP[:, l, :], Pb[:, l, :], start=True, stop=False))
                        p.pe(lambda e: e.matmul(self.ps[:, 6, l * PART:(l + 1) * PART], S[:, l, :], Qe[:, l, :], start=False, stop=True))
                    for l in range(4):
                        od = p.pe(lambda e: e.matmul(self.ps[:, 7, l * PART:(l + 1) * PART], KeT[:, l, :], VP[:, l, :], start=True, stop=True),
                                  mark=(l == 3))
                    p.dve.wait(od)
                    for d in range(2):
                        u = sub if d == 0 else 1 - sub
                        tok = (t * PART + u * CH) if d == 0 else ((7 - t) * PART + u * CH)
                        end = u * CH + (CH - 1 if d == 0 else 0)
                        yv = ycat[:, 4:8, bass.ds(tok, CH)]
                        p.dve(lambda e: e.tensor_tensor(yv, yv, self.ps[:, 6, 256 * d:256 * d + 256].rearrange("p (a t) -> p a t", t=CH),
                                                        ALU.add), chain=(d == 1))
                        p.dve(lambda e: e.tensor_tensor(S[:, 2 * d:2 * d + 2], S[:, 2 * d:2 * d + 2],
                                                        rep_last(E[:, 2 * d:2 * d + 2, GLEV, end:end + 1], PART), ALU.mult), chain=False)
                    p.dve(lambda e: e.tensor_tensor(S[:].rearrange("p a b -> p (a b)"), S[:].rearrange("p a b -> p (a b)"), self.ps[:, 7, :], ALU.add))
                    p.pe.wait(p.dve.counter.here())

            p.loop(NBLK, turn)
            p.meet()
        self.dump("d_glao", ycat[:, 4:8, :])
        with ExitStack() as ps_:
            inv = self.sb(ps_, "g_inv", [PART, TOK])
            tmp = self.sb(ps_, "g_tmp", [PART, 2, TOK])
            for h in range(4):
                self.rms_inverse(lambda c: ycat[:, 4 + h, :], 1, PART, inv[:], tmp)
                p.dve(lambda e: e.scalar_tensor_tensor(out=ycat[:, 4 + h, :], in0=ycat[:, 4 + h, :], scalar=self.col("gla_norm"),
                                                       in1=inv[:], op0=ALU.mult, op1=ALU.mult))
                p.dve(lambda e: e.tensor_tensor(ycat[:, 4 + h, :], ycat[:, 4 + h, :], gate[:, h, :], ALU.mult))
            p.meet()
        st.close()

    def rwkv(self, xn, ycat):
        p, i, nc = self.p, self.i, self.nc
        w_in = i["w_in"].rearrange("a k n -> (a k) n")
        sg_dram = nc.dram_tensor("sg_dram", (2, NBLK, PART, RW), F32, kind="Internal").ap()
        lo_dram = nc.dram_tensor("lo_dram", (3, PART, TOK), F32, kind="Internal").ap()
        st = ExitStack()
        rkv = self.sb(st, "r_rkv", [PART, 12, TOK])
        p.meet()
        with ExitStack() as gs:
            self.weight_slots(gs)
            zp = [self.sb(gs, f"r_zp{s}", [PART, TOK + 2]) for s in range(2)]
            sh = [self.sb(gs, f"r_sh{s}", [PART, TOK]) for s in range(2)]
            wlo = self.sb(gs, "r_wlo", [PART, TOK])
            alo = self.sb(gs, "r_alo", [CH, TOK])
            sglo = self.sb(gs, "r_sglo", [PART, TOK])
            for z in zp:
                p.dve(lambda e: e.memset(z[:, 0:1], 0.0))
                p.dve(lambda e: e.memset(z[:, TOK + 1:TOK + 2], 0.0))

            def shifted(par, bank, done, mu, dst, rows=PART):
                z, s = zp[par], sh[par]
                free = p.act(lambda e: e.activation(z[0:rows, 1:TOK + 1].rearrange("p (h t) -> p h t", h=2), bank[0:rows], ACTF.Copy),
                             after=[done, p.dve.counter.here()])
                p.dve(lambda e: e.tensor_tensor(s[0:rows], z[0:rows, 0:TOK], z[0:rows, 2:TOK + 2], ALU.add), after=free)
                p.dve(lambda e: e.scalar_tensor_tensor(out=s[0:rows], in0=s[0:rows], scalar=0.5, in1=z[0:rows, 1:TOK + 1],
                                                       op0=ALU.mult, op1=ALU.subtract))
                end = p.dve(lambda e: e.scalar_tensor_tensor(out=dst, in0=s[0:rows], scalar=mu, in1=z[0:rows, 1:TOK + 1],
                                                             op0=ALU.mult, op1=ALU.add))
                return free, end

            rhs = lambda k, h: xn[:, k, h * HALF:(h + 1) * HALF]
            parity = [0]

            def rkv_evac(n, bank, done):
                parity[0] ^= 1
                return [shifted(parity[0], bank, done, self.col("mu", n), rkv[:, n, :])[0]]

            self.gemm(lambda g: w_in[:, bass.ds(g * 256, 256)], DC, 6, 2, rhs, rkv_evac, None)

            def w_evac(n, bank, done):
                f, end = shifted(0, bank, done, self.col("mu", 12), wlo[:])
                p.act(lambda e: e.activation(wlo[:], wlo[:], ACTF.Tanh), after=end)
                return [f]

            self.gemm(lambda g: w_in[:, 1536:1664], DC, 1, 1, rhs, w_evac, None)
            self.gemm(lambda g: w_in[:, 1664:1728], DC, 1, 1, rhs,
                      lambda n, bank, done: [shifted(1, bank, done, self.col("mu_a", 0, CH), alo[:], CH)[0]], None, m=CH)

            def g_evac(n, bank, done):
                f, end = shifted(0, bank, done, self.col("mu_g"), sglo[:])
                p.act(lambda e: e.activation(sglo[:], sglo[:], ACTF.Sigmoid), after=end)
                return [f]

            self.gemm(lambda g: w_in[:, 1728:1856], DC, 1, 1, rhs, g_evac, None)
            p.meet()
            self.t_st.start(p.sp, lo_dram[0], wlo[:])
            self.t_st.start(p.sp, lo_dram[1, 0:CH], alo[:])
            p.meet(self.t_st.start(p.sp, lo_dram[2], sglo[:]))
        kb = xn
        self.dump("d_rkv", rkv[:])
        with ExitStack() as gs:
            wlo = self.sb(gs, "r_wlo2", [PART, TOK])
            alo = self.sb(gs, "r_alo2", [CH, TOK])
            wup = self.sb(gs, "r_wup", [PART, 2, RW])
            w0 = self.sb(gs, "r_w0", [PART, 2, RW])
            aup = self.sb(gs, "r_aup", [CH, RW])
            sg = self.sb(gs, "r_sg", [PART, 2, 2, RW])
            hones = self.sb(gs, "r_hones", [PART, PART])
            omka = self.sb(gs, "r_omka", [PART, 4])
            a = self.sb(gs, "r_a", [PART, TOK])
            t1 = self.sb(gs, "r_t1", [PART, TOK])
            t2 = self.sb(gs, "r_t2", [PART, TOK])
            z = p.dve(lambda e: e.memset(wup[:], 0.0))
            self.t_misc.start(p.sp, wlo[:], lo_dram[0])
            self.t_misc.start(p.sp, alo[:], lo_dram[1, 0:CH])
            self.t_misc.start(p.sp, hones[:], i["k_head_ones"])
            self.t_misc.start(p.sp, aup[:], i["rwkv_a_up"][0])
            for d in range(2):
                self.t_misc.start(p.sp, wup[CH * d:CH * d + CH, d, :], i["rwkv_w_up"][0, d], after=z)
                self.t_misc.start(p.sp, w0[:, d, :], i["rwkv_w0"][0, d:d + 1, :].to_broadcast([PART, RW]))
            p.meet(self.t_misc.here())
            stored = None
            for n in range(NBLK):
                b = n % 2
                for d in range(2):
                    done = p.pe(lambda e: e.matmul(self.ps[:, 2 * b + d, :], wlo[:, n * PART:(n + 1) * PART], wup[:, d, :],
                                                   start=True, stop=True), after=p.act.counter.here() if d == 0 else None, mark=(d == 1))
                m = p.dve(lambda e: e.tensor_tensor(sg[:, b], self.ps[:, 2 * b:2 * b + 2, :], w0[:], ALU.add),
                          after=[done, self.t_st.here()])
                s = p.act(lambda e: e.activation(sg[:, b], sg[:, b], ACTF.Sigmoid), after=m)
                stored = self.t_st.start(p.sp, sg_dram[:, n].rearrange("d p c -> p d c"), sg[:, b], after=s)
            p.dve(lambda e: e.tensor_scalar(omka[:], self.cols[:, self.cols_at["rwkv_k_a"]:self.cols_at["rwkv_k_a"] + 4], -1.0, 1.0,
                                            ALU.mult, ALU.add))
            for c in range(4):
                kk, bb, k = kb[:, c, :], kb[:, 4 + c, :], rkv[:, 4 + c, :]
                for h in range(2):
                    done = p.pe(lambda e: e.matmul(self.ps[:, 4 + h, :], aup[:, c * PART:(c + 1) * PART], alo[:, h * HALF:(h + 1) * HALF],
                                                   start=True, stop=True), after=p.act.counter.here(), mark=(h == 1))
                av = p.act(lambda e: e.activation(a[:].rearrange("p (h t) -> p h t", h=2), self.ps[:, 4:6, :], ACTF.Sigmoid,
                                                  bias=self.col("rwkv_a0", c)), after=[done, p.dve.counter.here()])
                p.dve(lambda e: e.tensor_scalar(kk, k, self.col("rwkv_k_k", c), None, ALU.mult))
                sq = p.dve(lambda e: e.tensor_tensor(t1[:], kk, kk, ALU.mult))
                for h in range(2):
                    done = p.pe(lambda e: e.matmul(self.ps[:, 6 + h, :], hones[:], t1[:, h * HALF:(h + 1) * HALF], start=True, stop=True),
                                after=sq, mark=(h == 1))
                p.dve(lambda e: e.tensor_scalar(t1[:].rearrange("p (h t) -> p h t", h=2), self.ps[:, 6:8, :], 1e-24, None, ALU.max), after=done)
                self.rsqrt(t1[:], bb, t2[:])
                p.dve(lambda e: e.tensor_tensor(kk, kk, bb, ALU.mult))
                p.dve(lambda e: e.tensor_tensor(bb, kk, a[:], ALU.mult), after=av)
                p.dve(lambda e: e.tensor_scalar(t1[:], a[:], self.col("rwkv_k_a", c), omka[:, c:c + 1], ALU.mult, ALU.add))
                p.dve(lambda e: e.tensor_tensor(k, k, t1[:], ALU.mult))
            p.meet(self.t_st.here())
        self.dump("d_kkb", kb[:])
        self.rwkv_scan(rkv, kb, ycat, sg_dram)
        self.dump("d_ry", ycat[:, 0:4, :])
        with ExitStack() as gs:
            hones = self.sb(gs, "r_hones2", [PART, PART])
            gup = self.sb(gs, "r_gup", [PART, RW])
            sglo = self.sb(gs, "r_sglo2", [PART, TOK])
            mu = self.sb(gs, "r_mu", [PART, TOK])
            t1 = self.sb(gs, "r_u1", [PART, TOK])
            t2 = self.sb(gs, "r_u2", [PART, TOK])
            t3 = self.sb(gs, "r_u3", [PART, TOK])
            self.t_misc.start(p.sp, hones[:], i["k_head_ones"])
            self.t_misc.start(p.sp, gup[:], i["rwkv_g_up"][0])
            self.t_misc.start(p.sp, sglo[:], lo_dram[2])
            p.meet(self.t_misc.here())
            two = lambda x: x.rearrange("p (h t) -> p h t", h=2)

            def head_sum(src, base, after):
                for h in range(2):
                    done = p.pe(lambda e: e.matmul(self.ps[:, base + h, :], hones[:], src[:, h * HALF:(h + 1) * HALF], start=True, stop=True),
                                after=after, mark=(h == 1))
                return done

            for c in range(4):
                y, r, k, v = ycat[:, c, :], rkv[:, c, :], rkv[:, 4 + c, :], rkv[:, 8 + c, :]
                done = head_sum(y, 0, p.dve.counter.here())
                p.dve(lambda e: e.scalar_tensor_tensor(out=two(y), in0=self.ps[:, 0:2, :], scalar=-1.0 / 64, in1=two(y),
                                                       op0=ALU.mult, op1=ALU.add), after=done)
                sq = p.dve(lambda e: e.tensor_tensor(t1[:], y, y, ALU.mult))
                done = head_sum(t1, 2, sq)
                p.dve(lambda e: e.tensor_scalar(two(t1[:]), self.ps[:, 2:4, :], 1.0 / 64, 64e-5, ALU.mult, ALU.add), after=done)
                self.rsqrt(t1[:], t2[:], t3[:])
                p.dve(lambda e: e.tensor_tensor(y, y, t2[:], ALU.mult))
                p.dve(lambda e: e.tensor_scalar(y, y, self.col("rwkv_ln_w", c), self.col("rwkv_ln_b", c), ALU.mult, ALU.add))
                m = p.dve(lambda e: e.scalar_tensor_tensor(out=t1[:], in0=r, scalar=self.col("rwkv_r_k", c), in1=k, op0=ALU.mult, op1=ALU.mult))
                done = head_sum(t1, 4, m)
                p.dve(lambda e: e.tensor_tensor(two(t2[:]), self.ps[:, 4:6, :], two(v), ALU.mult), after=done)
                p.dve(lambda e: e.tensor_tensor(y, y, t2[:], ALU.add))
                for h in range(2):
                    done = p.pe(lambda e: e.matmul(self.ps[:, 6 + h, :], gup[:, c * PART:(c + 1) * PART], sglo[:, h * HALF:(h + 1) * HALF],
                                                   start=True, stop=True), after=p.dve.counter.here(), mark=(h == 1))
                p.dve(lambda e: e.tensor_tensor(two(y), two(y), self.ps[:, 6:8, :], ALU.mult), after=done)
            p.meet()
        st.close()

    def rwkv_scan(self, rkv, kb, ycat, sg_dram):
        p, i = self.p, self.i
        ps = self.ps
        with ExitStack() as ls:
            L8 = LANES
            tri = self.sb(ls, "tri", [PART, 2, 2 * PART])
            gmask = self.sb(ls, "rgmask", [PART, 2, 2 * CH])
            lmask = self.sb(ls, "lmask", [PART, LEVELS, 2, CH])
            eye = self.sb(ls, "eye2", [PART, CH])
            sig = self.sb(ls, "s_sig", [PART, 2, RW])
            Ei = self.sb(ls, "s_Ei", [PART, L8, PART])
            En = self.sb(ls, "s_En", [PART, L8, PART])
            Ex = self.sb(ls, "s_Ex", [PART, L8, PART])
            AR = self.sb(ls, "s_AR", [PART, L8, 2, CH])
            Fb = self.sb(ls, "s_Fb", [PART, L8, PART])
            Bb = self.sb(ls, "s_Bb", [PART, L8, PART])
            Kb = self.sb(ls, "s_Kb", [PART, L8, PART])
            BT = self.sb(ls, "s_BT", [PART, L8, PART])
            KT = self.sb(ls, "s_KT", [PART, L8, PART])
            VT = self.sb(ls, "s_VT", [PART, L8, PART])
            Vc = self.sb(ls, "s_Vc", [PART, L8, CH])
            GB = self.sb(ls, "s_GB", [PART, L8, 2, CH])
            GK = self.sb(ls, "s_GK", [PART, L8, 2, CH])
            Nb = self.sb(ls, "s_Nb", [PART, L8, PART])
            Mk = self.sb(ls, "s_Mk", [PART, L8, PART])
            X = self.sb(ls, "s_X", [PART, L8, CH])
            XT = self.sb(ls, "s_XT", [PART, L8, CH])
            XTb = self.sb(ls, "s_XTb", [PART, L8, PART])
            T1 = self.sb(ls, "s_T1", [PART, L8, CH])
            T1b = self.sb(ls, "s_T1b", [PART, L8, PART])
            U = self.sb(ls, "s_U", [PART, L8, CH])
            S = self.sb(ls, "s_S", [PART, L8, CH])
            Sb = self.sb(ls, "s_Sb", [PART, L8, PART])
            fac = self.sb(ls, "s_fac", [PART, L8, 1])
            for t, n in ((tri, "k_tri"), (gmask, "k_gram_mask"), (lmask, "k_lev_mask"), (eye, "k_stack_eye")):
                v = t[:]
                if len(v.shape) == 3:
                    v = v.rearrange("p a b -> p (a b)")
                elif len(v.shape) == 4:
                    v = v.rearrange("p a b c -> p (a b c)")
                self.t_misc.start(p.sp, v, i[n])
            for t in (Fb[:], Bb[:], Kb[:], Nb[:], Mk[:], XTb[:], T1b[:], S[:], Sb[:], ycat[:, 0:4, :]):
                p.dve(lambda e: e.memset(t, 0.0))
            p.dve(lambda e: e.memset(fac[:], 1.0))
            p.meet(self.t_misc.here())
            HS = [slice(0, 64), slice(64, 128)]
            flat = lambda x: x.rearrange("p a b -> p (a b)")
            two = lambda base: ps[:, base:base + 2, :].rearrange("p a b -> p (a b)")
            l64 = lambda base: ps[:, base, :].rearrange("p (l t) -> p l t", t=CH)
            bank64 = lambda b, l: ps[:, b, l * CH:(l + 1) * CH]
            bank128 = lambda b, l: ps[:, b + l // 4, (l % 4) * PART:(l % 4 + 1) * PART]

            def spread(q, dst, src, after=None, chain=True, scale=None):
                for n, H in enumerate(HS):
                    if q is p.act:
                        done = q(lambda e: e.activation(dst[H, :, H], src[H], ACTF.Copy), after=after, chain=chain and n == 0)
                    else:
                        done = q(lambda e: e.tensor_copy(dst[H, :, H], src[H]), after=after, chain=chain and n == 0)
                return done

            def turn(t, last):
                self.t_in.start(p.sp, sig[:, 0, :], sg_dram[0, t], after=p.pe.counter.here())
                got = self.t_in.start(p.sp, sig[:, 1, :], sg_dram[1, 7 - t])
                p.pe.wait([got, p.act.counter.here(), p.dve.counter.here()])
                for l in range(L8):
                    d, pr = divmod(l, RPAIR)
                    done = p.pe(lambda e: e.matmul(ps[:, l // 2, (l % 2) * 256:(l % 2) * 256 + 256], sig[:, d, pr * PART:(pr + 1) * PART],
                                                   tri[:, d, :], start=True, stop=True), mark=(l == L8 - 1))
                cum = ps[:, 0:4, :].rearrange("p b (l x t) -> p (b l) x t", l=2, x=2)
                p.act(lambda e: e.activation(Ei[:], cum[:, :, 0, :], ACTF.Exp), after=[done, p.dve.counter.here()], chain=False)
                p.act(lambda e: e.activation(En[:], cum[:, :, 0, :], ACTF.Exp, scale=-1.0), chain=False)
                made = p.act(lambda e: e.activation(Ex[:], cum[:, :, 1, :], ACTF.Exp), chain=False)
                for sub in range(2):
                    free = p.pe.counter.here()
                    p.dve.wait([made, free])
                    p.act.wait(free)
                    for d in range(2):
                        u = sub if d == 0 else 1 - sub
                        tok = (t * PART + u * CH) if d == 0 else ((7 - t) * PART + u * CH)
                        L = slice(4 * d, 4 * d + 4)
                        tc = slice(u * CH, (u + 1) * CH)
                        T = bass.ds(tok, CH)
                        p.dve(lambda e: e.tensor_tensor(AR[:, L, 0], kb[:, 0:4, T], Ex[:, L, tc], ALU.mult), chain=False)
                        p.dve(lambda e: e.tensor_tensor(AR[:, L, 1], rkv[:, 0:4, T], Ei[:, L, tc], ALU.mult), chain=False)
                        for H in HS:
                            fb = p.act(lambda e: e.activation(Fb[H, L, H], rkv[H, 8:12, T], ACTF.Copy), chain=False)
                            p.dve(lambda e: e.tensor_tensor(Bb[H, L, H], kb[H, 4:8, T], En[H, L, tc], ALU.mult), chain=False)
                            ready = p.dve(lambda e: e.tensor_tensor(Kb[H, L, H], rkv[H, 4:8, T], En[H, L, tc], ALU.mult), chain=False)
                        end = u * CH + (CH - 1 if d == 0 else 0)
                        p.dve(lambda e: e.tensor_tensor(fac[:, L], fac[:, L], Ei[:, L, end:end + 1], ALU.mult))
                    p.dve(lambda e: e.tensor_tensor(S[:], S[:], rep_last(fac[:], CH), ALU.mult))
                    sready = spread(p.dve, Sb, S)
                    for d in range(2):
                        u = sub if d == 0 else 1 - sub
                        end = u * CH + (CH - 1 if d == 0 else 0)
                        L = slice(4 * d, 4 * d + 4)
                        p.dve(lambda e: e.tensor_copy(fac[:, L], Ei[:, L, end:end + 1]), chain=False)
                    p.pe.wait([ready, fb])
                    for l in range(L8):
                        gb = p.pe(lambda e: e.matmul(bank128(0, l), Bb[:, l, :], flat(AR[:, l]), start=True, stop=True), mark=(l == L8 - 1))
                    for l in range(L8):
                        gk = p.pe(lambda e: e.matmul(bank128(2, l), Kb[:, l, :], flat(AR[:, l]), start=True, stop=True), mark=(l == L8 - 1))
                    for l in range(L8):
                        tv = p.pe(lambda e: e.transpose(bank128(4, l), Fb[:, l, :], self.ident[:]), mark=(l == L8 - 1))
                    for l in range(L8):
                        tb = p.pe(lambda e: e.transpose(bank128(6, l), Bb[:, l, :], self.ident[:]), mark=(l == L8 - 1))
                    for G, base, dn in ((GB, 0, gb), (GK, 2, gk)):
                        for d in range(2):
                            L = slice(4 * d, 4 * d + 4)
                            p.dve(lambda e: e.tensor_tensor(G[:, L].rearrange("p l x t -> p l (x t)"),
                                                            ps[:, base + d, :].rearrange("p (l x) -> p l x", l=4),
                                                            bass_rep(gmask[:, d], 4), ALU.mult), after=dn, chain=False)
                    nb = spread(p.dve, Nb, GB[:, :, 0])
                    mk = spread(p.dve, Mk, GK[:, :, 0], chain=False)
                    v = p.act(lambda e: e.activation(flat(VT[:]), two(4), ACTF.Copy), after=tv, chain=False)
                    v = p.act(lambda e: e.activation(flat(BT[:]), two(6), ACTF.Copy), after=tb, chain=False)
                    for H in HS:
                        vc = p.dve(lambda e: e.tensor_copy(Vc[H], VT[H, :, H]), after=v, chain=False)
                    for l in range(L8):
                        tk = p.pe(lambda e: e.transpose(bank128(6, l), Kb[:, l, :], self.ident[:]), after=v, mark=(l == L8 - 1))
                    kt = p.act(lambda e: e.activation(flat(KT[:]), two(6), ACTF.Copy), after=tk, chain=False)
                    fb = spread(p.act, Fb, AR[:, :, 0], after=[tv, ready], chain=False)
                    p.dve(lambda e: e.tensor_copy(X[:], bass_rep(eye[:], L8)), chain=False)
                    p.dve(lambda e: e.tensor_copy(XT[:], bass_rep(eye[:], L8)), chain=False)
                    xt = spread(p.dve, XTb, XT)
                    for lev in range(LEVELS):
                        p.pe.wait([nb, p.dve.counter.here()])
                        for l in range(L8):
                            lx = p.pe(lambda e: e.matmul(bank64(0, l), Nb[:, l, :], X[:, l, :], start=True, stop=True), mark=(l == L8 - 1))
                        for d in range(2):
                            L = slice(4 * d, 4 * d + 4)
                            t1 = p.dve(lambda e: e.tensor_tensor(T1[:, L], l64(0)[:, L], bass_rep(lmask[:, lev, d], 4), ALU.mult), after=lx,
                                       chain=False)
                        t1b = spread(p.dve, T1b, T1)
                        p.pe.wait(t1)
                        if lev < LEVELS - 1:
                            for l in range(L8):
                                xx = p.pe(lambda e: e.matmul(bank64(1, l), XTb[:, l, :], T1[:, l, :], start=True, stop=True), mark=(l == L8 - 1))
                        p.pe.wait(t1b)
                        for l in range(L8):
                            xy = p.pe(lambda e: e.matmul(bank64(2, l), T1b[:, l, :], XT[:, l, :], start=True, stop=True), mark=(l == L8 - 1))
                        if lev < LEVELS - 1:
                            p.dve(lambda e: e.tensor_tensor(X[:], X[:], l64(1), ALU.subtract), after=xx, chain=False)
                        p.dve(lambda e: e.tensor_tensor(XT[:], XT[:], l64(2), ALU.subtract), after=xy, chain=False)
                        xt = spread(p.dve, XTb, XT)
                    p.pe.wait([sready, fb, mk, vc, kt])
                    for l in range(L8):
                        p.pe(lambda e: e.matmul(bank64(3, l), Fb[:, l, :], S[:, l, :], start=True, stop=False))
                        rh = p.pe(lambda e: e.matmul(bank64(3, l), Mk[:, l, :], Vc[:, l, :], start=False, stop=True), mark=(l == L8 - 1))
                    t1 = p.dve(lambda e: e.tensor_scalar(T1[:], l64(3), -1.0, None, ALU.mult), after=rh, chain=False)
                    p.pe.wait([t1, xt])
                    for l in range(L8):
                        uu = p.pe(lambda e: e.matmul(bank64(0, l), XTb[:, l, :], T1[:, l, :], start=True, stop=True), mark=(l == L8 - 1))
                    u_ = p.dve(lambda e: e.tensor_copy(U[:], l64(0)), after=uu, chain=False)
                    ub = spread(p.dve, T1b, U)
                    p.pe.wait(ub)
                    for l in range(L8):
                        p.pe(lambda e: e.matmul(bank64(4, l), Sb[:, l, :], AR[:, l, 1], start=True, stop=False))
                        p.pe(lambda e: e.matmul(bank64(4, l), T1b[:, l, :], GB[:, l, 1], start=False, stop=False))
                        yy = p.pe(lambda e: e.matmul(bank64(4, l), VT[:, l, :], GK[:, l, 1], start=False, stop=True), mark=(l == L8 - 1))
                    for l in range(L8):
                        p.pe(lambda e: e.matmul(bank64(5, l), BT[:, l, :], U[:, l, :], start=True, stop=False))
                        ss = p.pe(lambda e: e.matmul(bank64(5, l), KT[:, l, :], Vc[:, l, :], start=False, stop=True), mark=(l == L8 - 1))
                    for d in range(2):
                        u = sub if d == 0 else 1 - sub
                        tok = (t * PART + u * CH) if d == 0 else ((7 - t) * PART + u * CH)
                        yv = ycat[:, 0:4, bass.ds(tok, CH)]
                        p.dve(lambda e: e.tensor_tensor(yv, yv, l64(4)[:, 4 * d:4 * d + 4], ALU.add), after=yy)
                    p.dve(lambda e: e.tensor_tensor(S[:], S[:], l64(5), ALU.add), after=ss)

            p.loop(NBLK, turn)
            p.meet()


    def block1_tail(self, A, B):
        p, i = self.p, self.i
        two = lambda x: x.rearrange("p (h t) -> p h t", h=2)
        wide = lambda w, at=0: (lambda g: w[:, bass.ds(g * 256 + at, 256)])
        rhs = lambda x: (lambda k, h: x[:, k, h * HALF:(h + 1) * HALF])

        def keep(dst):
            return lambda n, bank, done: [p.act(lambda e: e.activation(two(dst[:, n, :]), bank, ACTF.Copy), after=done)]

        with ExitStack() as s:
            self.weight_slots(s)
            self.gemm(wide(i["w_out"][0]), DC, 4, 2, rhs(B), keep(A))
            p.meet()
            loaded = self.t_h.start(p.sp, B[:], self.h_dram)
            p.dve.wait(loaded)
            self.add_normed(A, "norm_mix_post", B, s)
            self.dump("d_h1", B[:])
        with ExitStack() as s:
            self.weight_slots(s, 22 * PART)
            hid = self.sb(s, "hid", [PART, DFF // PART, TOK])
            with ExitStack() as s2:
                inv = self.sb(s2, "f_inv", [PART, TOK])
                tmp = self.sb(s2, "f_tmp", [PART, 2, TOK])
                self.rms_inverse(lambda c: B[:, c, :], DC, D, inv[:], tmp)
                self.normed(lambda c: A[:, c, :], lambda c: B[:, c, :], inv[:], "norm_ffn_pre")
                p.meet()
            gate, up = i["ffn_gate"][0], i["ffn_up"][0]

            def gate_up(g, b, bank, done):
                if b == 0:
                    return [p.act(lambda e: e.activation(two(hid[:, g, :]), bank, ACTF.Silu), after=done)]
                return [p.dve(lambda e: e.tensor_tensor(two(hid[:, g, :]), two(hid[:, g, :]), bank, ALU.mult),
                              after=[done, p.act.counter.here()])]

            self.gemm(lambda g: [gate[:, bass.ds(g * PART, PART)], up[:, bass.ds(g * PART, PART)]], DC, DFF // PART, 2, rhs(A),
                      gate_up, split=True)
            p.meet()
            down = i["ffn_down"][0]
            self.gemm(lambda g: down[:, bass.ds(g * PART, PART)], DFF // PART, DC, 1, rhs(hid), keep(A))
            p.meet()
        with ExitStack() as s:
            self.weight_slots(s)
            with ExitStack() as s2:
                self.add_normed(A, "norm_ffn_post", B, s2)
            self.dump("d_h2", B[:])
            E = self.sb(s, "ple_e", [PART, DC, TOK])
            pT = self.sb(s, "pT", [PART, 2, TOK])
            prow = self.sb(s, "p_row", [PART, NBLK, 256])
            tmp = [self.sb(s, f"ple_t{n}", [PART, TOK]) for n in range(2)]
            got = self.t_misc.start(p.sp, prow[:], i["p"].rearrange("a b (n p) c -> p (a b n) c", p=PART), after=p.all_done())
            for c in range(2):
                for t in range(NBLK):
                    done = p.pe(lambda e: e.transpose(self.ps[:, 4 + 2 * c + t // 4, (t % 4) * PART:(t % 4 + 1) * PART],
                                                      prow[:, t, c * PART:(c + 1) * PART], self.ident[:]), after=[got, p.dve.counter.here()],
                                mark=(t == NBLK - 1))
                p.act(lambda e: e.activation(two(pT[:, c, :]), self.ps[:, 4 + 2 * c:6 + 2 * c, :], ACTF.Copy), after=done)
            p.meet()
            self.gemm(wide(i["ple_proj"][0]), 2, 4, 2, rhs(pT), keep(E))
            par = [0]

            def ple(n, bank, done):
                par[0] ^= 1
                t = tmp[par[0]]
                f = p.act(lambda e: e.activation(two(t[:]), bank, ACTF.Sigmoid, bias=self.col("ple_gate_b", n)),
                          after=[done, p.dve.counter.here()])
                p.dve(lambda e: e.tensor_tensor(A[:, n, :], t[:], E[:, n, :], ALU.mult), after=f)
                return [f]

            self.gemm(wide(i["ple_gate"][0]), DC, 4, 2, rhs(B), ple)
            p.meet()
        with ExitStack() as s2:
            self.add_normed(A, "norm_ple", B, s2)
        p.meet(self.t_h.start(p.sp, self.h_dram, B[:], after=p.dve.counter.here()))

    def ada(self, stack):
        p, i = self.p, self.i
        self.mod = self.sb(stack, "mod", [PART, 48, 2])
        self.gain = self.sb(stack, "gain", [PART, 3, DC])
        at = self.cols_at
        cols = lambda n: self.cols[:, at[n]:at[n] + DC]
        with ExitStack() as s:
            self.weight_slots(s, 4096)
            cc = self.sb(s, "cc", [PART, DC, 2])
            p.meet()
            p.act(lambda e: e.activation(cc[:, :, 0], cols("c_2"), ACTF.Silu))
            a = p.act(lambda e: e.activation(cc[:, :, 1], cols("c_ctx"), ACTF.Silu))
            w = i["w_ada_2"][0]
            self.gemm(lambda g: w[:, bass.ds(g * 512, 512)], DC, 12, 4, lambda k, h: cc[:, k, :],
                      lambda n, bank, done: [p.dve(lambda e: e.tensor_scalar(self.mod[:, n, :] if isinstance(n, int) else
                                                                             self.mod[:, bass.ds(n, 1), :].rearrange("p a b -> p (a b)"),
                                                                             bank[:, 0, 0:2], self.col("b_ada_2", n), None, ALU.add),
                                                   after=done)], a, tokens=2)
            for k, (g, sc, who) in enumerate((("norm1_g_2", 8, 0), ("norm1_g_2", 8, 1), ("norm2_g_2", 32, 0))):
                p.dve(lambda e: e.scalar_tensor_tensor(out=self.gain[:, k, :], in0=self.mod[:, sc:sc + DC, who], scalar=1.0, in1=cols(g),
                                                       op0=ALU.add, op1=ALU.mult))
            p.meet()

    def modulated(self, dst, x, inv, gain, shift, who):
        p = self.p
        for c in range(DC):
            p.dve(lambda e: e.scalar_tensor_tensor(out=dst(c), in0=x(c), scalar=self.gain[:, gain, c:c + 1], in1=inv, op0=ALU.mult, op1=ALU.mult))
            p.act(lambda e: e.activation(dst(c), dst(c), ACTF.Identity, bias=self.mod[:, shift + c, who:who + 1]), after=p.dve.counter.here())

    def block2_mixers(self, hxA, Y):
        p, i, nc, ps = self.p, self.i, self.nc, self.ps
        two = lambda x: x.rearrange("p (h t) -> p h t", h=2)
        rhs = lambda k, h: hxA[:, k, h * HALF:(h + 1) * HALF]
        w_in = i["w_in_2"][0]
        st = ExitStack()
        q = self.sb(st, "b_q", [PART, 4, TOK])
        qr = self.sb(st, "b_qr", [PART, 4, TOK])
        kr = self.sb(st, "b_kr", [PART, 4, TOK])
        VV = self.sb(st, "b_VV", [PART, ROWS - 1, RW])
        kc = self.sb(st, "b_kc", [PART, 4, CTX])
        vc = self.sb(st, "b_vc", [PART, 2, RW])
        with ExitStack() as s:
            self.weight_slots(s)
            hc = self.sb(s, "b_hc", [PART, DC, CTX])
            crow = self.sb(s, "b_crow", [PART, 2, D])
            inv = self.sb(s, "b_cinv", [PART, CTX])
            tmp = self.sb(s, "b_ctmp", [PART, 2, CTX])
            wv = self.sb(s, "b_wv", [PART, DC, RW])
            self.t_misc.start(p.sp, wv[:], w_in[:, 1024:1536].rearrange("(c p) n -> p c n", p=PART), after=p.all_done())
            got = self.t_misc.start(p.sp, crow[:], i["ctx_2"].rearrange("a (n p) c -> p (a n) c", p=PART))
            for c in range(DC):
                for n in range(2):
                    done = p.pe(lambda e: e.transpose(ps[:, c // 2, (c % 2) * 256 + n * PART:(c % 2) * 256 + (n + 1) * PART],
                                                      crow[:, n, c * PART:(c + 1) * PART], self.ident[:]), after=got,
                                mark=(c == DC - 1 and n == 1))
            p.act(lambda e: e.activation(hc[:].rearrange("p (b c) t -> p b (c t)", b=4), ps[:, 0:4, :], ACTF.Copy), after=done)
            self.rms_inverse(lambda c: hc[:, c, :], DC, D, inv[:], tmp, tokens=CTX)
            self.modulated(lambda c: hc[:, c, :], lambda c: hc[:, c, :], inv[:], 1, 0, 1)
            p.meet()
            self.gemm(lambda g: w_in[:, bass.ds(g * 256 + 512, 256)], DC, 2, 2, lambda k, h: hc[:, k, :],
                      lambda n, bank, done: [p.act(lambda e: e.activation(kc[:, n, :], bank[:, 0, 0:CTX], ACTF.Copy), after=done)],
                      tokens=CTX)
            p.meet()
            free = [None, None]
            for n in range(NBLK + 2):
                for k in range(DC):
                    src = hxA[:, k, n * PART:(n + 1) * PART] if n < NBLK else hc[:, k, (n - NBLK) * PART:(n - NBLK + 1) * PART]
                    done = p.pe(lambda e: e.matmul(ps[:, n % 2, :], src, wv[:, k, :], start=(k == 0), stop=(k == DC - 1)),
                                after=free[n % 2] if k == 0 else None, mark=(k == DC - 1))
                dst = VV[:, 2 * n, :] if n < NBLK else vc[:, n - NBLK, :]
                free[n % 2] = p.act(lambda e: e.activation(dst, ps[:, n % 2, :], ACTF.Copy), after=done)
            self.t_misc.start(p.sp, VV[0:64, 1:ROWS - 1:2, :], VV[64:128, 0:ROWS - 2:2, :], after=p.act.counter.here())
            p.meet(self.t_misc.start(p.sp, VV[64:128, 1:ROWS - 1:2, :], VV[0:64, 2:ROWS - 1:2, :]))
        self.dump("d_kc", kc[:])
        conv_dram = nc.dram_tensor("conv_dram", (PART, 4, TOK), F32, kind="Internal").ap()
        with ExitStack() as s:
            self.weight_slots(s)
            swap = self.sb(s, "b_swap", [PART, PART])
            cos = self.sb(s, "b_cos", [PART, TOK])
            sin = self.sb(s, "b_sin", [PART, TOK])
            t1 = self.sb(s, "b_t1", [PART, TOK])
            cp = self.sb(s, "b_cp", [PART, 4, TOK + TAPS - 1])
            sg = [self.sb(s, f"b_sg{n}", [PART, TOK]) for n in range(2)]
            for t, n in ((swap, "k_swap"), (cos, "k_rope_cos"), (sin, "k_rope_sin")):
                self.t_misc.start(p.sp, t[:], i[n], after=p.all_done())

            def qk(n, bank, done):
                dst = q[:, n, :] if self.which == 0 else kr[:, n, :]
                return [p.act(lambda e: e.activation(two(dst), bank, ACTF.Copy), after=done)]

            for self.which in range(2):
                self.gemm(lambda g: w_in[:, bass.ds(g * 256 + 512 * self.which, 256)], DC, 2, 2, rhs, qk)
            p.meet(self.t_misc.here())
            for c in range(8):
                src, dst = (q[:, c, :], qr[:, c, :]) if c < 4 else (kr[:, c - 4, :], kr[:, c - 4, :])
                base = 4 + 2 * (c % 2)
                for h in range(2):
                    done = p.pe(lambda e: e.matmul(ps[:, base + h, :], swap[:], src[:, h * HALF:(h + 1) * HALF], start=True, stop=True),
                                after=p.dve.counter.here(), mark=(h == 1))
                p.dve(lambda e: e.tensor_tensor(two(t1[:]), ps[:, base:base + 2, :], two(sin[:]), ALU.mult), after=done)
                p.dve(lambda e: e.tensor_tensor(dst, src, cos[:], ALU.mult))
                p.dve(lambda e: e.tensor_tensor(dst, dst, t1[:], ALU.add))
            pad = TAPS // 2
            p.dve(lambda e: e.memset(cp[:, :, 0:pad], 0.0))
            p.dve(lambda e: e.memset(cp[:, :, pad + TOK:], 0.0))
            p.meet()

            def glu(g, b, bank, done):
                t = sg[0]
                if b == 0:
                    return [p.act(lambda e: e.activation(two(t[:]), bank, ACTF.Sigmoid), after=[done, p.dve.counter.here()])]
                return [p.dve(lambda e: e.tensor_tensor(two(cp[:, g, pad:pad + TOK]), two(t[:]), bank, ALU.mult),
                              after=[done, p.act.counter.here()])]

            self.gemm(lambda g: [w_in[:, bass.ds(g * PART + 2048, PART)], w_in[:, bass.ds(g * PART + 1536, PART)]], DC, 4, 2, rhs, glu,
                      split=True)
            p.meet()

            def conv(n, last):
                o = Y[:, bass.ds(n + 4, 1), :].rearrange("p a t -> p (a t)")
                x = cp[:, bass.ds(n, 1), :].rearrange("p a t -> p (a t)")
                p.dve(lambda e: e.tensor_scalar(o, x[:, 0:TOK], self.col("dw", n), self.col("dw_bias_2", n), ALU.mult, ALU.add))
                for w in range(1, TAPS):
                    p.dve(lambda e: e.scalar_tensor_tensor(out=o, in0=x[:, w:w + TOK], scalar=self.col("dw", n + 4 * w), in1=o,
                                                           op0=ALU.mult, op1=ALU.add))

            p.loop(4, conv)
            p.meet()
        with ExitStack() as s:
            mean = self.sb(s, "b_mean", [PART, TOK])
            inv = self.sb(s, "b_inv", [PART, TOK])
            tmp = self.sb(s, "b_tmp", [PART, 2, TOK])
            p.dve(lambda e: e.tensor_tensor(mean[:], Y[:, 4, :], Y[:, 5, :], ALU.add))
            p.dve(lambda e: e.tensor_tensor(mean[:], mean[:], Y[:, 6, :], ALU.add))
            m = p.dve(lambda e: e.tensor_tensor(mean[:], mean[:], Y[:, 7, :], ALU.add))
            for h in range(2):
                done = p.pe(lambda e: e.matmul(ps[:, h, :], self.ones[:], mean[:, h * HALF:(h + 1) * HALF], start=True, stop=True), after=m,
                            mark=(h == 1))
            for c in range(4):
                y = Y[:, 4 + c, :]
                p.dve(lambda e: e.scalar_tensor_tensor(out=two(y), in0=ps[:, 0:2, :], scalar=-1.0 / RW, in1=two(y), op0=ALU.mult, op1=ALU.add),
                      after=done)
            self.rms_inverse(lambda c: Y[:, 4 + c, :], 4, RW, inv[:], tmp)
            for c in range(4):
                y = Y[:, 4 + c, :]
                m = p.dve(lambda e: e.tensor_tensor(y, y, inv[:], ALU.mult))
                m = p.dve(lambda e: e.tensor_scalar(y, y, self.col("conv_ln_g_2", c), self.col("conv_ln_b_2", c), ALU.mult, ALU.add))
                p.act(lambda e: e.activation(y, y, ACTF.Silu), after=m)
            p.meet()
        self.dump("d_conv", Y[:, 4:8, :])
        self.dump("d_qr", qr[:])
        self.dump("d_kr", kr[:])
        self.attention(q, qr, kr, VV, kc, vc, Y)
        st.close()

    def attention(self, q, qr, kr, VV, kc, vc, Y):
        p, i, nc, ps = self.p, self.i, self.nc, self.ps
        SC = 64 ** -0.5
        K8 = WIN_R * GRID
        pad_dram = nc.dram_tensor("rpb_dram", (HEADS, RPB_R, GRID, PART), F32, kind="Internal").ap()
        with ExitStack() as s:
            bias = self.sb(s, "a_bias", [PART, 4, RPB_R, GRID])
            cmask = self.sb(s, "a_cmask", [PART, GRID])
            eye = self.sb(s, "a_eye", [PART, CH])
            rp = self.sb(s, "a_rp", [HEADS * RPB_R, PART])
            Qb = [self.sb(s, f"a_Qb{n}", [PART, PART]) for n in range(4)]
            Qc = [self.sb(s, f"a_Qc{n}", [PART, PART]) for n in range(4)]
            sc = [self.sb(s, f"a_sc{n}", [PART, K8 + CTX]) for n in range(2)]
            P_ = [self.sb(s, f"a_P{n}", [PART, K8 + CTX]) for n in range(2)]
            PT = [self.sb(s, f"a_PT{n}", [PART, K8 + CTX]) for n in range(2)]
            ob = [self.sb(s, f"a_ob{n}", [PART, PART]) for n in range(2)]
            mx = self.sb(s, "a_mx", [PART, 4])
            sm = self.sb(s, "a_sm", [PART, 4])
            z = p.dve(lambda e: e.memset(rp[:], 0.0))
            for t in (*Qb, *Qc, *ob):
                p.dve(lambda e: e.memset(t[:], 0.0))
            self.t_misc.start(p.sp, cmask[:], i["k_col_mask"], after=z)
            self.t_misc.start(p.sp, eye[:], i["k_stack_eye"])
            a = self.t_misc.start(p.sp, rp[:, 48:48 + RPB_C], i["rpb_2"].rearrange("a h r c -> (a h r) c"))
            a = self.t_misc.start(p.sp, pad_dram.rearrange("h r q c -> (h r) q c"), bass_rep(rp[:], GRID), after=a)
            p.sp.wait(a)
            for h in range(HEADS):
                src = bass.AP(tensor=pad_dram.tensor, offset=h * RPB_R * GRID * PART + GRID - 1,
                              ap=[[PART - 1, GRID], [GRID * PART, RPB_R], [1, GRID]])
                H = (h % 2) * 64
                self.t_misc.start(p.sp, bias[H:H + 64, h // 2, :, :], src)
            p.meet(self.t_misc.here())
            for pr in range(4):
                p.dve(lambda e: e.tensor_tensor(bias[:, pr], bias[:, pr], bass_rep(cmask[:], RPB_R), ALU.add))
            p.meet()
            HS = [slice(0, 64), slice(64, 128)]

            def rows(r, rs, off):
                tok = r * GRID
                key = rs * GRID
                T = bass.ds(tok, GRID)
                p.dve.wait(p.pe.counter.here())
                for pr in range(4):
                    for H in HS:
                        p.dve(lambda e: e.tensor_copy(Qb[pr][H, H], qr[H, pr, T]), chain=False)
                        qd = p.dve(lambda e: e.tensor_copy(Qc[pr][H, H], q[H, pr, T]), chain=False)
                p.pe.wait([qd, p.act.counter.here()])
                exped = {}

                def scores(pr):
                    b = 2 * (pr % 2)
                    p.pe.wait(exped.get(("read", pr - 2)))
                    p.pe(lambda e: e.matmul(ps[:, b, :], Qb[pr][:], kr[:, pr, bass.ds(key, K8)], start=True, stop=True))
                    return p.pe(lambda e: e.matmul(ps[:, b + 1, 0:CTX], Qc[pr][:], kc[:, pr, :], start=True, stop=True), mark=True)

                def softmax(pr, done):
                    b, x = 2 * (pr % 2), pr % 2
                    p.dve(lambda e: e.scalar_tensor_tensor(
                        out=sc[x][:, 0:K8].rearrange("p (r c) -> p r c", c=GRID), in0=ps[:, b, :].rearrange("p (r c) -> p r c", c=GRID), scalar=SC,
                        in1=bias[:, pr, bass.ds(off, WIN_R), :], op0=ALU.mult, op1=ALU.add), after=[done, p.act.counter.here()])
                    exped["read", pr] = p.dve(lambda e: e.tensor_scalar(sc[x][:, K8:], ps[:, b + 1, 0:CTX], SC, None, ALU.mult))
                    p.dve(lambda e: e.tensor_reduce(mx[:, pr:pr + 1], sc[x][:], AX.X, ALU.max))
                    m = p.dve(lambda e: e.tensor_scalar(mx[:, pr:pr + 1], mx[:, pr:pr + 1], -1.0, None, ALU.mult))
                    return p.act(lambda e: e.activation(P_[x][:], sc[x][:], ACTF.Exp, bias=mx[:, pr:pr + 1], accum_out=sm[:, pr:pr + 1]),
                                 after=[m, p.pe.counter.here()])

                def values(pr, done):
                    x = pr % 2
                    p.pe.wait([done, p.dve.counter.here()])
                    for j in range(6):
                        t = p.pe(lambda e: e.transpose(ps[:, 4 + j // 4, (j % 4) * PART:(j % 4 + 1) * PART], P_[x][:, j * PART:(j + 1) * PART],
                                                       self.ident[:]), mark=(j == 5))
                    p.act(lambda e: e.activation(PT[x][:, 0:512], ps[:, 4, :], ACTF.Copy), after=t, chain=False)
                    c = p.act(lambda e: e.activation(PT[x][:, 512:], ps[:, 5, 0:256], ACTF.Copy), chain=False)
                    p.pe.wait(c)
                    for j in range(6):
                        v = VV[:, bass.ds(rs + 2 * j, 1), pr * PART:(pr + 1) * PART].rearrange("p a b -> p (a b)") if j < 4 \
                            else vc[:, j - 4, pr * PART:(pr + 1) * PART]
                        o = p.pe(lambda e: e.matmul(ps[:, 6, 0:PART], PT[x][:, j * PART:(j + 1) * PART], v, start=(j == 0), stop=(j == 5)),
                                 mark=(j == 5))
                    p.dve(lambda e: e.reciprocal(sm[:, pr:pr + 1], sm[:, pr:pr + 1]), after=o)
                    for H in HS:
                        n = p.dve(lambda e: e.tensor_scalar(ob[x][H, H], ps[H, 6, H], sm[H, pr:pr + 1], None, ALU.mult))
                    f = p.pe(lambda e: e.matmul(ps[:, 7, 0:GRID], ob[x][:], eye[:], start=True, stop=True), after=[n, p.act.counter.here()],
                             mark=True)
                    p.act(lambda e: e.activation(Y[:, pr, T], ps[:, 7, 0:GRID], ACTF.Copy), after=f)

                nxt = scores(0)
                for pr in range(4):
                    done = softmax(pr, nxt)
                    if pr < 3:
                        nxt = scores(pr + 1)
                    values(pr, done)

            lo, hi = WIN_R // 2, ROWS - WIN_R // 2
            p.loop(lo, lambda t, last: rows(t, 0, t * -1 + WIN_R - 1))
            p.loop(hi - lo, lambda t, last: rows(t + lo, t, WIN_R - 1 - lo))
            p.loop(ROWS - hi, lambda t, last: rows(t + hi, ROWS - WIN_R, t * -1 + WIN_R - 1 - lo))
            p.meet()
        self.dump("d_attn", Y[:, 0:4, :])

    def block2(self):
        p, i, ps = self.p, self.i, self.ps
        two = lambda x: x.rearrange("p (h t) -> p h t", h=2)
        st = ExitStack()
        self.ada(st)
        A = self.sb(st, "A2", [PART, DC, TOK])
        with ExitStack() as s:
            Y = self.sb(s, "Y2", [PART, DC, TOK])
            with ExitStack() as s2:
                inv = self.sb(s2, "b2_inv", [PART, TOK])
                tmp = self.sb(s2, "b2_tmp", [PART, 2, TOK])
                h = Y
                p.dve.wait(self.t_h.start(p.sp, h[:], self.h_dram, after=p.all_done()))
                p.act.wait(self.t_h.here())
                self.rms_inverse(lambda c: h[:, c, :], DC, D, inv[:], tmp)
                self.modulated(lambda c: A[:, c, :], lambda c: h[:, c, :], inv[:], 0, 0, 0)
                p.meet()
            self.dump("d_hx", A[:])
            self.block2_mixers(A, Y)
            self.weight_slots(s)
            h = A
            loaded = self.t_h.start(p.sp, h[:], self.h_dram, after=p.all_done())
            p.dve.wait(loaded)
            w = i["w_out_2"][0]

            def mix_out(n, bank, done):
                g1 = self.mod[:, 16 + n, 0:1] if isinstance(n, int) else self.mod[:, bass.ds(n + 16, 1), 0]
                return [p.dve(lambda e: e.scalar_tensor_tensor(out=two(h[:, n, :]), in0=bank, scalar=g1, in1=two(h[:, n, :]),
                                                               op0=ALU.mult, op1=ALU.add), after=done)]

            self.gemm(lambda g: w[:, bass.ds(g * 256, 256)], DC, 4, 2, lambda k, hh: Y[:, k, hh * HALF:(hh + 1) * HALF], mix_out)
            p.meet(self.t_h.start(p.sp, self.h_dram, h[:], after=p.dve.counter.here()))
        self.dump("d_h4", A[:])
        with ExitStack() as s:
            hid = self.sb(s, "hid2", [PART, DFF2 // PART, TOK])
            with ExitStack() as s2:
                inv = self.sb(s2, "m_inv", [PART, TOK])
                tmp = self.sb(s2, "m_tmp", [PART, 2, TOK])
                self.rms_inverse(lambda c: A[:, c, :], DC, D, inv[:], tmp)
                self.modulated(lambda c: A[:, c, :], lambda c: A[:, c, :], inv[:], 2, 24, 0)
                p.meet()
            with ExitStack() as s2:
                self.weight_slots(s2, 4096)
                w1, w2 = i["w_mlp1_2"][0], i["w_mlp2_2"][0]

                def relu2(n, bank, done):
                    f = p.act(lambda e: e.activation(two(hid[:, n, :]), bank, ACTF.Relu), after=done)
                    p.dve(lambda e: e.tensor_tensor(hid[:, n, :], hid[:, n, :], hid[:, n, :], ALU.mult), after=f)
                    return [f]

                self.gemm(lambda g: w1[:, bass.ds(g * 256, 256)], DC, 16, 2, lambda k, hh: A[:, k, hh * HALF:(hh + 1) * HALF], relu2)
                p.meet()

                def gated(n, bank, done):
                    g2 = self.mod[:, 40 + n, 0:1] if isinstance(n, int) else self.mod[:, bass.ds(n + 40, 1), 0]
                    return [p.dve(lambda e: e.tensor_scalar(two(A[:, n, :]), bank, g2, None, ALU.mult), after=done)]

                self.gemm(lambda g: w2[:, bass.ds(g * PART, PART)], DFF2 // PART, DC, 1, lambda k, hh: hid[:, k, hh * HALF:(hh + 1) * HALF],
                          gated)
                p.meet()
        with ExitStack() as s:
            h = self.sb(s, "h_last", [PART, DC, TOK])
            inv = self.sb(s, "l_inv", [PART, TOK])
            tmp = self.sb(s, "l_tmp", [PART, 2, TOK])
            row = [self.sb(s, f"o_row{n}", [PART, D]) for n in range(2)]
            loaded = self.t_h.start(p.sp, h[:], self.h_dram, after=p.all_done())
            p.dve.wait(loaded)
            for c in range(DC):
                p.dve(lambda e: e.tensor_tensor(h[:, c, :], h[:, c, :], A[:, c, :], ALU.add))
            self.rms_inverse(lambda c: h[:, c, :], DC, D, inv[:], tmp)
            self.normed(lambda c: h[:, c, :], lambda c: h[:, c, :], inv[:], "final_g")
            out = self.out.rearrange("b (n p) c -> n p (b c)", p=PART)
            p.meet()
            t_out = [Transfer(p, "t_out0"), Transfer(p, "t_out1")]
            copied = [None, None]
            for t in range(NBLK):
                x = t % 2
                for c in range(DC):
                    done = p.pe(lambda e: e.transpose(ps[:, 2 * x + c // 4, (c % 4) * PART:(c % 4 + 1) * PART], h[:, c, t * PART:(t + 1) * PART],
                                                      self.ident[:]), after=copied[x] if c == 0 else None, mark=(c == DC - 1))
                copied[x] = p.act(lambda e: e.activation(two(row[x][:]), ps[:, 2 * x:2 * x + 2, :], ACTF.Copy), after=[done, t_out[x].here()])
                t_out[x].start(p.sp, out[t], row[x][:], after=copied[x])
            p.meet(t_out[0].here(), t_out[1].here())
        st.close()

    def block1(self):
        with ExitStack() as s:
            B = self.sb(s, "B1", [PART, DC, TOK])
            A = self.sb(s, "A1", [PART, DC, TOK])
            with ExitStack() as s2:
                self.load_x(A, s2)
            self.gla(A, B)
            self.rwkv(A, B)
            self.block1_tail(A, B)


def bass_rep(ap, n):
    return ap.unsqueeze(1).to_broadcast([ap.shape[0], n] + list(ap.shape[1:]))


def rep_mid(ap, n):
    return ap.unsqueeze(2).to_broadcast([ap.shape[0], ap.shape[1], n, ap.shape[2]])


def rep_last(ap, n):
    return ap.to_broadcast([ap.shape[0], ap.shape[1], n])


def kernel(**inputs):
    import concourse.bacc as bacc
    from concourse.bass_utils import run_bass_kernel_spmd

    nc = bacc.Bacc("TRN2", target_bir_lowering=False, num_devices=1)
    given = {name: np.ascontiguousarray(a) for name, a in inputs.items()}
    given.update({f"k_{name}": a for name, a in constants().items()})
    ins, arrays = {}, {}
    for name, a in given.items():
        arrays[f"in_{name}_dram"] = a
        ins[name] = nc.dram_tensor(f"in_{name}_dram", a.shape, F32, kind="ExternalInput").ap()
    out = nc.dram_tensor("out_dram", (1, TOK, D), F32, kind="ExternalOutput").ap()
    k = Kernel(nc, ins, out)
    with ExitStack() as stack:
        k.setup(stack)
        k.block1()
        k.block2()
    r = run_bass_kernel_spmd(nc, [arrays], core_ids=[0])
    return r.results[0]["out_dram"]
```

```python
import math
from contextlib import ExitStack

import numpy as np

import concourse.bass as bass
from concourse import mybir

F32 = mybir.dt.float32
ALU = mybir.AluOpType
ACTF = mybir.ActivationFunctionType
AX = mybir.AxisListType

PART = 128
TOK = 1024
HALF = 512
D = 1024
DC = D // PART
CH = 64
NBLK = TOK // PART
RW = 512
RPAIR = 4
LANES = 2 * RPAIR
LEVELS = 6
GPAIR = 2
GLEV = LEVELS + 1
GSLOT = GLEV + 2
DFF = 2816
DFF2 = 4096
CTX = 256
HEADS = 8
GRID = 64
ROWS = TOK // GRID
WIN_R, WIN_C = 8, 16
RPB_R, RPB_C = 2 * WIN_R - 1, 2 * WIN_C - 1
TAPS = 31
NEG = -1.0e30
DECAY = -math.exp(-0.5)


def constants():
    c = {}
    f = np.float32
    c["ident"] = np.eye(PART, dtype=f)
    t = np.arange(PART)
    same = (t[:, None] // CH) == (t[None, :] // CH)
    tri = np.zeros((2, PART, 2, PART), f)
    s, q = t[:, None], t[None, :]
    for d, (inc, exc) in enumerate((((s <= q), (s < q)), ((s >= q), (s > q)))):
        tri[d, :, 0] = DECAY * np.where(same, inc.astype(f) - 0.5, 0)
        tri[d, :, 1] = DECAY * np.where(same, exc.astype(f) - 0.5, 0)
    c["tri"] = np.ascontiguousarray(tri.transpose(1, 0, 2, 3)).reshape(PART, -1)
    g = np.zeros((2, PART, GSLOT, PART), f)
    for d in range(2):
        pos = (t % CH) if d == 0 else (CH - 1 - t % CH)
        ps, pq = pos[:, None], pos[None, :]
        for lev in range(1, GLEV):
            w = 2 ** (lev - 1)
            mid = (pq // (2 * w)) * 2 * w + w
            m = np.where(pq >= mid, (ps >= mid) & (ps <= pq), (ps > pq) & (ps < mid))
            g[d, :, lev] = m & same
        g[d, :, GLEV] = (ps <= pq) & same
        g[d, :, GLEV + 1] = (ps > pq) & same
    g /= 16.0
    c["gsum"] = np.ascontiguousarray(g.transpose(1, 0, 2, 3)).reshape(PART, -1)
    tt = np.arange(CH)
    m = np.zeros((CH, 2, 2, CH), f)
    m[:, 0, 0] = tt[:, None] < tt[None, :]
    m[:, 0, 1] = tt[:, None] <= tt[None, :]
    m[:, 1, 0] = tt[:, None] > tt[None, :]
    m[:, 1, 1] = tt[:, None] >= tt[None, :]
    c["gram_mask"] = np.tile(m.reshape(CH, -1), (2, 1))
    lm = np.zeros((CH, LEVELS, 2, CH), f)
    gm = np.zeros((CH, 2, GLEV, CH), f)
    for d in range(2):
        pos = tt if d == 0 else CH - 1 - tt
        gm[:, d, 0] = np.eye(CH)
        for lev in range(LEVELS):
            w = 2 ** lev
            blk = pos // (2 * w)
            late = (pos % (2 * w)) >= w
            lm[:, lev, d] = (blk[:, None] == blk[None, :]) & late[:, None] & ~late[None, :]
            gm[:, d, lev + 1] = (blk[:, None] == blk[None, :]) & ~late[:, None] & late[None, :]
    c["lev_mask"] = np.tile(lm.reshape(CH, -1), (2, 1))
    c["gla_mask"] = np.tile(gm.reshape(CH, -1), (2, 1))
    c["stack_eye"] = np.tile(np.eye(CH, dtype=f), (2, 1))
    hb = (t[:, None] // CH) == (t[None, :] // CH)
    c["head_ones"] = hb.astype(f)
    c["head_sel"] = np.stack([t < CH, t >= CH], 1).astype(f)
    n = 16
    inv = (np.float32(10000.0) ** (-np.arange(n, dtype=f) / n)).astype(f)
    tok = np.arange(TOK)
    ch = np.arange(64)
    p = np.where((ch < 32)[:, None], (tok // GRID)[None, :], (tok % GRID)[None, :]).astype(f)
    ang = (p * inv[ch % n][:, None]).astype(f)
    sign = np.where((ch % 32) < 16, -1.0, 1.0).astype(f)[:, None]
    c["rope_cos"] = np.tile(np.cos(ang), (2, 1)).astype(f)
    c["rope_sin"] = np.tile(np.sin(ang) * sign, (2, 1)).astype(f)
    c["swap"] = (s == (q ^ 16)).astype(f)
    cs = np.clip(np.arange(GRID) - WIN_C // 2, 0, GRID - WIN_C)
    inside = (np.arange(GRID)[None, :] >= cs[:, None]) & (np.arange(GRID)[None, :] < cs[:, None] + WIN_C)
    c["col_mask"] = np.tile(np.where(inside, 0.0, NEG).astype(f), (2, 1))
    return c


class Done:

    def __init__(self, counter, count, per, turn):
        self.counter, self.count, self.per, self.turn = counter, count, per, turn

    def before(self):
        assert self.count >= self.per
        return Done(self.counter, self.count - self.per, self.per, self.turn)


class Counter:
    def __init__(self, prog, name, step):
        self.sem, self.step = prog.nc.alloc_semaphore(name), step
        self.prog, self.count, self.per = prog, 0, 0
        prog.counters.append(self)

    def here(self):
        return Done(self, self.count, self.per, self.prog.turn)


class Queue:

    def __init__(self, prog, name, eng, chained):
        self.prog, self.eng, self.chained = prog, eng, chained
        self.counter = Counter(prog, name, 1)
        self.seen = {}

    def wait(self, done):
        if self.prog.dry or done is None:
            return
        if isinstance(done, (list, tuple)):
            for d in done:
                self.wait(d)
            return
        key = (done.counter, done.per)
        if done.count <= self.seen.get(key, 0) or (done.count == 0 and not done.per):
            return
        self.seen[key] = done.count
        step = done.counter.step
        value = done.count * step
        if done.per:
            assert done.count > 0
            value = done.turn * (done.per * step) + value
        self.eng.wait_ge(done.counter.sem, value)

    def __call__(self, make, after=None, mark=None, chain=None):
        self.wait(after)
        if self.chained if chain is None else chain:
            self.wait(self.counter.here())
        if self.chained if mark is None else mark:
            self.counter.count += 1
            if not self.prog.dry:
                make(self.eng).then_inc(self.counter.sem, 1)
        elif not self.prog.dry:
            make(self.eng)
        return self.counter.here()


class Transfer:

    def __init__(self, prog, name):
        self.prog, self.counter = prog, Counter(prog, name, 16)

    def start(self, queue, out, in_, after=None):
        queue.wait(after)
        self.counter.count += 1
        if not self.prog.dry:
            queue.eng.dma_start(out, in_).then_inc(self.counter.sem, 16)
        return self.counter.here()

    def here(self):
        return self.counter.here()


class Prog:
    def __init__(self, nc):
        self.nc, self.counters, self.dry, self.turn = nc, [], False, None
        self.pe = Queue(self, "pe", nc.tensor, False)
        self.act = Queue(self, "act", nc.scalar, True)
        self.dve = Queue(self, "dve", nc.vector, True)
        self.pool = Queue(self, "pool", nc.gpsimd, True)
        self.sp = Queue(self, "sp", nc.sync, False)
        self.engines = (self.pe, self.act, self.dve, self.pool)

    def loop(self, turns, body):
        if turns <= 0:
            return
        start = [c.count for c in self.counters]
        self.dry = True
        left = body(0, None)
        self.dry = False
        for c, s in zip(self.counters, start):
            c.per, c.count = c.count - s, s
        seen = [dict(q.seen) for q in (*self.engines, self.sp)]
        with self.nc.Fori(0, turns) as turn:
            self.turn = turn
            last = None
            if left is not None:
                last = {k: [Done(d.counter, d.count, d.counter.per, turn).before() for d in v]
                        for k, v in left.items()}
            body(turn, last)
        self.turn = None
        for c, s in zip(self.counters, start):
            assert c.count == s + c.per
            c.count, c.per = s + c.per * turns, 0
        for q, s in zip((*self.engines, self.sp), seen):
            q.seen = s

    def all_done(self):
        return [q.counter.here() for q in self.engines]

    def meet(self, *more):
        done = [*self.all_done(), *more]
        for q in (*self.engines, self.sp):
            q.wait(done)


class Columns:

    def __init__(self):
        self.rows, self.at = [], {}
        self.n = 0

    def add(self, name, ap2d):
        self.at[name] = self.n
        r = 0
        n = ap2d.shape[0]
        while r < n:
            k = min(n - r, PART - self.n % PART)
            self.rows.append((self.n, k, ap2d[r:r + k, :]))
            self.n += k
            r += k


def blocks(ap):
    return ap.rearrange("(n p) -> n p", p=PART)


class Kernel:
    def __init__(self, nc, ins, out, only=None, dumps=None):
        self.nc, self.i, self.out = nc, ins, out
        self.p = Prog(nc)
        self.only, self.dumps, self.made = only, dumps or {}, 0
        self.ps = nc.alloc_psum_tensor("ps", [PART, 8, HALF], F32)
        self.t_misc = Transfer(self.p, "t_misc")
        self.t_w = [Transfer(self.p, "t_w0"), Transfer(self.p, "t_w1")]
        self.t_h = Transfer(self.p, "t_h")
        self.t_st = Transfer(self.p, "t_st")
        self.t_in = Transfer(self.p, "t_in")
        self.h_dram = ins.get("h_dram")
        if self.h_dram is None:
            self.h_dram = nc.dram_tensor("h_dram", (PART, DC, TOK), F32, kind="Internal").ap()

    def sb(self, stack, name, shape):
        self.made = self.made + 1
        return stack.enter_context(self.nc.sbuf_tensor(f"{name}_{self.made}", shape, F32))

    def dump(self, name, ap):
        if name in self.dumps:
            self.p.meet()
            self.t_misc.start(self.p.sp, self.dumps[name], ap)
            self.p.meet(self.t_misc.here())

    def col(self, name, k=0, rows=PART):
        at = self.cols_at[name]
        if isinstance(k, int):
            return self.cols[0:rows, at + k:at + k + 1]
        return self.cols[0:rows, bass.ds(k + at, 1)]

    def setup(self, stack):
        p, i = self.p, self.i
        c = Columns()
        for n in ("norm_mix_pre", "norm_mix_post", "norm_ffn_pre", "norm_ffn_post", "norm_ple", "ple_gate_b",
                  "rwkv_a0", "rwkv_k_k", "rwkv_k_a", "rwkv_ln_w", "rwkv_ln_b", "norm1_g_2", "norm2_g_2",
                  "b_ada_2", "dw_bias_2", "conv_ln_g_2", "conv_ln_b_2"):
            c.add(n, i[n].rearrange("a (n p) -> (a n) p", p=PART))
        c.add("rwkv_r_k", i["rwkv_r_k"].rearrange("a (n two) p -> (a n) (two p)", two=2))
        mu = i["rwkv_mu"]
        c.add("mu", mu[:, 0:3 * RW + PART].rearrange("a (n p) -> (a n) p", p=PART))
        c.add("mu_g", mu[:, 1728:1856])
        c.add("mu_a", mu[:, 1664:1728])
        c.add("gla_norm", i["gla_norm"])
        c.add("conv", i["gla_conv"].rearrange("a w b (n p) -> (a w b n) p", p=PART))
        c.add("dw", i["dw_kernel_2"].rearrange("a w (n p) -> (a w n) p", p=PART))
        c.add("final_g", blocks(i["final_g_2"]))
        c.add("c_2", i["c_2"].rearrange("a (n p) -> (a n) p", p=PART))
        c.add("c_ctx", blocks(i["c_ctx_2"]))
        self.cols_at = c.at
        nt = -(-c.n // PART)
        self.cols = self.sb(stack, "cols", [PART, nt * PART])
        self.ident = self.sb(stack, "ident", [PART, PART])
        self.ones = self.sb(stack, "ones", [PART, PART])
        self.st = self.sb(stack, "small", [PART, 3, 64])
        self.t_misc.start(p.sp, self.ident[:], i["k_ident"])
        p.dve(lambda e: e.memset(self.ones[:], 1.0))
        with ExitStack() as tmp:
            rows = self.sb(tmp, "rows", [PART, nt, PART])
            zeroed = p.dve(lambda e: e.memset(rows[:], 0.0))
            for at, k, src in c.rows:
                w = src.shape[1]
                self.t_misc.start(p.sp, rows[at % PART:at % PART + k, at // PART, 0:w], src, after=zeroed)
            for t in range(nt):
                done = p.pe(lambda e: e.transpose(self.ps[:, 0, t * PART:(t + 1) * PART], rows[:, t, :],
                                                  self.ident[:]), after=self.t_misc.here(), mark=True)
            p.dve(lambda e: e.tensor_copy(self.cols[:], self.ps[:, 0, 0:nt * PART]), after=done)
            p.meet()

    def weight_slots(self, stack, cols=2048):
        self.w = [self.sb(stack, f"w{s}", [PART, cols]) for s in range(2)]

    def gemm(self, weights, kc, groups, nb, rhs, evac, after=None, tokens=TOK, m=PART, split=False):
        p = self.p
        nh = -(-tokens // HALF)
        tw = min(tokens, HALF)
        slot = [w[:, 0:kc * nb * m].rearrange("p (c n) -> p c n", c=kc) for w in self.w]
        free = {0: list(p.all_done()), 1: list(p.all_done())}

        def load(g, s, freed):
            parts = weights(g) if split else [weights(g)]
            for b, w in enumerate(parts):
                wide = w.shape[1]
                self.t_w[s].start(p.sp, slot[s][:, :, b * wide:(b + 1) * wide], w.rearrange("(c p) n -> p c n", p=PART),
                                  after=freed)

        def compute(g, s):
            loaded = self.t_w[s].here()
            for b in range(nb):
                pair = (s * nb + b) % 2
                bank = self.ps[:, 2 * pair:2 * pair + 2, :]
                p.pe.wait(loaded)
                p.pe.wait(free[pair])
                for h in range(nh):
                    for k in range(kc):
                        done = p.pe(lambda e: e.matmul(bank[0:m, h, 0:tw], slot[s][:, k, b * m:(b + 1) * m],
                                                       rhs(k, h), start=(k == 0), stop=(k == kc - 1)),
                                    mark=(h == nh - 1 and k == kc - 1))
                free[pair] = evac(g, b, bank, done) if split else evac(g * nb + b, bank, done)
            return done

        p.pe.wait(after)
        start = p.all_done()
        load(0, 0, start)
        if groups > 1:
            load(1, 1, start)
        turns = groups // 2 - 1
        if turns < 2:
            turns = 0

        def turn(t, last):
            if last is not None:
                free[0], free[1] = last["f0"], last["f1"]
            for s in range(2):
                used = compute(t * 2 + s, s)
                load(t * 2 + s + 2, s, used)
            return {"f0": free[0], "f1": free[1]}

        if turns:
            p.pe.wait([free[0], free[1]])
            p.loop(turns, turn)
            free[0] = free[1] = p.all_done()
        for g in range(2 * turns, groups):
            used = compute(g, g % 2)
            if g + 2 < groups:
                load(g + 2, g % 2, used)
        return p.all_done()

    def token_sums(self, src, sel, col, after, tokens=TOK):
        p = self.p
        nb = tokens // PART
        p.pe.wait(after)
        for t in range(nb):
            done = p.pe(lambda e: e.matmul(self.ps[:, 4, col + 2 * t:col + 2 * t + 2], src[:, t * PART:(t + 1) * PART], sel,
                                           start=True, stop=True), mark=(t == nb - 1))
        return done

    def rsqrt_small(self, n, after, op0, c0, op1=None, c1=None):
        p = self.p
        v, y, t = (self.st[:, k, 0:n] for k in range(3))
        m = p.dve(lambda e: e.tensor_scalar(v, self.ps[:, 4, 0:n], c0, c1, op0, op1) if op1 is not None else
                  e.tensor_scalar(v, self.ps[:, 4, 0:n], c0, None, op0), after=after)
        done = p.act(lambda e: e.activation(y, v, ACTF.Sqrt), after=m)
        p.dve(lambda e: e.reciprocal(y, y), after=done)
        p.dve(lambda e: e.tensor_tensor(t, y, y, ALU.mult))
        p.dve(lambda e: e.tensor_tensor(t, t, v, ALU.mult))
        p.dve(lambda e: e.tensor_scalar(t, t, -0.5, 1.5, ALU.mult, ALU.add))
        return p.dve(lambda e: e.tensor_tensor(y, y, t, ALU.mult))

    def over_channels(self, cols, tmp, after, bank=6):
        p = self.p
        nb, heads = cols.shape[1], cols.shape[2]
        w = PART // heads
        wide = tmp[:, 0:nb * PART].rearrange("p (b h w) -> p b h w", b=nb, h=heads)
        src = cols.unsqueeze(3).to_broadcast([PART, nb, heads, w])
        m = p.dve(lambda e: e.tensor_copy(wide, src), after=[after, p.pe.counter.here()])
        p.pe.wait(m)
        for t in range(nb):
            done = p.pe(lambda e: e.transpose(self.ps[:, bank + t // 4, (t % 4) * PART:(t % 4 + 1) * PART], tmp[:, t * PART:(t + 1) * PART],
                                              self.ident[:]), mark=(t == nb - 1))
        return done

    def rms_inverse(self, x, nblk, width, inv, tmp, tokens=TOK, eps=1e-6):
        p = self.p
        nb = tokens // PART
        start = p.all_done()
        added = [start, start]
        for c in range(nblk):
            dst = inv if c == 0 else tmp[:, c % 2, :]
            sq = p.act(lambda e: e.activation(dst, x(c), ACTF.Square), after=added[c % 2], chain=False)
            if c:
                added[c % 2] = p.dve(lambda e: e.tensor_tensor(inv, inv, tmp[:, c % 2, :], ALU.add), after=[sq, start])
        sums = self.token_sums(inv, self.ones[:, 0:2], 0, [sq, added, start], tokens)
        m = self.rsqrt_small(2 * nb, sums, ALU.mult, 1.0 / width, ALU.add, eps)
        y = self.st[:, 1, 0:2 * nb].rearrange("p (b two) -> p b two", two=2)[:, :, 0:1]
        done = self.over_channels(y, tmp[:, 0, :] if nb * PART <= tokens else None, m)
        nh = -(-tokens // HALF)
        tw = min(tokens, HALF)
        done = p.act(lambda e: e.activation(inv.rearrange("p (h t) -> p h t", h=nh), self.ps[:, 6:6 + nh, 0:tw], ACTF.Copy), after=done)
        p.dve.wait(done)
        return done

    def normed(self, dst, x, inv, name, nblk=DC):
        p = self.p
        for c in range(nblk):
            p.dve(lambda e: e.scalar_tensor_tensor(out=dst(c), in0=x(c), scalar=self.col(name, c), in1=inv,
                                                   op0=ALU.mult, op1=ALU.mult))

    def add_normed(self, y, name, h, stack):
        p = self.p
        inv = self.sb(stack, "an_inv", [PART, TOK])
        tmp = self.sb(stack, "an_tmp", [PART, 2, TOK])
        self.rms_inverse(lambda c: y[:, c, :], DC, D, inv[:], tmp)
        self.normed(lambda c: y[:, c, :], lambda c: y[:, c, :], inv[:], name)
        for c in range(DC):
            p.dve(lambda e: e.tensor_tensor(h[:, c, :], h[:, c, :], y[:, c, :], ALU.add))
        p.meet()

    def load_x(self, xn, stack):
        p = self.p
        x = self.i["x"].rearrange("b (n p) c -> n p (b c)", p=PART)
        row = self.sb(stack, "x_row", [PART, D])
        p.meet()

        def turn(t, last):
            got = self.t_in.start(p.sp, row[:], x[t], after=p.pe.counter.here())
            p.pe.wait([got, p.dve.counter.here()])
            for c in range(DC):
                done = p.pe(lambda e: e.transpose(self.ps[:, c // 4, (c % 4) * PART:(c % 4 + 1) * PART],
                                                  row[:, c * PART:(c + 1) * PART], self.ident[:]), mark=(c == DC - 1))
            p.dve(lambda e: e.tensor_copy(
                xn[:, :, bass.ts(t, PART)].rearrange("p (a b) t -> p a b t", b=4),
                self.ps[:, 0:2, :].rearrange("p a (b t) -> p a b t", t=PART)), after=done)

        p.loop(NBLK, turn)
        kept = self.t_h.start(p.sp, self.h_dram, xn[:], after=p.dve.counter.here())
        inv = self.sb(stack, "x_inv", [PART, TOK])
        tmp = self.sb(stack, "x_tmp", [PART, 2, TOK])
        self.rms_inverse(lambda c: xn[:, c, :], DC, D, inv[:], tmp)
        p.dve.wait(kept)
        self.normed(lambda c: xn[:, c, :], lambda c: xn[:, c, :], inv[:], "norm_mix_pre")
        p.meet()

    def gla(self, xn, ycat):
        p, i, nc = self.p, self.i, self.nc
        w_in = i["w_in"].rearrange("a k n -> (a k) n")
        st = ExitStack()
        qkv = self.sb(st, "g_qkv", [PART, 8, TOK])
        gate = self.sb(st, "g_gate", [PART, 4, TOK])
        la_dram = nc.dram_tensor("la_dram", (NBLK, PART, 512), F32, kind="Internal").ap()
        p.meet()
        with ExitStack() as gs:
            self.weight_slots(gs)
            zp = [self.sb(gs, f"g_zp{s}", [PART, TOK + 2]) for s in range(2)]
            cv = [self.sb(gs, f"g_cv{s}", [PART, TOK]) for s in range(2)]
            alo = self.sb(gs, "g_alo", [32, TOK])
            aup = self.sb(gs, "g_aup", [32, 512])
            ab = self.sb(gs, "g_ab", [PART, 512])
            la = self.sb(gs, "g_la", [PART, NBLK, 512])
            lb = self.sb(gs, "g_lb", [PART, NBLK, 512])
            for z in zp:
                p.dve(lambda e: e.memset(z[:, 0:1], 0.0))
                p.dve(lambda e: e.memset(z[:, TOK + 1:TOK + 2], 0.0))
            zeroed = p.dve(lambda e: e.memset(aup[:], 0.0))
            for d in range(2):
                self.t_misc.start(p.sp, aup[16 * d:16 * d + 16, 256 * d:256 * d + 256], i["gla_a_up"][0, d], after=zeroed)
                self.t_misc.start(p.sp, ab[:, 256 * d:256 * d + 256], i["gla_a_b"][0, d:d + 1, :].to_broadcast([PART, 256]))

            parity = [0]

            def conv_evac(n, bank, done):
                parity[0] ^= 1
                z, o = zp[parity[0]], cv[parity[0]]
                free = p.act(lambda e: e.activation(z[:, 1:TOK + 1].rearrange("p (h t) -> p h t", h=2), bank, ACTF.Copy),
                             after=done)
                p.dve(lambda e: e.tensor_scalar(o[:], z[:, 0:TOK], self.col("conv", n), None, ALU.mult), after=free)
                p.dve(lambda e: e.scalar_tensor_tensor(out=o[:], in0=z[:, 1:TOK + 1], scalar=self.col("conv", n + 8),
                                                       in1=o[:], op0=ALU.mult, op1=ALU.add))
                c = p.dve(lambda e: e.scalar_tensor_tensor(out=o[:], in0=z[:, 2:TOK + 2], scalar=self.col("conv", n + 16),
                                                           in1=o[:], op0=ALU.mult, op1=ALU.add))
                p.act(lambda e: e.activation(qkv[:, n, :], o[:], ACTF.Silu), after=c)
                return [free]

            self.gemm(lambda g: w_in[:, bass.ds(g * 256 + 1856, 256)], DC, 4, 2, lambda k, h: xn[:, k, h * HALF:(h + 1) * HALF],
                      conv_evac, None)

            def gate_evac(n, bank, done):
                return [p.act(lambda e: e.activation(gate[:, n, :].rearrange("p (h t) -> p h t", h=2), bank, ACTF.Silu),
                              after=done)]

            self.gemm(lambda g: w_in[:, bass.ds(g * 256 + 2880, 256)], DC, 2, 2, lambda k, h: xn[:, k, h * HALF:(h + 1) * HALF],
                      gate_evac, None)

            def alo_evac(n, bank, done):
                return [p.act(lambda e: e.activation(alo[:].rearrange("p (h t) -> p h t", h=2), bank[0:32], ACTF.Copy), after=done)]

            self.gemm(lambda g: w_in[:, 3392:3424], DC, 1, 1, lambda k, h: xn[:, k, h * HALF:(h + 1) * HALF], alo_evac, None, m=32)
            p.act(lambda e: e.activation(qkv[:, 0:2, :], qkv[:, 0:2, :], ACTF.Copy, scale=CH ** -0.5))
            p.meet(self.t_misc.here())
            for n in range(NBLK):
                done = p.pe(lambda e: e.matmul(self.ps[:, n, :], alo[:, n * PART:(n + 1) * PART], aup[:], start=True, stop=True),
                            mark=True)
            abb = bass_rep(ab[:], NBLK)
            p.dve(lambda e: e.tensor_tensor(la[:], self.ps[:], abb, ALU.add), after=done)
            m = p.dve(lambda e: e.scalar_tensor_tensor(out=lb[:], in0=la[:], scalar=-1.0, in1=la[:], op0=ALU.mult, op1=ALU.min))
            a = p.act(lambda e: e.activation(lb[:], lb[:], ACTF.Exp), after=m)
            a = p.act(lambda e: e.activation(lb[:], lb[:], ACTF.Ln, bias=1.0))
            p.dve(lambda e: e.tensor_scalar(la[:], la[:], 0.0, None, ALU.min))
            m = p.dve(lambda e: e.tensor_tensor(la[:], la[:], lb[:], ALU.subtract), after=a)
            kept = self.t_misc.start(p.sp, la_dram.rearrange("n p c -> p n c"), la[:], after=m)
            p.meet(kept)
        self.dump("d_qkv", qkv[:])
        with ExitStack() as ls:
            gsum = self.sb(ls, "gsum", [PART, 2, GSLOT, PART])
            mask = self.sb(ls, "gmask", [PART, 2, GLEV, CH])
            lat = self.sb(ls, "g_lat", [PART, 2, 256])
            E = self.sb(ls, "g_E", [PART, 4, GSLOT, PART])
            Qs = self.sb(ls, "g_Qs", [PART, 4, GLEV, CH])
            Qe = self.sb(ls, "g_Qe", [PART, 4, PART])
            Kb = self.sb(ls, "g_Kb", [PART, 4, GLEV + 1, PART])
            VT = self.sb(ls, "g_VT", [PART, 4, PART])
            KeT = self.sb(ls, "g_KeT", [PART, 4, PART])
            VP = self.sb(ls, "g_VP", [PART, 4, PART])
            SM = self.sb(ls, "g_SM", [PART, 4, GLEV, CH])
            Pc = self.sb(ls, "g_Pc", [PART, 4, CH])
            Pb = self.sb(ls, "g_Pb", [PART, 4, PART])
            S = self.sb(ls, "g_S", [PART, 4, PART])
            self.t_misc.start(p.sp, gsum[:].rearrange("p a b c -> p (a b c)"), i["k_gsum"])
            self.t_misc.start(p.sp, mask[:].rearrange("p a b c -> p (a b c)"), i["k_gla_mask"])
            for t in (Qe, Kb, Pb, S):
                p.dve(lambda e: e.memset(t[:], 0.0))
            p.dve(lambda e: e.memset(ycat[:, 4:8, :], 0.0))
            p.dve(lambda e: e.memset(E[:, :, 0, :], 1.0))
            p.meet(self.t_misc.here())

            def turn(t, last):
                self.t_in.start(p.sp, lat[:, 0, :], la_dram[t, :, 0:256], after=p.pe.counter.here())
                got = self.t_in.start(p.sp, lat[:, 1, :], la_dram[7 - t, :, 256:512])
                p.pe.wait([got, p.act.counter.here(), p.dve.counter.here()])
                for d in range(2):
                    for pr in range(2):
                        for s in range(2):
                            done = p.pe(lambda e: e.matmul(self.ps[:, 4 * d + 2 * pr + s, :], lat[:, d, pr * PART:(pr + 1) * PART],
                                                           gsum[:, d, 1 + 4 * s:5 + 4 * s, :], start=True, stop=True),
                                        mark=True)
                for l in range(4):
                    made = p.act(lambda e: e.activation(E[:, l, 1:GSLOT, :].rearrange("p a b -> p (a b)"),
                                                        self.ps[:, 2 * l:2 * l + 2, :].rearrange("p a b -> p (a b)"), ACTF.Exp),
                                 after=[done, p.dve.counter.here()])
                p.pool.wait(made)
                for sub in range(2):
                    for d in range(2):
                        u = sub if d == 0 else 1 - sub
                        tok = (t * PART + u * CH) if d == 0 else (t * -PART + (7 * PART + u * CH))
                        eu = E[:, 2 * d:2 * d + 2, :, u * CH:(u + 1) * CH]
                        L = slice(2 * d, 2 * d + 2)
                        p.dve.wait([made, p.pe.counter.here()])
                        q = qkv[:, 0:2, bass.ds(tok, CH)]
                        p.dve(lambda e: e.tensor_tensor(Qs[:, L], rep_mid(q, GLEV), eu[:, :, 0:GLEV], ALU.mult), chain=False)
                        for h in range(2):
                            H = slice(64 * h, 64 * h + 64)
                            qh, kh = qkv[H, 0:2, bass.ds(tok, CH)], qkv[H, 2:4, bass.ds(tok, CH)]
                            p.dve(lambda e: e.tensor_tensor(Qe[H, L, H], qh, eu[H, :, GLEV], ALU.mult), chain=False)
                            p.dve(lambda e: e.tensor_tensor(Kb[H, L, 0:GLEV, H], rep_mid(kh, GLEV), eu[H, :, 0:GLEV], ALU.mult),
                                  chain=False)
                            ready = p.dve(lambda e: e.tensor_tensor(Kb[H, L, GLEV, H], kh, eu[H, :, GLEV + 1], ALU.mult), chain=False)
                        vsrc = qkv[:, 4:8, bass.ds(tok, CH)]
                        vready = p.act(lambda e: e.activation(VT[:, L].rearrange("p l (h t) -> p (l h) t", h=2), vsrc, ACTF.Copy),
                                       after=p.pe.counter.here(), chain=False)
                    p.pe.wait([ready, vready])
                    for l in range(4):
                        p.pe(lambda e: e.transpose(self.ps[:, 0, l * PART:(l + 1) * PART], Kb[:, l, GLEV, :], self.ident[:]))
                    for l in range(4):
                        tr = p.pe(lambda e: e.transpose(self.ps[:, 1, l * PART:(l + 1) * PART], VT[:, l, :], self.ident[:]), mark=(l == 3))
                    for l in range(4):
                        for v in range(GLEV):
                            sc = p.pe(lambda e: e.matmul(self.ps[:, 2 + l, v * CH:(v + 1) * CH], Kb[:, l, v, :], Qs[:, l, v, :],
                                                         start=True, stop=True), mark=(l == 3 and v == GLEV - 1))
                    p.act(lambda e: e.activation(KeT[:].rearrange("p a b -> p (a b)"), self.ps[:, 0, :], ACTF.Copy), after=tr, chain=False)
                    tv = p.act(lambda e: e.activation(VP[:].rearrange("p a b -> p (a b)"), self.ps[:, 1, :], ACTF.Copy), chain=False)
                    for d in range(2):
                        L = slice(2 * d, 2 * d + 2)
                        p.dve(lambda e: e.tensor_tensor(SM[:, L].rearrange("p l v t -> p l (v t)"), self.ps[:, 2 + 2 * d:4 + 2 * d, 0:GLEV * CH],
                                                        bass_rep(mask[:, d].rearrange("p v t -> p (v t)"), 2), ALU.mult), after=sc, chain=False)
                    p.dve(lambda e: e.tensor_reduce(Pc[:], SM[:].rearrange("p l v t -> p l t v"), AX.X, ALU.add))
                    for h in range(2):
                        H = slice(64 * h, 64 * h + 64)
                        pb = p.dve(lambda e: e.tensor_copy(Pb[H, :, H], Pc[H]), chain=(h == 0))
                    p.pe.wait([pb, tv])
                    for l in range(4):
                        p.pe(lambda e: e.matmul(self.ps[:, 6, l * PART:(l + 1) * PART], VP[:, l, :], Pb[:, l, :], start=True, stop=False))
                        p.pe(lambda e: e.matmul(self.ps[:, 6, l * PART:(l + 1) * PART], S[:, l, :], Qe[:, l, :], start=False, stop=True))
                    for l in range(4):
                        od = p.pe(lambda e: e.matmul(self.ps[:, 7, l * PART:(l + 1) * PART], KeT[:, l, :], VP[:, l, :], start=True, stop=True),
                                  mark=(l == 3))
                    p.dve.wait(od)
                    for d in range(2):
                        u = sub if d == 0 else 1 - sub
                        tok = (t * PART + u * CH) if d == 0 else (t * -PART + (7 * PART + u * CH))
                        end = u * CH + (CH - 1 if d == 0 else 0)
                        yv = ycat[:, 4:8, bass.ds(tok, CH)]
                        p.dve(lambda e: e.tensor_tensor(yv, yv, self.ps[:, 6, 256 * d:256 * d + 256].rearrange("p (a t) -> p a t", t=CH),
                                                        ALU.add), chain=(d == 1))
                        p.dve(lambda e: e.tensor_tensor(S[:, 2 * d:2 * d + 2], S[:, 2 * d:2 * d + 2],
                                                        rep_last(E[:, 2 * d:2 * d + 2, GLEV, end:end + 1], PART), ALU.mult), chain=False)
                    p.dve(lambda e: e.tensor_tensor(S[:].rearrange("p a b -> p (a b)"), S[:].rearrange("p a b -> p (a b)"), self.ps[:, 7, :], ALU.add))
                    p.pe.wait(p.dve.counter.here())

            p.loop(NBLK, turn)
            p.meet()
        self.dump("d_glao", ycat[:, 4:8, :])
        with ExitStack() as ps_:
            inv = self.sb(ps_, "g_inv", [PART, TOK])
            tmp = self.sb(ps_, "g_tmp", [PART, 2, TOK])
            for h in range(4):
                self.rms_inverse(lambda c: ycat[:, 4 + h, :], 1, PART, inv[:], tmp)
                p.dve(lambda e: e.scalar_tensor_tensor(out=ycat[:, 4 + h, :], in0=ycat[:, 4 + h, :], scalar=self.col("gla_norm"),
                                                       in1=inv[:], op0=ALU.mult, op1=ALU.mult))
                p.dve(lambda e: e.tensor_tensor(ycat[:, 4 + h, :], ycat[:, 4 + h, :], gate[:, h, :], ALU.mult))
            p.meet()
        st.close()

    def rwkv(self, xn, ycat):
        p, i, nc = self.p, self.i, self.nc
        w_in = i["w_in"].rearrange("a k n -> (a k) n")
        sg_dram = nc.dram_tensor("sg_dram", (2, NBLK, PART, RW), F32, kind="Internal").ap()
        lo_dram = nc.dram_tensor("lo_dram", (3, PART, TOK), F32, kind="Internal").ap()
        st = ExitStack()
        rkv = self.sb(st, "r_rkv", [PART, 12, TOK])
        p.meet()
        with ExitStack() as gs:
            self.weight_slots(gs)
            zp = [self.sb(gs, f"r_zp{s}", [PART, TOK + 2]) for s in range(2)]
            sh = [self.sb(gs, f"r_sh{s}", [PART, TOK]) for s in range(2)]
            wlo = self.sb(gs, "r_wlo", [PART, TOK])
            alo = self.sb(gs, "r_alo", [CH, TOK])
            sglo = self.sb(gs, "r_sglo", [PART, TOK])
            for z in zp:
                p.dve(lambda e: e.memset(z[:, 0:1], 0.0))
                p.dve(lambda e: e.memset(z[:, TOK + 1:TOK + 2], 0.0))

            def shifted(par, bank, done, mu, dst, rows=PART):
                z, s = zp[par], sh[par]
                free = p.act(lambda e: e.activation(z[0:rows, 1:TOK + 1].rearrange("p (h t) -> p h t", h=2), bank[0:rows], ACTF.Copy),
                             after=[done, p.dve.counter.here()])
                p.dve(lambda e: e.tensor_tensor(s[0:rows], z[0:rows, 0:TOK], z[0:rows, 2:TOK + 2], ALU.add), after=free)
                p.dve(lambda e: e.scalar_tensor_tensor(out=s[0:rows], in0=s[0:rows], scalar=0.5, in1=z[0:rows, 1:TOK + 1],
                                                       op0=ALU.mult, op1=ALU.subtract))
                end = p.dve(lambda e: e.scalar_tensor_tensor(out=dst, in0=s[0:rows], scalar=mu, in1=z[0:rows, 1:TOK + 1],
                                                             op0=ALU.mult, op1=ALU.add))
                return free, end

            rhs = lambda k, h: xn[:, k, h * HALF:(h + 1) * HALF]
            parity = [0]

            def rkv_evac(n, bank, done):
                parity[0] ^= 1
                return [shifted(parity[0], bank, done, self.col("mu", n), rkv[:, n, :])[0]]

            self.gemm(lambda g: w_in[:, bass.ds(g * 256, 256)], DC, 6, 2, rhs, rkv_evac, None)

            def w_evac(n, bank, done):
                f, end = shifted(0, bank, done, self.col("mu", 12), wlo[:])
                p.act(lambda e: e.activation(wlo[:], wlo[:], ACTF.Tanh), after=end)
                return [f]

            self.gemm(lambda g: w_in[:, 1536:1664], DC, 1, 1, rhs, w_evac, None)
            self.gemm(lambda g: w_in[:, 1664:1728], DC, 1, 1, rhs,
                      lambda n, bank, done: [shifted(1, bank, done, self.col("mu_a", 0, CH), alo[:], CH)[0]], None, m=CH)

            def g_evac(n, bank, done):
                f, end = shifted(0, bank, done, self.col("mu_g"), sglo[:])
                p.act(lambda e: e.activation(sglo[:], sglo[:], ACTF.Sigmoid), after=end)
                return [f]

            self.gemm(lambda g: w_in[:, 1728:1856], DC, 1, 1, rhs, g_evac, None)
            p.meet()
            self.t_st.start(p.sp, lo_dram[0], wlo[:])
            self.t_st.start(p.sp, lo_dram[1, 0:CH], alo[:])
            p.meet(self.t_st.start(p.sp, lo_dram[2], sglo[:]))
        kb = xn
        self.dump("d_rkv", rkv[:])
        with ExitStack() as gs:
            wlo = self.sb(gs, "r_wlo2", [PART, TOK])
            alo = self.sb(gs, "r_alo2", [CH, TOK])
            wup = self.sb(gs, "r_wup", [PART, 2, RW])
            w0 = self.sb(gs, "r_w0", [PART, 2, RW])
            aup = self.sb(gs, "r_aup", [CH, RW])
            sg = self.sb(gs, "r_sg", [PART, 2, 2, RW])
            hsel = self.sb(gs, "r_hsel", [PART, 2])
            omka = self.sb(gs, "r_omka", [PART, 4])
            a = self.sb(gs, "r_a", [PART, TOK])
            t1 = self.sb(gs, "r_t1", [PART, TOK])
            t2 = self.sb(gs, "r_t2", [PART, TOK])
            z = p.dve(lambda e: e.memset(wup[:], 0.0))
            self.t_misc.start(p.sp, wlo[:], lo_dram[0])
            self.t_misc.start(p.sp, alo[:], lo_dram[1, 0:CH])
            self.t_misc.start(p.sp, hsel[:], i["k_head_sel"])
            self.t_misc.start(p.sp, aup[:], i["rwkv_a_up"][0])
            for d in range(2):
                self.t_misc.start(p.sp, wup[CH * d:CH * d + CH, d, :], i["rwkv_w_up"][0, d], after=z)
                self.t_misc.start(p.sp, w0[:, d, :], i["rwkv_w0"][0, d:d + 1, :].to_broadcast([PART, RW]))
            p.meet(self.t_misc.here())
            stored = None
            for n in range(NBLK):
                b = n % 2
                for d in range(2):
                    done = p.pe(lambda e: e.matmul(self.ps[:, 2 * b + d, :], wlo[:, n * PART:(n + 1) * PART], wup[:, d, :],
                                                   start=True, stop=True), after=p.act.counter.here() if d == 0 else None, mark=(d == 1))
                m = p.dve(lambda e: e.tensor_tensor(sg[:, b], self.ps[:, 2 * b:2 * b + 2, :], w0[:], ALU.add),
                          after=[done, self.t_st.here()])
                s = p.act(lambda e: e.activation(sg[:, b], sg[:, b], ACTF.Sigmoid), after=m)
                stored = self.t_st.start(p.sp, sg_dram[:, n].rearrange("d p c -> p d c"), sg[:, b], after=s)
            p.dve(lambda e: e.tensor_scalar(omka[:], self.cols[:, self.cols_at["rwkv_k_a"]:self.cols_at["rwkv_k_a"] + 4], -1.0, 1.0,
                                            ALU.mult, ALU.add))
            t12, freed = (t1, t2), [None, None]
            for c in range(4):
                kk, k = kb[:, c, :], rkv[:, 4 + c, :]
                p.dve(lambda e: e.tensor_scalar(kk, k, self.col("rwkv_k_k", c), None, ALU.mult))
                sq = p.dve(lambda e: e.tensor_tensor(t12[c % 2][:], kk, kk, ALU.mult), after=freed[c % 2])
                freed[c % 2] = sums = self.token_sums(t12[c % 2], hsel[:], 16 * c, sq)
            m = self.rsqrt_small(64, sums, ALU.max, 1e-24)
            for c in range(4):
                kk, bb, k = kb[:, c, :], kb[:, 4 + c, :], rkv[:, 4 + c, :]
                spread = self.over_channels(self.st[:, 1, 16 * c:16 * c + 16].rearrange("p (b h) -> p b h", h=2), t2, m)
                p.pe.wait(p.act.counter.here())
                for h in range(2):
                    done = p.pe(lambda e: e.matmul(self.ps[:, h, :], aup[:, c * PART:(c + 1) * PART], alo[:, h * HALF:(h + 1) * HALF],
                                                   start=True, stop=True), mark=(h == 1))
                av = p.act(lambda e: e.activation(a[:].rearrange("p (h t) -> p h t", h=2), self.ps[:, 0:2, :], ACTF.Sigmoid,
                                                  bias=self.col("rwkv_a0", c)), after=[done, p.dve.counter.here()])
                p.dve(lambda e: e.tensor_tensor(kk.rearrange("p (h t) -> p h t", h=2), kk.rearrange("p (h t) -> p h t", h=2),
                                                self.ps[:, 6:8, :], ALU.mult), after=spread)
                p.dve(lambda e: e.tensor_tensor(bb, kk, a[:], ALU.mult), after=av)
                p.dve(lambda e: e.tensor_scalar(t1[:], a[:], self.col("rwkv_k_a", c), omka[:, c:c + 1], ALU.mult, ALU.add))
                p.dve(lambda e: e.tensor_tensor(k, k, t1[:], ALU.mult))
            p.meet(self.t_st.here())
        self.dump("d_kkb", kb[:])
        self.rwkv_scan(rkv, kb, ycat, sg_dram)
        self.dump("d_ry", ycat[:, 0:4, :])
        with ExitStack() as gs:
            hones = self.sb(gs, "r_hones2", [PART, PART])
            hsel = self.sb(gs, "r_hsel2", [PART, 2])
            gup = self.sb(gs, "r_gup", [PART, RW])
            sglo = self.sb(gs, "r_sglo2", [PART, TOK])
            mu = self.sb(gs, "r_mu", [PART, TOK])
            t1 = self.sb(gs, "r_u1", [PART, TOK])
            t2 = self.sb(gs, "r_u2", [PART, TOK])
            t3 = self.sb(gs, "r_u3", [PART, TOK])
            self.t_misc.start(p.sp, hones[:], i["k_head_ones"])
            self.t_misc.start(p.sp, hsel[:], i["k_head_sel"])
            self.t_misc.start(p.sp, gup[:], i["rwkv_g_up"][0])
            self.t_misc.start(p.sp, sglo[:], lo_dram[2])
            p.meet(self.t_misc.here())
            two = lambda x: x.rearrange("p (h t) -> p h t", h=2)

            def head_sum(src, base, after):
                for h in range(2):
                    done = p.pe(lambda e: e.matmul(self.ps[:, base + h, :], hones[:], src[:, h * HALF:(h + 1) * HALF], start=True, stop=True),
                                after=after, mark=(h == 1))
                return done

            t12, freed = (t1, t3), [None, None]
            for c in range(4):
                y = ycat[:, c, :]
                done = head_sum(y, 2 * (c % 2), p.dve.counter.here())
                p.dve(lambda e: e.scalar_tensor_tensor(out=two(y), in0=self.ps[:, 2 * (c % 2):2 * (c % 2) + 2, :], scalar=-1.0 / 64, in1=two(y),
                                                       op0=ALU.mult, op1=ALU.add), after=done)
                sq = p.dve(lambda e: e.tensor_tensor(t12[c % 2][:], y, y, ALU.mult), after=freed[c % 2])
                freed[c % 2] = sums = self.token_sums(t12[c % 2], hsel[:], 16 * c, sq)
            m = self.rsqrt_small(64, sums, ALU.mult, 1.0 / 64, ALU.add, 64e-5)
            for c in range(4):
                y, r, k, v = ycat[:, c, :], rkv[:, c, :], rkv[:, 4 + c, :], rkv[:, 8 + c, :]
                spread = self.over_channels(self.st[:, 1, 16 * c:16 * c + 16].rearrange("p (b h) -> p b h", h=2), t3, m)
                p.dve(lambda e: e.tensor_tensor(two(y), two(y), self.ps[:, 6:8, :], ALU.mult), after=spread)
                p.dve(lambda e: e.tensor_scalar(y, y, self.col("rwkv_ln_w", c), self.col("rwkv_ln_b", c), ALU.mult, ALU.add))
                m_ = p.dve(lambda e: e.scalar_tensor_tensor(out=t1[:], in0=r, scalar=self.col("rwkv_r_k", c), in1=k, op0=ALU.mult, op1=ALU.mult))
                done = head_sum(t1, 2, m_)
                p.dve(lambda e: e.tensor_tensor(two(t2[:]), self.ps[:, 2:4, :], two(v), ALU.mult), after=done)
                p.dve(lambda e: e.tensor_tensor(y, y, t2[:], ALU.add))
                for h in range(2):
                    done = p.pe(lambda e: e.matmul(self.ps[:, 0 + h, :], gup[:, c * PART:(c + 1) * PART], sglo[:, h * HALF:(h + 1) * HALF],
                                                   start=True, stop=True), after=p.dve.counter.here(), mark=(h == 1))
                p.dve(lambda e: e.tensor_tensor(two(y), two(y), self.ps[:, 0:2, :], ALU.mult), after=done)
            p.meet()
        st.close()

    def rwkv_scan(self, rkv, kb, ycat, sg_dram):
        p, i, ps = self.p, self.i, self.ps
        pe, act, dve = p.pe, p.act, p.dve
        DIRS = range(2)
        with ExitStack() as ls:
            tri = self.sb(ls, "tri", [PART, 2, 2 * PART])
            gmask = self.sb(ls, "gram_mask", [PART, 2, 2, CH])
            lmask = self.sb(ls, "lev_mask", [PART, LEVELS, 2, CH])
            eye = self.sb(ls, "eye", [PART, CH])
            sig = self.sb(ls, "sig", [PART, 2, RW])
            Ei, En, Ex = (self.sb(ls, f"s_{n}", [PART, LANES, PART]) for n in ("Ei", "En", "Ex"))
            AR = self.sb(ls, "s_AR", [PART, LANES, 2, CH])
            bd = {n: self.sb(ls, f"s_{n}", [PART, LANES, PART])
                  for n in ("Vb", "Ab", "Bb", "Kb", "Nb", "Mk", "XTb", "Tb", "Sb", "BT", "KT", "VT")}
            Vb, Ab, Bb, Kb, Nb, Mk, XTb, Tb, Sb, BT, KT, VT = bd.values()
            cm = {n: self.sb(ls, f"s_{n}", [PART, LANES, CH]) for n in ("Vc", "Mrb", "Mrk", "X", "XT", "T", "Rn", "S")}
            Vc, Mrb, Mrk, X, XT, T, Rn, S = cm.values()
            fac = self.sb(ls, "s_fac", [PART, LANES, 1])
            for t, n in ((tri[:].rearrange("p a b -> p (a b)"), "k_tri"), (gmask[:].rearrange("p a b c -> p (a b c)"), "k_gram_mask"),
                         (lmask[:].rearrange("p a b c -> p (a b c)"), "k_lev_mask"), (eye[:], "k_stack_eye")):
                self.t_misc.start(p.sp, t, i[n])
            for t in (Vb[:], Ab[:], Bb[:], Kb[:], Nb[:], Mk[:], XTb[:], Tb[:], S[:], Sb[:], ycat[:, 0:4, :]):
                dve(lambda e: e.memset(t, 0.0), chain=False)
            dve(lambda e: e.memset(fac[:], 1.0), chain=False)
            p.meet(self.t_misc.here())
            HS = [slice(0, 64), slice(64, 128)]
            L = [slice(0, 4), slice(4, 8)]
            lanes = [range(0, 4), range(4, 8)]
            half_bank = lambda d, b: ps[:, 4 * d + b, 0:256].rearrange("p (l t) -> p l t", t=CH)
            full_bank = lambda d, b: ps[:, 4 * d + b, :].rearrange("p (l t) -> p l t", t=PART)

            def each(d, b, width, lhsT, rhs, after, start=True, stop=True):
                pe.wait(after)
                for l in lanes[d]:
                    at = (l - 4 * d) * width
                    done = pe(lambda e: e.matmul(ps[:, 4 * d + b, at:at + width], lhsT(l), rhs(l), start=start, stop=stop),
                              mark=(l == lanes[d][-1]))
                return done

            def sums(d, b, terms, after):
                pe.wait(after)
                for l in lanes[d]:
                    at = (l - 4 * d) * CH
                    for n, (lhsT, rhs) in enumerate(terms):
                        done = pe(lambda e: e.matmul(ps[:, 4 * d + b, at:at + CH], lhsT(l), rhs(l), start=(n == 0), stop=(n == len(terms) - 1)),
                                  mark=(l == lanes[d][-1] and n == len(terms) - 1))
                return done

            def turned(d, b, src, after):
                pe.wait(after)
                for l in lanes[d]:
                    at = (l - 4 * d) * PART
                    done = pe(lambda e: e.transpose(ps[:, 4 * d + b, at:at + PART], src[:, l, :], self.ident[:]), mark=(l == lanes[d][-1]))
                return done

            def spread(dst, d, src, after):
                for H in HS:
                    done = act(lambda e: e.activation(dst[H, L[d], H], src(H), ACTF.Copy), after=after, chain=False)
                return done

            def turn(t, last):
                before = p.all_done()
                self.t_in.start(p.sp, sig[:, 0, :], sg_dram[0, t], after=before)
                got = self.t_in.start(p.sp, sig[:, 1, :], sg_dram[1, 7 - t])
                made = [None, None]
                pe.wait([got, before])
                for d in DIRS:
                    for l in lanes[d]:
                        x = l - 4 * d
                        done = pe(lambda e: e.matmul(ps[:, 4 * d + x // 2, (x % 2) * 256:(x % 2) * 256 + 256],
                                                     sig[:, d, x * PART:(x + 1) * PART], tri[:, d, :], start=True, stop=True), mark=(x == 3))
                    cum = ps[:, 4 * d:4 * d + 2, :].rearrange("p b (l x t) -> p (b l) x t", l=2, x=2)
                    act(lambda e: e.activation(Ex[:, L[d]], cum[:, :, 1, :], ACTF.Exp), after=[done, before], chain=False)
                    act(lambda e: e.activation(En[:, L[d]], cum[:, :, 0, :], ACTF.Exp, scale=-1.0), chain=False)
                    made[d] = act(lambda e: e.activation(Ei[:, L[d]], cum[:, :, 0, :], ACTF.Exp), chain=False)
                end = [before, before]
                for sub in range(2):
                    where = [(t * PART + sub * CH, sub), (t * -PART + (7 * PART + (1 - sub) * CH), 1 - sub)]
                    ab, kr, vb, sc, sb = ([None, None] for _ in range(5))
                    for d in DIRS:
                        tok, u = where[d]
                        tc, W = slice(u * CH, (u + 1) * CH), bass.ds(tok, CH)
                        last_tok = u * CH + (CH - 1 if d == 0 else 0)
                        vb[d] = spread(Vb, d, lambda H: rkv[H, 8:12, W], end[d])
                        dve.wait([end[d], made[d]])
                        dve(lambda e: e.tensor_tensor(AR[:, L[d], 0], kb[:, 0:4, W], Ex[:, L[d], tc], ALU.mult), chain=False)
                        for H in HS:
                            dve(lambda e: e.tensor_tensor(Bb[H, L[d], H], kb[H, 4:8, W], En[H, L[d], tc], ALU.mult), chain=False)
                        ab[d] = dve(lambda e: e.tensor_tensor(AR[:, L[d], 1], rkv[:, 0:4, W], Ei[:, L[d], tc], ALU.mult), chain=False)
                        for H in HS:
                            kr[d] = dve(lambda e: e.tensor_tensor(Kb[H, L[d], H], rkv[H, 4:8, W], En[H, L[d], tc], ALU.mult), chain=False)
                        f = dve(lambda e: e.tensor_tensor(fac[:, L[d]], fac[:, L[d]], Ei[:, L[d], last_tok:last_tok + 1], ALU.mult), chain=False)
                        sc[d] = dve(lambda e: e.tensor_tensor(S[:, L[d]], S[:, L[d]], rep_last(fac[:, L[d]], CH), ALU.mult), after=f, chain=False)
                        dve(lambda e: e.tensor_copy(fac[:, L[d]], Ei[:, L[d], last_tok:last_tok + 1]), after=sc[d], chain=False)
                    gb, gk, tv, tb, tk = ([None, None] for _ in range(5))
                    for d in DIRS:
                        gb[d] = each(d, 0, PART, lambda l: Bb[:, l, :], lambda l: AR[:, l].rearrange("p a b -> p (a b)"), [ab[d], end[d]])
                        gk[d] = each(d, 1, PART, lambda l: Kb[:, l, :], lambda l: AR[:, l].rearrange("p a b -> p (a b)"), kr[d])
                        tv[d] = turned(d, 2, Vb, vb[d])
                        tb[d] = turned(d, 3, Bb, None)
                    nb, mk, mr, vt, vc, bt, kt, af = ([None, None] for _ in range(8))
                    for d in DIRS:
                        for H in HS:
                            nb[d] = dve(lambda e: e.tensor_tensor(Nb[H, L[d], H], full_bank(d, 0)[H, :, 0:CH], bass_rep(gmask[H, d, 0], 4), ALU.mult),
                                        after=gb[d], chain=False)
                        af[d] = spread(Ab, d, lambda H: AR[H, L[d], 0], ab[d])
                    for d in DIRS:
                        for H in HS:
                            mk[d] = dve(lambda e: e.tensor_tensor(Mk[H, L[d], H], full_bank(d, 1)[H, :, 0:CH], bass_rep(gmask[H, d, 0], 4), ALU.mult),
                                        after=gk[d], chain=False)
                        act(lambda e: e.activation(VT[:, L[d]], full_bank(d, 2), ACTF.Copy), after=tv[d], chain=False)
                        for H in HS:
                            vc[d] = act(lambda e: e.activation(Vc[H, L[d]], full_bank(d, 2)[H, :, H], ACTF.Copy), chain=False)
                        tk[d] = turned(d, 2, Kb, vc[d])
                        sb[d] = spread(Sb, d, lambda H: S[H, L[d]], sc[d])
                    for d in DIRS:
                        dve(lambda e: e.tensor_tensor(Mrb[:, L[d]], full_bank(d, 0)[:, :, CH:], bass_rep(gmask[:, d, 1], 4), ALU.mult),
                            after=gb[d], chain=False)
                        mr[d] = dve(lambda e: e.tensor_tensor(Mrk[:, L[d]], full_bank(d, 1)[:, :, CH:], bass_rep(gmask[:, d, 1], 4), ALU.mult),
                                    chain=False)
                        bt[d] = act(lambda e: e.activation(BT[:, L[d]], full_bank(d, 3), ACTF.Copy), after=tb[d], chain=False)
                    rh, rn = [None, None], [None, None]
                    for d in DIRS:
                        rh[d] = sums(d, 3, ((lambda l: Ab[:, l, :], lambda l: S[:, l, :]), (lambda l: Mk[:, l, :], lambda l: Vc[:, l, :])),
                                     [af[d], sc[d], mk[d], bt[d]])
                        kt[d] = act(lambda e: e.activation(KT[:, L[d]], full_bank(d, 2), ACTF.Copy), after=tk[d], chain=False)
                    for d in DIRS:
                        rn[d] = dve(lambda e: e.tensor_scalar(Rn[:, L[d]], half_bank(d, 3), -1.0, None, ALU.mult), after=rh[d], chain=False)
                    x, xt, xb, xy = ([None, None] for _ in range(4))
                    for lev in range(LEVELS):
                        first, final = lev == 0, lev == LEVELS - 1
                        cur_x = (lambda l: eye[:]) if first else (lambda l: X[:, l, :])
                        cur_xt = (lambda l: eye[:]) if first else (lambda l: XT[:, l, :])
                        cur_xb = (lambda l: self.ident[:]) if first else (lambda l: XTb[:, l, :])
                        lx, tm, t2, xx = ([None, None] for _ in range(4))
                        for d in DIRS:
                            lx[d] = each(d, 0, CH, lambda l: Nb[:, l, :], cur_x, [nb[d], mr[d], x[d]])
                        for d in DIRS:
                            tm[d] = dve(lambda e: e.tensor_tensor(T[:, L[d]], half_bank(d, 0), bass_rep(lmask[:, lev, d], 4), ALU.mult),
                                        after=[lx[d], xy[d]], chain=False)
                            t2[d] = spread(Tb, d, lambda H: T[H, L[d]], [tm[d], xy[d]])
                        if not final:
                            for d in DIRS:
                                xx[d] = each(d, 1, CH, cur_xb, lambda l: T[:, l, :], [tm[d], xb[d]])
                        for d in DIRS:
                            xy[d] = each(d, 2, CH, lambda l: Tb[:, l, :], cur_xt, [t2[d], kt[d], xt[d]])
                        for d in DIRS:
                            if not final:
                                old = bass_rep(eye[:], 4) if first else X[:, L[d]]
                                x[d] = dve(lambda e: e.tensor_tensor(X[:, L[d]], old, half_bank(d, 1), ALU.subtract), after=[xx[d], x[d]], chain=False)
                            old = bass_rep(eye[:], 4) if first else XT[:, L[d]]
                            xt[d] = dve(lambda e: e.tensor_tensor(XT[:, L[d]], old, half_bank(d, 2), ALU.subtract), after=[xy[d], xt[d]], chain=False)
                            xb[d] = spread(XTb, d, lambda H: XT[H, L[d]], xt[d])
                    uu, uc, ub = ([None, None] for _ in range(3))
                    for d in DIRS:
                        uu[d] = each(d, 0, CH, lambda l: XTb[:, l, :], lambda l: Rn[:, l, :], [rn[d], xb[d]])
                    for d in DIRS:
                        uc[d] = dve(lambda e: e.tensor_copy(T[:, L[d]], half_bank(d, 0)), after=uu[d], chain=False)
                        ub[d] = spread(Tb, d, lambda H: T[H, L[d]], uc[d])
                    yy, ss = [None, None], [None, None]
                    for d in DIRS:
                        ss[d] = sums(d, 3, ((lambda l: BT[:, l, :], lambda l: T[:, l, :]), (lambda l: KT[:, l, :], lambda l: Vc[:, l, :])),
                                     [uc[d], bt[d], kt[d]])
                        yy[d] = sums(d, 1, ((lambda l: Sb[:, l, :], lambda l: AR[:, l, 1]), (lambda l: Tb[:, l, :], lambda l: Mrb[:, l, :]),
                                            (lambda l: VT[:, l, :], lambda l: Mrk[:, l, :])), [ub[d], sb[d]])
                    for d in DIRS:
                        s1 = dve(lambda e: e.tensor_tensor(S[:, L[d]], S[:, L[d]], half_bank(d, 3), ALU.add), after=ss[d], chain=False)
                    for d in DIRS:
                        yv = ycat[:, 0:4, bass.ds(where[d][0], CH)]
                        e1 = dve(lambda e: e.tensor_tensor(yv, yv, half_bank(d, 1), ALU.add), after=yy[d])
                        end[d] = [e1, yy[d]]

            p.loop(NBLK, turn)
            p.meet()

    def block1_tail(self, A, B):
        p, i = self.p, self.i
        two = lambda x: x.rearrange("p (h t) -> p h t", h=2)
        wide = lambda w, at=0: (lambda g: w[:, bass.ds(g * 256 + at, 256)])
        rhs = lambda x: (lambda k, h: x[:, k, h * HALF:(h + 1) * HALF])

        def keep(dst):
            return lambda n, bank, done: [p.act(lambda e: e.activation(two(dst[:, n, :]), bank, ACTF.Copy), after=done)]

        with ExitStack() as s:
            self.weight_slots(s)
            self.gemm(wide(i["w_out"][0]), DC, 4, 2, rhs(B), keep(A))
            p.meet()
            loaded = self.t_h.start(p.sp, B[:], self.h_dram)
            p.dve.wait(loaded)
            self.add_normed(A, "norm_mix_post", B, s)
            self.dump("d_h1", B[:])
        with ExitStack() as s:
            self.weight_slots(s, 22 * PART)
            hid = self.sb(s, "hid", [PART, DFF // PART, TOK])
            with ExitStack() as s2:
                inv = self.sb(s2, "f_inv", [PART, TOK])
                tmp = self.sb(s2, "f_tmp", [PART, 2, TOK])
                self.rms_inverse(lambda c: B[:, c, :], DC, D, inv[:], tmp)
                self.normed(lambda c: A[:, c, :], lambda c: B[:, c, :], inv[:], "norm_ffn_pre")
                p.meet()
            gate, up = i["ffn_gate"][0], i["ffn_up"][0]

            def gate_up(g, b, bank, done):
                if b == 0:
                    return [p.act(lambda e: e.activation(two(hid[:, g, :]), bank, ACTF.Silu), after=done)]
                return [p.dve(lambda e: e.tensor_tensor(two(hid[:, g, :]), two(hid[:, g, :]), bank, ALU.mult),
                              after=[done, p.act.counter.here()])]

            self.gemm(lambda g: [gate[:, bass.ds(g * PART, PART)], up[:, bass.ds(g * PART, PART)]], DC, DFF // PART, 2, rhs(A),
                      gate_up, split=True)
            p.meet()
            down = i["ffn_down"][0]
            self.gemm(lambda g: down[:, bass.ds(g * PART, PART)], DFF // PART, DC, 1, rhs(hid), keep(A))
            p.meet()
        with ExitStack() as s:
            self.weight_slots(s)
            with ExitStack() as s2:
                self.add_normed(A, "norm_ffn_post", B, s2)
            self.dump("d_h2", B[:])
            E = self.sb(s, "ple_e", [PART, DC, TOK])
            pT = self.sb(s, "pT", [PART, 2, TOK])
            prow = self.sb(s, "p_row", [PART, NBLK, 256])
            tmp = [self.sb(s, f"ple_t{n}", [PART, TOK]) for n in range(2)]
            got = self.t_misc.start(p.sp, prow[:], i["p"].rearrange("a b (n p) c -> p (a b n) c", p=PART), after=p.all_done())
            for c in range(2):
                for t in range(NBLK):
                    done = p.pe(lambda e: e.transpose(self.ps[:, 4 + 2 * c + t // 4, (t % 4) * PART:(t % 4 + 1) * PART],
                                                      prow[:, t, c * PART:(c + 1) * PART], self.ident[:]), after=[got, p.dve.counter.here()],
                                mark=(t == NBLK - 1))
                p.act(lambda e: e.activation(two(pT[:, c, :]), self.ps[:, 4 + 2 * c:6 + 2 * c, :], ACTF.Copy), after=done)
            p.meet()
            self.gemm(wide(i["ple_proj"][0]), 2, 4, 2, rhs(pT), keep(E))
            par = [0]

            def ple(n, bank, done):
                par[0] ^= 1
                t = tmp[par[0]]
                f = p.act(lambda e: e.activation(two(t[:]), bank, ACTF.Sigmoid, bias=self.col("ple_gate_b", n)),
                          after=[done, p.dve.counter.here()])
                p.dve(lambda e: e.tensor_tensor(A[:, n, :], t[:], E[:, n, :], ALU.mult), after=f)
                return [f]

            self.gemm(wide(i["ple_gate"][0]), DC, 4, 2, rhs(B), ple)
            p.meet()
        with ExitStack() as s2:
            self.add_normed(A, "norm_ple", B, s2)
        p.meet(self.t_h.start(p.sp, self.h_dram, B[:], after=p.dve.counter.here()))

    def ada(self, stack):
        p, i = self.p, self.i
        self.mod = self.sb(stack, "mod", [PART, 48, 2])
        self.gain = self.sb(stack, "gain", [PART, 3, DC])
        at = self.cols_at
        cols = lambda n: self.cols[:, at[n]:at[n] + DC]
        with ExitStack() as s:
            self.weight_slots(s, 4096)
            cc = self.sb(s, "cc", [PART, DC, 2])
            p.meet()
            p.act(lambda e: e.activation(cc[:, :, 0], cols("c_2"), ACTF.Silu))
            a = p.act(lambda e: e.activation(cc[:, :, 1], cols("c_ctx"), ACTF.Silu))
            w = i["w_ada_2"][0]
            self.gemm(lambda g: w[:, bass.ds(g * 512, 512)], DC, 12, 4, lambda k, h: cc[:, k, :],
                      lambda n, bank, done: [p.dve(lambda e: e.tensor_scalar(self.mod[:, n, :] if isinstance(n, int) else
                                                                             self.mod[:, bass.ds(n, 1), :].rearrange("p a b -> p (a b)"),
                                                                             bank[:, 0, 0:2], self.col("b_ada_2", n), None, ALU.add),
                                                   after=done)], a, tokens=2)
            for k, (g, sc, who) in enumerate((("norm1_g_2", 8, 0), ("norm1_g_2", 8, 1), ("norm2_g_2", 32, 0))):
                p.dve(lambda e: e.scalar_tensor_tensor(out=self.gain[:, k, :], in0=self.mod[:, sc:sc + DC, who], scalar=1.0, in1=cols(g),
                                                       op0=ALU.add, op1=ALU.mult))
            p.meet()

    def modulated(self, dst, x, inv, gain, shift, who):
        p = self.p
        for c in range(DC):
            p.dve(lambda e: e.scalar_tensor_tensor(out=dst(c), in0=x(c), scalar=self.gain[:, gain, c:c + 1], in1=inv, op0=ALU.mult, op1=ALU.mult))
            p.act(lambda e: e.activation(dst(c), dst(c), ACTF.Identity, bias=self.mod[:, shift + c, who:who + 1]), after=p.dve.counter.here())

    def block2_mixers(self, hxA, Y):
        p, i, nc, ps = self.p, self.i, self.nc, self.ps
        two = lambda x: x.rearrange("p (h t) -> p h t", h=2)
        rhs = lambda k, h: hxA[:, k, h * HALF:(h + 1) * HALF]
        w_in = i["w_in_2"][0]
        st = ExitStack()
        q = self.sb(st, "b_q", [PART, 4, TOK])
        qr = self.sb(st, "b_qr", [PART, 4, TOK])
        kr = self.sb(st, "b_kr", [PART, 4, TOK])
        VV = self.sb(st, "b_VV", [PART, ROWS - 1, RW])
        kc = self.sb(st, "b_kc", [PART, 4, CTX])
        vc = self.sb(st, "b_vc", [PART, 2, RW])
        with ExitStack() as s:
            self.weight_slots(s)
            hc = self.sb(s, "b_hc", [PART, DC, CTX])
            crow = self.sb(s, "b_crow", [PART, 2, D])
            inv = self.sb(s, "b_cinv", [PART, CTX])
            tmp = self.sb(s, "b_ctmp", [PART, 2, CTX])
            wv = self.sb(s, "b_wv", [PART, DC, RW])
            self.t_misc.start(p.sp, wv[:], w_in[:, 1024:1536].rearrange("(c p) n -> p c n", p=PART), after=p.all_done())
            got = self.t_misc.start(p.sp, crow[:], i["ctx_2"].rearrange("a (n p) c -> p (a n) c", p=PART))
            for c in range(DC):
                for n in range(2):
                    done = p.pe(lambda e: e.transpose(ps[:, c // 2, (c % 2) * 256 + n * PART:(c % 2) * 256 + (n + 1) * PART],
                                                      crow[:, n, c * PART:(c + 1) * PART], self.ident[:]), after=got,
                                mark=(c == DC - 1 and n == 1))
            p.act(lambda e: e.activation(hc[:].rearrange("p (b c) t -> p b (c t)", b=4), ps[:, 0:4, :], ACTF.Copy), after=done)
            self.rms_inverse(lambda c: hc[:, c, :], DC, D, inv[:], tmp, tokens=CTX)
            self.modulated(lambda c: hc[:, c, :], lambda c: hc[:, c, :], inv[:], 1, 0, 1)
            p.meet()
            self.gemm(lambda g: w_in[:, bass.ds(g * 256 + 512, 256)], DC, 2, 2, lambda k, h: hc[:, k, :],
                      lambda n, bank, done: [p.act(lambda e: e.activation(kc[:, n, :], bank[:, 0, 0:CTX], ACTF.Copy), after=done)],
                      tokens=CTX)
            p.meet()
            free = [None, None]
            for n in range(NBLK + 2):
                for k in range(DC):
                    src = hxA[:, k, n * PART:(n + 1) * PART] if n < NBLK else hc[:, k, (n - NBLK) * PART:(n - NBLK + 1) * PART]
                    done = p.pe(lambda e: e.matmul(ps[:, n % 2, :], src, wv[:, k, :], start=(k == 0), stop=(k == DC - 1)),
                                after=free[n % 2] if k == 0 else None, mark=(k == DC - 1))
                dst = VV[:, 2 * n, :] if n < NBLK else vc[:, n - NBLK, :]
                free[n % 2] = p.act(lambda e: e.activation(dst, ps[:, n % 2, :], ACTF.Copy), after=done)
            self.t_misc.start(p.sp, VV[0:64, 1:ROWS - 1:2, :], VV[64:128, 0:ROWS - 2:2, :], after=p.act.counter.here())
            p.meet(self.t_misc.start(p.sp, VV[64:128, 1:ROWS - 1:2, :], VV[0:64, 2:ROWS - 1:2, :]))
        self.dump("d_kc", kc[:])
        conv_dram = nc.dram_tensor("conv_dram", (PART, 4, TOK), F32, kind="Internal").ap()
        with ExitStack() as s:
            self.weight_slots(s)
            swap = self.sb(s, "b_swap", [PART, PART])
            cos = self.sb(s, "b_cos", [PART, TOK])
            sin = self.sb(s, "b_sin", [PART, TOK])
            t1 = self.sb(s, "b_t1", [PART, TOK])
            cp = self.sb(s, "b_cp", [PART, 4, TOK + TAPS - 1])
            sg = [self.sb(s, f"b_sg{n}", [PART, TOK]) for n in range(2)]
            for t, n in ((swap, "k_swap"), (cos, "k_rope_cos"), (sin, "k_rope_sin")):
                self.t_misc.start(p.sp, t[:], i[n], after=p.all_done())

            def qk(n, bank, done):
                dst = q[:, n, :] if self.which == 0 else kr[:, n, :]
                return [p.act(lambda e: e.activation(two(dst), bank, ACTF.Copy), after=done)]

            for self.which in range(2):
                self.gemm(lambda g: w_in[:, bass.ds(g * 256 + 512 * self.which, 256)], DC, 2, 2, rhs, qk)
            p.meet(self.t_misc.here())
            for c in range(8):
                src, dst = (q[:, c, :], qr[:, c, :]) if c < 4 else (kr[:, c - 4, :], kr[:, c - 4, :])
                base = 4 + 2 * (c % 2)
                for h in range(2):
                    done = p.pe(lambda e: e.matmul(ps[:, base + h, :], swap[:], src[:, h * HALF:(h + 1) * HALF], start=True, stop=True),
                                after=p.dve.counter.here(), mark=(h == 1))
                p.dve(lambda e: e.tensor_tensor(two(t1[:]), ps[:, base:base + 2, :], two(sin[:]), ALU.mult), after=done)
                p.dve(lambda e: e.tensor_tensor(dst, src, cos[:], ALU.mult))
                p.dve(lambda e: e.tensor_tensor(dst, dst, t1[:], ALU.add))
            pad = TAPS // 2
            p.dve(lambda e: e.memset(cp[:, :, 0:pad], 0.0))
            p.dve(lambda e: e.memset(cp[:, :, pad + TOK:], 0.0))
            p.meet()

            def glu(g, b, bank, done):
                t = sg[0]
                if b == 0:
                    return [p.act(lambda e: e.activation(two(t[:]), bank, ACTF.Sigmoid), after=[done, p.dve.counter.here()])]
                return [p.dve(lambda e: e.tensor_tensor(two(cp[:, g, pad:pad + TOK]), two(t[:]), bank, ALU.mult),
                              after=[done, p.act.counter.here()])]

            self.gemm(lambda g: [w_in[:, bass.ds(g * PART + 2048, PART)], w_in[:, bass.ds(g * PART + 1536, PART)]], DC, 4, 2, rhs, glu,
                      split=True)
            p.meet()

            def conv(n, last):
                o = Y[:, bass.ds(n + 4, 1), :].rearrange("p a t -> p (a t)")
                x = cp[:, bass.ds(n, 1), :].rearrange("p a t -> p (a t)")
                p.dve(lambda e: e.tensor_scalar(o, x[:, 0:TOK], self.col("dw", n), self.col("dw_bias_2", n), ALU.mult, ALU.add))
                for w in range(1, TAPS):
                    p.dve(lambda e: e.scalar_tensor_tensor(out=o, in0=x[:, w:w + TOK], scalar=self.col("dw", n + 4 * w), in1=o,
                                                           op0=ALU.mult, op1=ALU.add))

            p.loop(4, conv)
            p.meet()
        with ExitStack() as s:
            mean = self.sb(s, "b_mean", [PART, TOK])
            inv = self.sb(s, "b_inv", [PART, TOK])
            tmp = self.sb(s, "b_tmp", [PART, 2, TOK])
            p.dve(lambda e: e.tensor_tensor(mean[:], Y[:, 4, :], Y[:, 5, :], ALU.add))
            p.dve(lambda e: e.tensor_tensor(mean[:], mean[:], Y[:, 6, :], ALU.add))
            m = p.dve(lambda e: e.tensor_tensor(mean[:], mean[:], Y[:, 7, :], ALU.add))
            for h in range(2):
                done = p.pe(lambda e: e.matmul(ps[:, h, :], self.ones[:], mean[:, h * HALF:(h + 1) * HALF], start=True, stop=True), after=m,
                            mark=(h == 1))
            for c in range(4):
                y = Y[:, 4 + c, :]
                p.dve(lambda e: e.scalar_tensor_tensor(out=two(y), in0=ps[:, 0:2, :], scalar=-1.0 / RW, in1=two(y), op0=ALU.mult, op1=ALU.add),
                      after=done)
            self.rms_inverse(lambda c: Y[:, 4 + c, :], 4, RW, inv[:], tmp)
            for c in range(4):
                y = Y[:, 4 + c, :]
                m = p.dve(lambda e: e.tensor_tensor(y, y, inv[:], ALU.mult))
                m = p.dve(lambda e: e.tensor_scalar(y, y, self.col("conv_ln_g_2", c), self.col("conv_ln_b_2", c), ALU.mult, ALU.add))
                p.act(lambda e: e.activation(y, y, ACTF.Silu), after=m)
            p.meet()
        self.dump("d_conv", Y[:, 4:8, :])
        self.dump("d_qr", qr[:])
        self.dump("d_kr", kr[:])
        self.attention(q, qr, kr, VV, kc, vc, Y)
        st.close()

    def attention(self, q, qr, kr, VV, kc, vc, Y):
        p, i, nc, ps = self.p, self.i, self.nc, self.ps
        SC = 64 ** -0.5
        K8 = WIN_R * GRID
        pad_dram = nc.dram_tensor("rpb_dram", (HEADS, RPB_R, GRID, PART), F32, kind="Internal").ap()
        with ExitStack() as s:
            bias = self.sb(s, "a_bias", [PART, 4, RPB_R, GRID])
            cmask = self.sb(s, "a_cmask", [PART, GRID])
            eye = self.sb(s, "a_eye", [PART, CH])
            rp = self.sb(s, "a_rp", [HEADS * RPB_R, PART])
            Qb = self.sb(s, "a_Qb", [PART, 4, PART])
            Qc = self.sb(s, "a_Qc", [PART, 4, PART])
            sc = [self.sb(s, f"a_sc{n}", [PART, K8 + CTX]) for n in range(2)]
            P_ = [self.sb(s, f"a_P{n}", [PART, K8 + CTX]) for n in range(2)]
            PT = [self.sb(s, f"a_PT{n}", [PART, K8 + CTX]) for n in range(2)]
            ob = self.sb(s, "a_ob", [PART, 4, PART])
            mx = self.sb(s, "a_mx", [PART, 4])
            sm = self.sb(s, "a_sm", [PART, 4])
            z = p.dve(lambda e: e.memset(rp[:], 0.0))
            for t in (Qb, Qc, ob):
                p.dve(lambda e: e.memset(t[:], 0.0))
            self.t_misc.start(p.sp, cmask[:], i["k_col_mask"], after=z)
            self.t_misc.start(p.sp, eye[:], i["k_stack_eye"])
            a = self.t_misc.start(p.sp, rp[:, 48:48 + RPB_C], i["rpb_2"].rearrange("a h r c -> (a h r) c"))
            a = self.t_misc.start(p.sp, pad_dram.rearrange("h r q c -> (h r) q c"), bass_rep(rp[:], GRID), after=a)
            p.sp.wait(a)
            for h in range(HEADS):
                src = bass.AP(tensor=pad_dram.tensor, offset=h * RPB_R * GRID * PART + GRID - 1,
                              ap=[[PART - 1, GRID], [GRID * PART, RPB_R], [1, GRID]])
                H = (h % 2) * 64
                self.t_misc.start(p.sp, bias[H:H + 64, h // 2, :, :], src)
            p.meet(self.t_misc.here())
            for pr in range(4):
                p.dve(lambda e: e.tensor_tensor(bias[:, pr], bias[:, pr], bass_rep(cmask[:], RPB_R), ALU.add))
            p.meet()
            HS = [slice(0, 64), slice(64, 128)]

            def rows(r, rs, off):
                pe, act, dve = p.pe, p.act, p.dve
                key = rs * GRID
                T = bass.ds(r * GRID, GRID)
                before = p.all_done()
                dve.wait(before)
                act.wait(before)
                pe.wait(before)
                for H in HS:
                    qd = dve(lambda e: e.tensor_copy(Qb[H, :, H], qr[H, :, T]), chain=False)
                    qa = act(lambda e: e.activation(Qc[H, :, H], q[H, :, T], ACTF.Copy), chain=False)
                got, read, exped, turned, moved, out = ({} for _ in range(6))

                def scores(u):
                    b = 2 * (u % 2)
                    pe.wait([qd, qa, read.get(u - 2)])
                    pe(lambda e: e.matmul(ps[:, b, :], Qb[:, u, :], kr[:, u, bass.ds(key, K8)], start=True, stop=True))
                    got[u] = pe(lambda e: e.matmul(ps[:, b + 1, 0:CTX], Qc[:, u, :], kc[:, u, :], start=True, stop=True), mark=True)

                def softmax(u):
                    b, x = 2 * (u % 2), u % 2
                    c = act(lambda e: e.activation(sc[x][:, K8:], ps[:, b + 1, 0:CTX], ACTF.Copy, scale=SC), after=[got[u], exped.get(u - 2)], chain=False)
                    w = dve(lambda e: e.scalar_tensor_tensor(
                        out=sc[x][:, 0:K8].rearrange("p (r c) -> p r c", c=GRID), in0=ps[:, b, :].rearrange("p (r c) -> p r c", c=GRID), scalar=SC,
                        in1=bias[:, u, bass.ds(off, WIN_R), :], op0=ALU.mult, op1=ALU.add), after=[got[u], exped.get(u - 2)], chain=False)
                    read[u] = [c, w]
                    m = dve(lambda e: e.tensor_reduce(mx[:, u:u + 1], sc[x][:], AX.X, ALU.max, negate=True), after=[w, c], chain=False)
                    exped[u] = act(lambda e: e.activation(P_[x][:], sc[x][:], ACTF.Exp, bias=mx[:, u:u + 1], accum_out=sm[:, u:u + 1]),
                                   after=[m, turned.get(u - 2)], chain=False)

                def turn_probs(u):
                    x = u % 2
                    pe.wait([exped[u], moved.get(u - 1)])
                    for j in range(6):
                        turned[u] = pe(lambda e: e.transpose(ps[:, 4 + j // 4, (j % 4) * PART:(j % 4 + 1) * PART], P_[x][:, j * PART:(j + 1) * PART],
                                                             self.ident[:]), mark=(j == 5))
                    a = act(lambda e: e.activation(PT[x][:, 0:512], ps[:, 4, :], ACTF.Copy), after=[turned[u], out.get(u - 2)], chain=False)
                    d = dve(lambda e: e.tensor_copy(PT[x][:, 512:], ps[:, 5, 0:256]), after=[turned[u], out.get(u - 2)], chain=False)
                    moved[u] = [a, d]

                def values(u):
                    x = u % 2
                    pe.wait(moved[u])
                    for j in range(6):
                        v = VV[:, bass.ds(rs + 2 * j, 1), u * PART:(u + 1) * PART].rearrange("p a b -> p (a b)") if j < 4 \
                            else vc[:, j - 4, u * PART:(u + 1) * PART]
                        out[u] = pe(lambda e: e.matmul(ps[:, 6, u * PART:(u + 1) * PART], PT[x][:, j * PART:(j + 1) * PART], v,
                                                       start=(j == 0), stop=(j == 5)), mark=(j == 5))

                scores(0)
                scores(1)
                for u in range(4):
                    softmax(u)
                    if u + 2 < 4:
                        scores(u + 2)
                    turn_probs(u)
                    if u:
                        values(u - 1)
                values(3)
                n = dve(lambda e: e.reciprocal(sm[:], sm[:]), after=exped[3], chain=False)
                o6 = ps[:, 6, :].rearrange("p (u c) -> p u c", u=4)
                for H in HS:
                    n2 = dve(lambda e: e.tensor_tensor(ob[H, :, H], o6[H, :, H], sm[H].unsqueeze(2).to_broadcast([64, 4, 64]), ALU.mult),
                             after=[n, out[3]], chain=False)
                pe.wait(n2)
                for u in range(4):
                    f = pe(lambda e: e.matmul(ps[:, 7, u * GRID:(u + 1) * GRID], ob[:, u, :], eye[:], start=True, stop=True), mark=(u == 3))
                act(lambda e: e.activation(Y[:, 0:4, T], ps[:, 7, 0:4 * GRID].rearrange("p (u c) -> p u c", u=4), ACTF.Copy), after=f, chain=False)

            lo, hi = WIN_R // 2, ROWS - WIN_R // 2
            p.loop(lo, lambda t, last: rows(t, 0, t * -1 + WIN_R - 1))
            p.loop(hi - lo, lambda t, last: rows(t + lo, t, WIN_R - 1 - lo))
            p.loop(ROWS - hi, lambda t, last: rows(t + hi, ROWS - WIN_R, t * -1 + WIN_R - 1 - lo))
            p.meet()
        self.dump("d_attn", Y[:, 0:4, :])

    def block2(self):
        p, i, ps = self.p, self.i, self.ps
        two = lambda x: x.rearrange("p (h t) -> p h t", h=2)
        st = ExitStack()
        self.ada(st)
        A = self.sb(st, "A2", [PART, DC, TOK])
        with ExitStack() as s:
            Y = self.sb(s, "Y2", [PART, DC, TOK])
            with ExitStack() as s2:
                inv = self.sb(s2, "b2_inv", [PART, TOK])
                tmp = self.sb(s2, "b2_tmp", [PART, 2, TOK])
                h = Y
                p.dve.wait(self.t_h.start(p.sp, h[:], self.h_dram, after=p.all_done()))
                p.act.wait(self.t_h.here())
                self.rms_inverse(lambda c: h[:, c, :], DC, D, inv[:], tmp)
                self.modulated(lambda c: A[:, c, :], lambda c: h[:, c, :], inv[:], 0, 0, 0)
                p.meet()
            self.dump("d_hx", A[:])
            self.block2_mixers(A, Y)
            self.weight_slots(s)
            h = A
            loaded = self.t_h.start(p.sp, h[:], self.h_dram, after=p.all_done())
            p.dve.wait(loaded)
            w = i["w_out_2"][0]

            def mix_out(n, bank, done):
                g1 = self.mod[:, 16 + n, 0:1] if isinstance(n, int) else self.mod[:, bass.ds(n + 16, 1), 0]
                return [p.dve(lambda e: e.scalar_tensor_tensor(out=two(h[:, n, :]), in0=bank, scalar=g1, in1=two(h[:, n, :]),
                                                               op0=ALU.mult, op1=ALU.add), after=done)]

            self.gemm(lambda g: w[:, bass.ds(g * 256, 256)], DC, 4, 2, lambda k, hh: Y[:, k, hh * HALF:(hh + 1) * HALF], mix_out)
            p.meet(self.t_h.start(p.sp, self.h_dram, h[:], after=p.dve.counter.here()))
        self.dump("d_h4", A[:])
        with ExitStack() as s:
            hid = self.sb(s, "hid2", [PART, DFF2 // PART, TOK])
            with ExitStack() as s2:
                inv = self.sb(s2, "m_inv", [PART, TOK])
                tmp = self.sb(s2, "m_tmp", [PART, 2, TOK])
                self.rms_inverse(lambda c: A[:, c, :], DC, D, inv[:], tmp)
                self.modulated(lambda c: A[:, c, :], lambda c: A[:, c, :], inv[:], 2, 24, 0)
                p.meet()
            with ExitStack() as s2:
                self.weight_slots(s2, 4096)
                w1, w2 = i["w_mlp1_2"][0], i["w_mlp2_2"][0]

                def relu2(n, bank, done):
                    f = p.act(lambda e: e.activation(two(hid[:, n, :]), bank, ACTF.Relu), after=done)
                    p.dve(lambda e: e.tensor_tensor(hid[:, n, :], hid[:, n, :], hid[:, n, :], ALU.mult), after=f)
                    return [f]

                self.gemm(lambda g: w1[:, bass.ds(g * 256, 256)], DC, 16, 2, lambda k, hh: A[:, k, hh * HALF:(hh + 1) * HALF], relu2)
                p.meet()

                def gated(n, bank, done):
                    g2 = self.mod[:, 40 + n, 0:1] if isinstance(n, int) else self.mod[:, bass.ds(n + 40, 1), 0]
                    return [p.dve(lambda e: e.tensor_scalar(two(A[:, n, :]), bank, g2, None, ALU.mult), after=done)]

                self.gemm(lambda g: w2[:, bass.ds(g * PART, PART)], DFF2 // PART, DC, 1, lambda k, hh: hid[:, k, hh * HALF:(hh + 1) * HALF],
                          gated)
                p.meet()
        with ExitStack() as s:
            h = self.sb(s, "h_last", [PART, DC, TOK])
            inv = self.sb(s, "l_inv", [PART, TOK])
            tmp = self.sb(s, "l_tmp", [PART, 2, TOK])
            row = [self.sb(s, f"o_row{n}", [PART, D]) for n in range(2)]
            loaded = self.t_h.start(p.sp, h[:], self.h_dram, after=p.all_done())
            p.dve.wait(loaded)
            for c in range(DC):
                p.dve(lambda e: e.tensor_tensor(h[:, c, :], h[:, c, :], A[:, c, :], ALU.add))
            self.rms_inverse(lambda c: h[:, c, :], DC, D, inv[:], tmp)
            self.normed(lambda c: h[:, c, :], lambda c: h[:, c, :], inv[:], "final_g")
            out = self.out.rearrange("b (n p) c -> n p (b c)", p=PART)
            p.meet()
            t_out = [Transfer(p, "t_out0"), Transfer(p, "t_out1")]
            copied = [None, None]
            for t in range(NBLK):
                x = t % 2
                for c in range(DC):
                    done = p.pe(lambda e: e.transpose(ps[:, 2 * x + c // 4, (c % 4) * PART:(c % 4 + 1) * PART], h[:, c, t * PART:(t + 1) * PART],
                                                      self.ident[:]), after=copied[x] if c == 0 else None, mark=(c == DC - 1))
                copied[x] = p.act(lambda e: e.activation(two(row[x][:]), ps[:, 2 * x:2 * x + 2, :], ACTF.Copy), after=[done, t_out[x].here()])
                t_out[x].start(p.sp, out[t], row[x][:], after=copied[x])
            p.meet(t_out[0].here(), t_out[1].here())
        st.close()

    def block1(self):
        with ExitStack() as s:
            B = self.sb(s, "B1", [PART, DC, TOK])
            A = self.sb(s, "A1", [PART, DC, TOK])
            with ExitStack() as s2:
                self.load_x(A, s2)
            self.gla(A, B)
            self.rwkv(A, B)
            self.block1_tail(A, B)


def bass_rep(ap, n):
    return ap.unsqueeze(1).to_broadcast([ap.shape[0], n] + list(ap.shape[1:]))


def rep_mid(ap, n):
    return ap.unsqueeze(2).to_broadcast([ap.shape[0], ap.shape[1], n, ap.shape[2]])


def rep_last(ap, n):
    return ap.to_broadcast([ap.shape[0], ap.shape[1], n])


def kernel(**inputs):
    import concourse.bacc as bacc
    from concourse.bass_utils import run_bass_kernel_spmd

    nc = bacc.Bacc("TRN2", target_bir_lowering=False, num_devices=1)
    given = {name: np.ascontiguousarray(a) for name, a in inputs.items()}
    given.update({f"k_{name}": a for name, a in constants().items()})
    ins, arrays = {}, {}
    for name, a in given.items():
        arrays[f"in_{name}_dram"] = a
        ins[name] = nc.dram_tensor(f"in_{name}_dram", a.shape, F32, kind="ExternalInput").ap()
    out = nc.dram_tensor("out_dram", (1, TOK, D), F32, kind="ExternalOutput").ap()
    k = Kernel(nc, ins, out)
    with ExitStack() as stack:
        k.setup(stack)
        k.block1()
        k.block2()
    r = run_bass_kernel_spmd(nc, [arrays], core_ids=[0])
    return r.results[0]["out_dram"]
```

```python
import math
from contextlib import ExitStack

import numpy as np

import concourse.bass as bass
from concourse import mybir

F32 = mybir.dt.float32
F32R = mybir.dt.float32r
ALU = mybir.AluOpType
ACTF = mybir.ActivationFunctionType
AX = mybir.AxisListType

PART = 128
TOK = 1024
HALF = 512
D = 1024
DC = D // PART
CH = 64
NBLK = TOK // PART
RW = 512
RPAIR = 4
LANES = 2 * RPAIR
LEVELS = 6
GPAIR = 2
GLEV = LEVELS + 1
GSLOT = GLEV + 2
DFF = 2816
DFF2 = 4096
CTX = 256
HEADS = 8
GRID = 64
ROWS = TOK // GRID
WIN_R, WIN_C = 8, 16
RPB_R, RPB_C = 2 * WIN_R - 1, 2 * WIN_C - 1
TAPS = 31
HEAD_START = 24
NEG = -1.0e30
DECAY = -math.exp(-0.5)


def constants():
    c = {}
    f = np.float32
    c["ident"] = np.eye(PART, dtype=f)
    t = np.arange(PART)
    same = (t[:, None] // CH) == (t[None, :] // CH)
    tri = np.zeros((2, PART, 2, PART), f)
    s, q = t[:, None], t[None, :]
    for d, (inc, exc) in enumerate((((s <= q), (s < q)), ((s >= q), (s > q)))):
        tri[d, :, 0] = DECAY * np.where(same, inc.astype(f) - 0.5, 0)
        tri[d, :, 1] = DECAY * np.where(same, exc.astype(f) - 0.5, 0)
    c["tri"] = np.ascontiguousarray(tri.transpose(1, 0, 2, 3)).reshape(PART, -1)
    g = np.zeros((2, PART, GSLOT, PART), f)
    for d in range(2):
        pos = (t % CH) if d == 0 else (CH - 1 - t % CH)
        ps, pq = pos[:, None], pos[None, :]
        for lev in range(1, GLEV):
            w = 2 ** (lev - 1)
            mid = (pq // (2 * w)) * 2 * w + w
            m = np.where(pq >= mid, (ps >= mid) & (ps <= pq), (ps > pq) & (ps < mid))
            g[d, :, lev] = m & same
        g[d, :, GLEV] = (ps <= pq) & same
        g[d, :, GLEV + 1] = (ps > pq) & same
    g /= 16.0
    c["gsum"] = np.ascontiguousarray(g.transpose(1, 0, 2, 3)).reshape(PART, -1)
    tt = np.arange(CH)
    m = np.zeros((CH, 2, 2, CH), f)
    m[:, 0, 0] = tt[:, None] < tt[None, :]
    m[:, 0, 1] = tt[:, None] <= tt[None, :]
    m[:, 1, 0] = tt[:, None] > tt[None, :]
    m[:, 1, 1] = tt[:, None] >= tt[None, :]
    c["gram_mask"] = np.tile(m.reshape(CH, -1), (2, 1))
    lm = np.zeros((CH, LEVELS, 2, CH), f)
    gm = np.zeros((CH, 2, GLEV, CH), f)
    for d in range(2):
        pos = tt if d == 0 else CH - 1 - tt
        gm[:, d, 0] = np.eye(CH)
        for lev in range(LEVELS):
            w = 2 ** lev
            blk = pos // (2 * w)
            late = (pos % (2 * w)) >= w
            lm[:, lev, d] = (blk[:, None] == blk[None, :]) & late[:, None] & ~late[None, :]
            gm[:, d, lev + 1] = (blk[:, None] == blk[None, :]) & ~late[:, None] & late[None, :]
    c["lev_mask"] = np.tile(lm.reshape(CH, -1), (2, 1))
    c["gla_mask"] = np.tile(gm.reshape(CH, -1), (2, 1))
    c["stack_eye"] = np.tile(np.eye(CH, dtype=f), (2, 1))
    hb = (t[:, None] // CH) == (t[None, :] // CH)
    c["head_ones"] = hb.astype(f)
    c["head_sel"] = np.stack([t < CH, t >= CH], 1).astype(f)
    n = 16
    inv = (np.float32(10000.0) ** (-np.arange(n, dtype=f) / n)).astype(f)
    tok = np.arange(TOK)
    ch = np.arange(64)
    p = np.where((ch < 32)[:, None], (tok // GRID)[None, :], (tok % GRID)[None, :]).astype(f)
    ang = (p * inv[ch % n][:, None]).astype(f)
    sign = np.where((ch % 32) < 16, -1.0, 1.0).astype(f)[:, None]
    c["rope_cos"] = np.tile(np.cos(ang), (2, 1)).astype(f)
    c["rope_sin"] = np.tile(np.sin(ang) * sign, (2, 1)).astype(f)
    c["swap"] = (s == (q ^ 16)).astype(f)
    cs = np.clip(np.arange(GRID) - WIN_C // 2, 0, GRID - WIN_C)
    inside = (np.arange(GRID)[None, :] >= cs[:, None]) & (np.arange(GRID)[None, :] < cs[:, None] + WIN_C)
    c["col_mask"] = np.tile(np.where(inside, 0.0, NEG).astype(f), (2, 1))
    return c


class Done:

    def __init__(self, counter, count, per, turn):
        self.counter, self.count, self.per, self.turn = counter, count, per, turn

    def before(self):
        assert self.count >= self.per
        return Done(self.counter, self.count - self.per, self.per, self.turn)


class Counter:
    def __init__(self, prog, name, step):
        self.sem, self.step = prog.nc.alloc_semaphore(name), step
        self.prog, self.count, self.per = prog, 0, 0
        prog.counters.append(self)

    def here(self):
        return Done(self, self.count, self.per, self.prog.turn)


class Queue:

    def __init__(self, prog, name, eng, chained):
        self.prog, self.eng, self.chained = prog, eng, chained
        self.counter = Counter(prog, name, 1)
        self.seen = {}

    def wait(self, done):
        if self.prog.dry or done is None:
            return
        if isinstance(done, (list, tuple)):
            for d in done:
                self.wait(d)
            return
        key = (done.counter, done.per)
        if done.count <= self.seen.get(key, 0) or (done.count == 0 and not done.per):
            return
        self.seen[key] = done.count
        step = done.counter.step
        value = done.count * step
        if done.per:
            assert done.count > 0
            value = done.turn * (done.per * step) + value
        self.eng.wait_ge(done.counter.sem, value)

    def __call__(self, make, after=None, mark=None, chain=None):
        self.wait(after)
        if self.chained if chain is None else chain:
            self.wait(self.counter.here())
        if self.chained if mark is None else mark:
            self.counter.count += 1
            if not self.prog.dry:
                make(self.eng).then_inc(self.counter.sem, 1)
        elif not self.prog.dry:
            make(self.eng)
        return self.counter.here()


class Transfer:

    def __init__(self, prog, name):
        self.prog, self.counter = prog, Counter(prog, name, 16)

    def start(self, queue, out, in_, after=None):
        queue.wait(after)
        self.counter.count += 1
        if not self.prog.dry:
            queue.eng.dma_start(out, in_).then_inc(self.counter.sem, 16)
        return self.counter.here()

    def here(self):
        return self.counter.here()


class Prog:
    def __init__(self, nc):
        self.nc, self.counters, self.dry, self.turn = nc, [], False, None
        self.pe = Queue(self, "pe", nc.tensor, False)
        self.act = Queue(self, "act", nc.scalar, True)
        self.dve = Queue(self, "dve", nc.vector, True)
        self.pool = Queue(self, "pool", nc.gpsimd, True)
        self.sp = Queue(self, "sp", nc.sync, False)
        self.engines = (self.pe, self.act, self.dve, self.pool)

    def loop(self, turns, body):
        if turns <= 0:
            return
        start = [c.count for c in self.counters]
        self.dry = True
        left = body(0, None)
        self.dry = False
        for c, s in zip(self.counters, start):
            c.per, c.count = c.count - s, s
        seen = [dict(q.seen) for q in (*self.engines, self.sp)]
        with self.nc.Fori(0, turns) as turn:
            self.turn = turn
            last = None
            if left is not None:
                last = {k: [Done(d.counter, d.count, d.counter.per, turn).before() for d in v]
                        for k, v in left.items()}
            body(turn, last)
        self.turn = None
        for c, s in zip(self.counters, start):
            assert c.count == s + c.per
            c.count, c.per = s + c.per * turns, 0
        for q, s in zip((*self.engines, self.sp), seen):
            q.seen = s

    def all_done(self):
        return [q.counter.here() for q in self.engines]

    def meet(self, *more):
        done = [*self.all_done(), *more]
        for q in (*self.engines, self.sp):
            q.wait(done)


class Columns:

    def __init__(self):
        self.rows, self.at = [], {}
        self.n = 0

    def add(self, name, ap2d):
        self.at[name] = self.n
        r = 0
        n = ap2d.shape[0]
        while r < n:
            k = min(n - r, PART - self.n % PART)
            self.rows.append((self.n, k, ap2d[r:r + k, :]))
            self.n += k
            r += k


def blocks(ap):
    return ap.rearrange("(n p) -> n p", p=PART)


class Kernel:
    def __init__(self, nc, ins, out, only=None, dumps=None):
        self.nc, self.i, self.out = nc, ins, out
        self.p = Prog(nc)
        self.only, self.dumps, self.made = only, dumps or {}, 0
        self.ps = nc.alloc_psum_tensor("ps", [PART, 8, HALF], F32)
        self.t_misc = Transfer(self.p, "t_misc")
        self.t_w = [Transfer(self.p, "t_w0"), Transfer(self.p, "t_w1")]
        self.t_d = [Transfer(self.p, "t_d0"), Transfer(self.p, "t_d1")]
        self.t_h = Transfer(self.p, "t_h")
        self.t_st = Transfer(self.p, "t_st")
        self.t_in = Transfer(self.p, "t_in")
        self.h_dram = ins.get("h_dram")
        if self.h_dram is None:
            self.h_dram = nc.dram_tensor("h_dram", (PART, DC, TOK), F32, kind="Internal").ap()

    def sb(self, stack, name, shape, dt=F32):
        self.made = self.made + 1
        return stack.enter_context(self.nc.sbuf_tensor(f"{name}_{self.made}", shape, dt))

    def dump(self, name, ap):
        if name in self.dumps:
            self.p.meet()
            self.t_misc.start(self.p.sp, self.dumps[name], ap)
            self.p.meet(self.t_misc.here())

    def col(self, name, k=0, rows=PART):
        at = self.cols_at[name]
        if isinstance(k, int):
            return self.cols[0:rows, at + k:at + k + 1]
        return self.cols[0:rows, bass.ds(k + at, 1)]

    def setup(self, stack):
        p, i = self.p, self.i
        c = Columns()
        for n in ("norm_mix_pre", "norm_mix_post", "norm_ffn_pre", "norm_ffn_post", "norm_ple", "ple_gate_b",
                  "rwkv_a0", "rwkv_k_k", "rwkv_k_a", "rwkv_ln_w", "rwkv_ln_b", "norm1_g_2", "norm2_g_2",
                  "b_ada_2", "dw_bias_2", "conv_ln_g_2", "conv_ln_b_2"):
            c.add(n, i[n].rearrange("a (n p) -> (a n) p", p=PART))
        c.add("rwkv_r_k", i["rwkv_r_k"].rearrange("a (n two) p -> (a n) (two p)", two=2))
        mu = i["rwkv_mu"]
        c.add("mu", mu[:, 0:3 * RW + PART].rearrange("a (n p) -> (a n) p", p=PART))
        c.add("mu_g", mu[:, 1728:1856])
        c.add("mu_a", mu[:, 1664:1728])
        c.add("gla_norm", i["gla_norm"])
        c.add("conv", i["gla_conv"].rearrange("a w b (n p) -> (a w b n) p", p=PART))
        c.add("dw", i["dw_kernel_2"].rearrange("a w (n p) -> (a w n) p", p=PART))
        c.add("final_g", blocks(i["final_g_2"]))
        c.add("c_2", i["c_2"].rearrange("a (n p) -> (a n) p", p=PART))
        c.add("c_ctx", blocks(i["c_ctx_2"]))
        self.cols_at = c.at
        nt = -(-c.n // PART)
        self.cols = self.sb(stack, "cols", [PART, nt * PART])
        self.ident = self.sb(stack, "ident", [PART, PART])
        self.ones = self.sb(stack, "ones", [PART, PART])
        self.st = self.sb(stack, "small", [PART, 3, 64])
        self.t_misc.start(p.sp, self.ident[:], i["k_ident"])
        p.dve(lambda e: e.memset(self.ones[:], 1.0))
        with ExitStack() as tmp:
            rows = self.sb(tmp, "rows", [PART, nt, PART])
            zeroed = p.dve(lambda e: e.memset(rows[:], 0.0))
            for at, k, src in c.rows:
                w = src.shape[1]
                self.t_misc.start(p.sp, rows[at % PART:at % PART + k, at // PART, 0:w], src, after=zeroed)
            for t in range(nt):
                done = p.pe(lambda e: e.transpose(self.ps[:, 0, t * PART:(t + 1) * PART], rows[:, t, :],
                                                  self.ident[:]), after=self.t_misc.here(), mark=True)
            p.dve(lambda e: e.tensor_copy(self.cols[:], self.ps[:, 0, 0:nt * PART]), after=done)
            p.meet()

    def weight_slots(self, stack, cols=2048):
        self.w = [self.sb(stack, f"w{s}", [PART, cols]) for s in range(2)]

    def gemm(self, weights, kc, groups, nb, rhs, evac, after=None, tokens=TOK, m=PART, split=False, start=None):
        p = self.p
        nh = -(-tokens // HALF)
        tw = min(tokens, HALF)
        slot = [w[:, 0:kc * nb * m].rearrange("p (c n) -> p c n", c=kc) for w in self.w]
        start = p.all_done() if start is None else start
        free = {0: start, 1: start}

        def load(g, s, freed):
            parts = weights(g) if split else [weights(g)]
            for b, w in enumerate(parts):
                wide = w.shape[1]
                self.t_w[s].start(p.sp, slot[s][:, :, b * wide:(b + 1) * wide], w.rearrange("(c p) n -> p c n", p=PART),
                                  after=freed)

        def compute(g, s):
            loaded = self.t_w[s].here()
            for b in range(nb):
                pair = (s * nb + b) % 2
                bank = self.ps[:, 2 * pair:2 * pair + 2, :]
                p.pe.wait(loaded)
                p.pe.wait(free[pair])
                for h in range(nh):
                    for k in range(kc):
                        done = p.pe(lambda e: e.matmul(bank[0:m, h, 0:tw], slot[s][:, k, b * m:(b + 1) * m],
                                                       rhs(k, h), start=(k == 0), stop=(k == kc - 1)),
                                    mark=(h == nh - 1 and k == kc - 1))
                free[pair] = evac(g, b, bank, done) if split else evac(g * nb + b, bank, done)
            return done

        p.pe.wait(after)
        load(0, 0, start)
        if groups > 1:
            load(1, 1, start)
        turns = groups // 2 - 1
        if turns < 2:
            turns = 0

        def turn(t, last):
            if last is not None:
                free[0], free[1] = last["f0"], last["f1"]
            for s in range(2):
                used = compute(t * 2 + s, s)
                load(t * 2 + s + 2, s, used)
            return {"f0": free[0], "f1": free[1]}

        if turns:
            p.pe.wait([free[0], free[1]])
            left = {}
            p.loop(turns, lambda t, last: left.update(turn(t, last)) or left)
            free[0] = free[1] = [d.counter.here() for k in left.values() for d in flat_list(k)]
        for g in range(2 * turns, groups):
            used = compute(g, g % 2)
            if g + 2 < groups:
                load(g + 2, g % 2, used)
        return p.all_done()

    def in_two_parts(self, high, low, x, after=None):
        p = self.p
        rounded = p.act(lambda e: e.activation(high, x, ACTF.Copy), after=after)
        return [rounded, p.dve(lambda e: e.tensor_tensor(low, x, high.bitcast(F32), ALU.subtract), after=rounded)]

    def fused_mlp(self, stack, nblk, ups, down, make_x, x, activate, add):
        p = self.p
        nb = len(ups(0))
        wide = nb * D
        tiles = lambda name, cols, dt: [self.sb(stack, f"{name}{k}", [PART, cols], dt) for k in range(2)]
        uw, uh, ul = tiles("up", wide, F32), tiles("up_h", wide, F32R), tiles("up_l", wide, F32R)
        dw, dh, dl = tiles("dn", D, F32), tiles("dn_h", D, F32R), tiles("dn_l", D, F32R)
        hh, hl = tiles("hid_h", TOK, F32R), tiles("hid_l", TOK, F32R)
        start = p.all_done()
        now = {f"{k}{n}": list(start) for k in "uUdDh" for n in range(2)}
        now.update({f"b{n}": list(start) for n in range(4)})
        now["a"] = list(start)

        def load_up(g, s):
            for b, w in enumerate(ups(g)):
                self.t_w[s].start(p.sp, uw[s][:, b * D:(b + 1) * D].rearrange("p (c n) -> p c n", c=DC),
                                  w.rearrange("(c p) n -> p c n", p=PART), after=now[f"u{s}"][-1])

        def load_down(g, s):
            self.t_d[s].start(p.sp, dw[s][:], down(g), after=now[f"d{s}"][-1])

        def part_up(s):
            now[f"u{s}"] = self.in_two_parts(uh[s][:], ul[s][:], uw[s][:], [self.t_w[s].here(), *now[f"U{s}"]])

        def part_down(s):
            now[f"d{s}"] = self.in_two_parts(dh[s][:], dl[s][:], dw[s][:], [self.t_d[s].here(), *now[f"D{s}"]])

        def product(bank, terms, after, out):
            p.pe.wait(after)
            for h in range(2):
                pairs = [(w, v) for (wh, wl), (vh, vl) in terms(h) for w, v in ((wh, vh), (wh, vl), (wl, vh))]
                for k, (w, v) in enumerate(pairs):
                    done = p.pe(lambda e: e.matmul(bank[:, h, :], w, v, start=(k == 0), stop=(k == len(pairs) - 1)),
                                mark=(h == 1 and k == len(pairs) - 1))
                    if k < len(pairs) - 1 or h == 0:
                        yield
            out.append(done)

        def up(s):
            for b in range(nb):
                pair = b if nb == 2 else s
                bank = self.ps[:, 2 * pair:2 * pair + 2, :]
                col = lambda w, k: w[s][:, b * D + k * PART:b * D + (k + 1) * PART]
                out = []
                yield from product(bank, lambda h: [((col(uh, k), col(ul, k)), tuple(v[:, k, h * HALF:(h + 1) * HALF] for v in x))
                                                    for k in range(DC)], [*now[f"u{s}"], *now[f"b{pair}"]], out)
                tile, ready, read = activate(b, bank, out[0], now["a"])
                now[f"b{pair}"] = [read]
                if b == nb - 1:
                    now[f"U{s}"] = out
                    now[f"h{s}"] = now["a"] = self.in_two_parts(hh[s][:], hl[s][:], tile, [ready, *now[f"D{s}"]])
                yield

        def add_down(s):
            for n in range(DC):
                pair = 2 + n % 2
                bank = self.ps[:, 2 * pair:2 * pair + 2, :]
                col = lambda w: w[s][:, n * PART:(n + 1) * PART]
                half = lambda v, h: v[s][:, h * HALF:(h + 1) * HALF]
                out = []
                yield from product(bank, lambda h: [((col(dh), col(dl)), (half(hh, h), half(hl, h)))],
                                   [*now[f"d{s}"], *now[f"h{s}"], *now[f"b{pair}"]], out)
                now[f"b{pair}"] = [add(n, bank, out[0])]
                now[f"D{s}"] = out
                yield

        def run(matmuls, n):
            for _ in range(n):
                next(matmuls)

        def step(g, s, more_up=True, more_load=True, more_down=True):
            ups_left, downs = up(s), add_down(1 - s)
            run(ups_left, HEAD_START)
            for n in range(DC):
                run(downs, 6)
                run(ups_left, (nb * DC * 6 - HEAD_START) // DC)
                if n == 1:
                    if more_up:
                        part_up(1 - s)
                    if more_load:
                        load_up(g + 3, 1 - s)
                if n == 3:
                    part_down(s)
                    if more_down:
                        load_down(g + 2, s)

        for g in range(2):
            load_up(g, g)
            load_down(g, g)
        make_x()
        part_up(0)
        load_up(2, 0)
        part_up(1)
        load_up(3, 1)
        part_down(0)
        load_down(2, 0)
        run(up(0), nb * DC * 6)
        turns = (nblk - 4) // 2
        before = [d for v in now.values() for d in v]
        for q in (p.pe, p.act, p.dve, p.sp):
            q.wait(before)

        def turn(t, last):
            if last is not None:
                now.update(last)
            for k in (1, 2):
                step(t * 2 + k, k % 2)
            return dict(now)

        held = dict(now)
        p.loop(turns, turn)
        for k in now:
            now[k] = [d.counter.here() for d in held[k]] if not turns else [d.counter.here() for d in now[k]]
        for g in range(2 * turns + 1, nblk):
            step(g, g % 2, g + 1 < nblk, g + 3 < nblk, g + 2 < nblk)
        run(add_down((nblk - 1) % 2), DC * 6)

    def token_sums(self, src, sel, col, after, tokens=TOK):
        p = self.p
        nb = tokens // PART
        p.pe.wait(after)
        for t in range(nb):
            done = p.pe(lambda e: e.matmul(self.ps[:, 4, col + 2 * t:col + 2 * t + 2], src[:, t * PART:(t + 1) * PART], sel,
                                           start=True, stop=True), mark=(t == nb - 1))
        return done

    def rsqrt_small(self, n, after, op0, c0, op1=None, c1=None):
        p = self.p
        v, y, t = (self.st[:, k, 0:n] for k in range(3))
        m = p.dve(lambda e: e.tensor_scalar(v, self.ps[:, 4, 0:n], c0, c1, op0, op1) if op1 is not None else
                  e.tensor_scalar(v, self.ps[:, 4, 0:n], c0, None, op0), after=after)
        done = p.act(lambda e: e.activation(y, v, ACTF.Sqrt), after=m)
        p.dve(lambda e: e.reciprocal(y, y), after=done)
        p.dve(lambda e: e.tensor_tensor(t, y, y, ALU.mult))
        p.dve(lambda e: e.tensor_tensor(t, t, v, ALU.mult))
        p.dve(lambda e: e.tensor_scalar(t, t, -0.5, 1.5, ALU.mult, ALU.add))
        return p.dve(lambda e: e.tensor_tensor(y, y, t, ALU.mult))

    def over_channels(self, cols, tmp, after, bank=6):
        p = self.p
        nb, heads = cols.shape[1], cols.shape[2]
        w = PART // heads
        wide = tmp[:, 0:nb * PART].rearrange("p (b h w) -> p b h w", b=nb, h=heads)
        src = cols.unsqueeze(3).to_broadcast([PART, nb, heads, w])
        m = p.dve(lambda e: e.tensor_copy(wide, src), after=[after, p.pe.counter.here()])
        p.pe.wait(m)
        for t in range(nb):
            done = p.pe(lambda e: e.transpose(self.ps[:, bank + t // 4, (t % 4) * PART:(t % 4 + 1) * PART], tmp[:, t * PART:(t + 1) * PART],
                                              self.ident[:]), mark=(t == nb - 1))
        return done

    def rms_inverse(self, x, nblk, width, inv, tmp, tokens=TOK, eps=1e-6):
        p = self.p
        nb = tokens // PART
        start = p.all_done()
        added = [start, start]
        for c in range(nblk):
            dst = inv if c == 0 else tmp[:, c % 2, :]
            sq = p.act(lambda e: e.activation(dst, x(c), ACTF.Square), after=added[c % 2], chain=False)
            if c:
                added[c % 2] = p.dve(lambda e: e.tensor_tensor(inv, inv, tmp[:, c % 2, :], ALU.add), after=[sq, start])
        sums = self.token_sums(inv, self.ones[:, 0:2], 0, [sq, added, start], tokens)
        m = self.rsqrt_small(2 * nb, sums, ALU.mult, 1.0 / width, ALU.add, eps)
        y = self.st[:, 1, 0:2 * nb].rearrange("p (b two) -> p b two", two=2)[:, :, 0:1]
        done = self.over_channels(y, tmp[:, 0, :] if nb * PART <= tokens else None, m)
        nh = -(-tokens // HALF)
        tw = min(tokens, HALF)
        done = p.act(lambda e: e.activation(inv.rearrange("p (h t) -> p h t", h=nh), self.ps[:, 6:6 + nh, 0:tw], ACTF.Copy), after=done)
        p.dve.wait(done)
        return done

    def normed(self, dst, x, inv, name, nblk=DC):
        p = self.p
        for c in range(nblk):
            p.dve(lambda e: e.scalar_tensor_tensor(out=dst(c), in0=x(c), scalar=self.col(name, c), in1=inv,
                                                   op0=ALU.mult, op1=ALU.mult))

    def add_normed(self, y, name, h, stack):
        p = self.p
        inv = self.sb(stack, "an_inv", [PART, TOK])
        tmp = self.sb(stack, "an_tmp", [PART, 2, TOK])
        self.rms_inverse(lambda c: y[:, c, :], DC, D, inv[:], tmp)
        self.normed(lambda c: y[:, c, :], lambda c: y[:, c, :], inv[:], name)
        p.dve.wait(self.t_h.here())
        for c in range(DC):
            p.dve(lambda e: e.tensor_tensor(h[:, c, :], h[:, c, :], y[:, c, :], ALU.add))
        p.meet()

    def load_x(self, xn, stack):
        p = self.p
        x = self.i["x"].rearrange("b (n p) c -> n p (b c)", p=PART)
        row = self.sb(stack, "x_row", [PART, D])
        p.meet()

        def turn(t, last):
            got = self.t_in.start(p.sp, row[:], x[t], after=p.pe.counter.here())
            p.pe.wait([got, p.dve.counter.here()])
            for c in range(DC):
                done = p.pe(lambda e: e.transpose(self.ps[:, c // 4, (c % 4) * PART:(c % 4 + 1) * PART],
                                                  row[:, c * PART:(c + 1) * PART], self.ident[:]), mark=(c == DC - 1))
            p.dve(lambda e: e.tensor_copy(
                xn[:, :, bass.ts(t, PART)].rearrange("p (a b) t -> p a b t", b=4),
                self.ps[:, 0:2, :].rearrange("p a (b t) -> p a b t", t=PART)), after=done)

        p.loop(NBLK, turn)
        kept = self.t_h.start(p.sp, self.h_dram, xn[:], after=p.dve.counter.here())
        inv = self.sb(stack, "x_inv", [PART, TOK])
        tmp = self.sb(stack, "x_tmp", [PART, 2, TOK])
        self.rms_inverse(lambda c: xn[:, c, :], DC, D, inv[:], tmp)
        p.dve.wait(kept)
        self.normed(lambda c: xn[:, c, :], lambda c: xn[:, c, :], inv[:], "norm_mix_pre")
        p.meet()

    def gla(self, xn, ycat):
        p, i, nc = self.p, self.i, self.nc
        w_in = i["w_in"].rearrange("a k n -> (a k) n")
        st = ExitStack()
        qkv = self.sb(st, "g_qkv", [PART, 8, TOK])
        gate = self.sb(st, "g_gate", [PART, 4, TOK])
        la_dram = nc.dram_tensor("la_dram", (NBLK, PART, 512), F32, kind="Internal").ap()
        p.meet()
        with ExitStack() as gs:
            self.weight_slots(gs)
            zp = [self.sb(gs, f"g_zp{s}", [PART, TOK + 2]) for s in range(2)]
            cv = [self.sb(gs, f"g_cv{s}", [PART, TOK]) for s in range(2)]
            alo = self.sb(gs, "g_alo", [32, TOK])
            aup = self.sb(gs, "g_aup", [32, 512])
            ab = self.sb(gs, "g_ab", [PART, 512])
            la = self.sb(gs, "g_la", [PART, NBLK, 512])
            lb = self.sb(gs, "g_lb", [PART, NBLK, 512])
            for z in zp:
                p.dve(lambda e: e.memset(z[:, 0:1], 0.0))
                p.dve(lambda e: e.memset(z[:, TOK + 1:TOK + 2], 0.0))
            zeroed = p.dve(lambda e: e.memset(aup[:], 0.0))
            for d in range(2):
                self.t_misc.start(p.sp, aup[16 * d:16 * d + 16, 256 * d:256 * d + 256], i["gla_a_up"][0, d], after=zeroed)
                self.t_misc.start(p.sp, ab[:, 256 * d:256 * d + 256], i["gla_a_b"][0, d:d + 1, :].to_broadcast([PART, 256]))

            parity = [0]

            def conv_evac(n, bank, done):
                parity[0] ^= 1
                z, o = zp[parity[0]], cv[parity[0]]
                free = p.act(lambda e: e.activation(z[:, 1:TOK + 1].rearrange("p (h t) -> p h t", h=2), bank, ACTF.Copy),
                             after=done)
                p.dve(lambda e: e.tensor_scalar(o[:], z[:, 0:TOK], self.col("conv", n), None, ALU.mult), after=free)
                p.dve(lambda e: e.scalar_tensor_tensor(out=o[:], in0=z[:, 1:TOK + 1], scalar=self.col("conv", n + 8),
                                                       in1=o[:], op0=ALU.mult, op1=ALU.add))
                c = p.dve(lambda e: e.scalar_tensor_tensor(out=o[:], in0=z[:, 2:TOK + 2], scalar=self.col("conv", n + 16),
                                                           in1=o[:], op0=ALU.mult, op1=ALU.add))
                p.act(lambda e: e.activation(qkv[:, n, :], o[:], ACTF.Silu), after=c)
                return [free]

            self.gemm(lambda g: w_in[:, bass.ds(g * 256 + 1856, 256)], DC, 4, 2, lambda k, h: xn[:, k, h * HALF:(h + 1) * HALF],
                      conv_evac, None)

            def gate_evac(n, bank, done):
                return [p.act(lambda e: e.activation(gate[:, n, :].rearrange("p (h t) -> p h t", h=2), bank, ACTF.Silu),
                              after=done)]

            self.gemm(lambda g: w_in[:, bass.ds(g * 256 + 2880, 256)], DC, 2, 2, lambda k, h: xn[:, k, h * HALF:(h + 1) * HALF],
                      gate_evac, None)

            def alo_evac(n, bank, done):
                return [p.act(lambda e: e.activation(alo[:].rearrange("p (h t) -> p h t", h=2), bank[0:32], ACTF.Copy), after=done)]

            self.gemm(lambda g: w_in[:, 3392:3424], DC, 1, 1, lambda k, h: xn[:, k, h * HALF:(h + 1) * HALF], alo_evac, None, m=32)
            p.act(lambda e: e.activation(qkv[:, 0:2, :], qkv[:, 0:2, :], ACTF.Copy, scale=CH ** -0.5))
            p.meet(self.t_misc.here())
            for n in range(NBLK):
                done = p.pe(lambda e: e.matmul(self.ps[:, n, :], alo[:, n * PART:(n + 1) * PART], aup[:], start=True, stop=True),
                            mark=True)
            halves, low = (slice(0, NBLK // 2), slice(NBLK // 2, NBLK)), [None, None]
            for n, h in enumerate(halves):
                p.dve(lambda e: e.tensor_tensor(la[:, h], self.ps[:, h], bass_rep(ab[:], NBLK // 2), ALU.add), after=done)
                m = p.dve(lambda e: e.scalar_tensor_tensor(out=lb[:, h], in0=la[:, h], scalar=-1.0, in1=la[:, h], op0=ALU.mult, op1=ALU.min))
                low[n] = p.act(lambda e: e.activation(lb[:, h], lb[:, h], ACTF.Exp), after=m)
                p.dve(lambda e: e.tensor_scalar(la[:, h], la[:, h], 0.0, None, ALU.min))
            for n, h in enumerate(halves):
                a = p.act(lambda e: e.activation(lb[:, h], lb[:, h], ACTF.Ln, bias=1.0), after=low[n])
                m = p.dve(lambda e: e.tensor_tensor(la[:, h], la[:, h], lb[:, h], ALU.subtract), after=a)
            kept = self.t_misc.start(p.sp, la_dram.rearrange("n p c -> p n c"), la[:], after=m)
            p.meet(kept)
        self.dump("d_qkv", qkv[:])
        with ExitStack() as ls:
            gsum = self.sb(ls, "gsum", [PART, 2, GSLOT, PART])
            mask = self.sb(ls, "gmask", [PART, 2, GLEV, CH])
            lat = self.sb(ls, "g_lat", [PART, 2, 256])
            E = self.sb(ls, "g_E", [PART, 4, GSLOT, PART])
            Qs = self.sb(ls, "g_Qs", [PART, 4, GLEV, CH])
            Qe = self.sb(ls, "g_Qe", [PART, 4, PART])
            Kb = self.sb(ls, "g_Kb", [PART, 4, GLEV + 1, PART])
            VT = self.sb(ls, "g_VT", [PART, 4, PART])
            KeT = self.sb(ls, "g_KeT", [PART, 4, PART])
            VP = self.sb(ls, "g_VP", [PART, 4, PART])
            SM = self.sb(ls, "g_SM", [PART, 4, GLEV, CH])
            Pc = self.sb(ls, "g_Pc", [PART, 4, CH])
            Pb = self.sb(ls, "g_Pb", [PART, 4, PART])
            S = self.sb(ls, "g_S", [PART, 4, PART])
            self.t_misc.start(p.sp, gsum[:].rearrange("p a b c -> p (a b c)"), i["k_gsum"])
            self.t_misc.start(p.sp, mask[:].rearrange("p a b c -> p (a b c)"), i["k_gla_mask"])
            for t in (Qe[:], Pb[:], S[:], ycat[:, 4:8, :]):
                p.dve(lambda e: e.memset(t, 0.0), chain=False)
            p.dve(lambda e: e.memset(E[:, :, 0, :], 1.0), chain=False)
            p.pool(lambda e: e.memset(Kb[:], 0.0))
            p.meet(self.t_misc.here())

            pe, act, dve, pool, ps = p.pe, p.act, p.dve, p.pool, self.ps
            DIRS, HS, L = range(2), [slice(0, 64), slice(64, 128)], [slice(0, 2), slice(2, 4)]

            def turn(t, last):
                before = p.all_done()
                self.t_in.start(p.sp, lat[:, 0, :], la_dram[t, :, 0:256], after=before)
                loaded = self.t_in.start(p.sp, lat[:, 1, :], la_dram[t * -1 + 7, :, 256:512])
                pe.wait([loaded, before])
                made = [None, None]
                for d in DIRS:
                    for pr in range(2):
                        for s in range(2):
                            done = pe(lambda e: e.matmul(ps[:, 4 * d + 2 * pr + s, :], lat[:, d, pr * PART:(pr + 1) * PART],
                                                         gsum[:, d, 1 + 4 * s:5 + 4 * s, :], start=True, stop=True), mark=True)
                        made[d] = act(lambda e: e.activation(E[:, 2 * d + pr, 1:GSLOT, :].rearrange("p a b -> p (a b)"),
                                                             ps[:, 4 * d + 2 * pr:4 * d + 2 * pr + 2, :].rearrange("p a b -> p (a b)"), ACTF.Exp),
                                      after=[done, before], chain=False)
                end = [before, before]
                for sub in range(2):
                    where = [(t * PART + sub * CH, sub), (t * -PART + (7 * PART + (1 - sub) * CH), 1 - sub)]
                    qd, kd, ke, vd, tr, sc, tv = ([None, None] for _ in range(7))
                    for d in DIRS:
                        tok, u = where[d]
                        W = bass.ds(tok, CH)
                        eu = E[:, L[d], :, u * CH:(u + 1) * CH]
                        vd[d] = act(lambda e: e.activation(VT[:, L[d]].rearrange("p l (h t) -> p (l h) t", h=2), qkv[:, 4:8, W], ACTF.Copy),
                                    after=end[d], chain=False)
                        for q_ in (dve, pool):
                            q_.wait([end[d], made[d]])
                        for H in HS:
                            ke[d] = pool(lambda e: e.tensor_tensor(Kb[H, L[d], GLEV, H], qkv[H, 2:4, W], eu[H, :, GLEV + 1], ALU.mult), chain=False)
                        for H in HS:
                            qe = pool(lambda e: e.tensor_tensor(Qe[H, L[d], H], qkv[H, 0:2, W], eu[H, :, GLEV], ALU.mult), chain=False)
                        qd[d] = [qe, dve(lambda e: e.tensor_tensor(Qs[:, L[d]], rep_mid(qkv[:, 0:2, W], GLEV), eu[:, :, 0:GLEV], ALU.mult), chain=False)]
                        for H in HS:
                            kd[d] = dve(lambda e: e.tensor_tensor(Kb[H, L[d], 0:GLEV, H], rep_mid(qkv[H, 2:4, W], GLEV), eu[H, :, 0:GLEV], ALU.mult),
                                        chain=False)
                    for d in DIRS:
                        pe.wait([ke[d], vd[d], end[d]])
                        for l in range(2):
                            pe(lambda e: e.transpose(ps[:, 4 * d, l * PART:(l + 1) * PART], Kb[:, 2 * d + l, GLEV, :], self.ident[:]))
                        for l in range(2):
                            tr[d] = pe(lambda e: e.transpose(ps[:, 4 * d, 256 + l * PART:256 + (l + 1) * PART], VT[:, 2 * d + l, :], self.ident[:]),
                                       mark=(l == 1))
                        act(lambda e: e.activation(KeT[:, L[d]].rearrange("p a b -> p (a b)"), ps[:, 4 * d, 0:256], ACTF.Copy), after=tr[d], chain=False)
                        tv[d] = act(lambda e: e.activation(VP[:, L[d]].rearrange("p a b -> p (a b)"), ps[:, 4 * d, 256:512], ACTF.Copy), chain=False)
                    for d in DIRS:
                        pe.wait([qd[d], kd[d]])
                        for l in range(2):
                            for v in range(GLEV):
                                for H in HS:
                                    sc[d] = pe(lambda e: e.matmul(ps[H, 4 * d + 1 + l, v * CH:(v + 1) * CH], Kb[:, 2 * d + l, v, H],
                                                                  Qs[:, 2 * d + l, v, :], start=True, stop=True),
                                               mark=(l == 1 and v == GLEV - 1 and H is HS[1]))
                    pc, pb, oo, ss, sm = ([None, None] for _ in range(5))
                    for d in DIRS:
                        m = dve(lambda e: e.tensor_tensor(SM[:, L[d]].rearrange("p l v t -> p l (v t)"), ps[:, 4 * d + 1:4 * d + 3, 0:GLEV * CH],
                                                          bass_rep(mask[:, d].rearrange("p v t -> p (v t)"), 2), ALU.mult), after=sc[d], chain=False)
                        pc[d] = dve(lambda e: e.tensor_reduce(Pc[:, L[d]], SM[:, L[d]].rearrange("p l v t -> p l t v"), AX.X, ALU.add), after=m,
                                    chain=False)
                        for H in HS:
                            pb[d] = act(lambda e: e.activation(Pb[H, L[d], H], Pc[H, L[d]], ACTF.Copy), after=pc[d], chain=False)
                    for d in DIRS:
                        last_tok = where[d][1] * CH + (CH - 1 if d == 0 else 0)
                        pe.wait([tv[d], pb[d]])
                        for l in range(2):
                            ss[d] = pe(lambda e: e.matmul(ps[:, 4 * d + 3, 256 + l * PART:256 + (l + 1) * PART], KeT[:, 2 * d + l, :], VP[:, 2 * d + l, :],
                                                          start=True, stop=True), mark=False)
                        for l in range(2):
                            at = ps[:, 4 * d + 3, l * PART:(l + 1) * PART]
                            pe(lambda e: e.matmul(at, VP[:, 2 * d + l, :], Pb[:, 2 * d + l, :], start=True, stop=False))
                            oo[d] = pe(lambda e: e.matmul(at, S[:, 2 * d + l, :], Qe[:, 2 * d + l, :], start=False, stop=True), mark=(l == 1))
                        yv = ycat[:, 4:8, bass.ds(where[d][0], CH)]
                        y = dve(lambda e: e.tensor_tensor(yv, yv, ps[:, 4 * d + 3, 0:256].rearrange("p (a t) -> p a t", t=CH), ALU.add), after=oo[d])
                        m = dve(lambda e: e.tensor_tensor(S[:, L[d]], S[:, L[d]], rep_last(E[:, L[d], GLEV, last_tok:last_tok + 1], PART), ALU.mult),
                                chain=False)
                        m = dve(lambda e: e.tensor_tensor(S[:, L[d]], S[:, L[d]], ps[:, 4 * d + 3, 256:512].rearrange("p (a b) -> p a b", a=2), ALU.add),
                                after=m, chain=False)
                        end[d] = [m, oo[d]]

            p.loop(NBLK, turn)
            p.meet()
        self.dump("d_glao", ycat[:, 4:8, :])
        with ExitStack() as ps_:
            two = lambda x: x.rearrange("p (h t) -> p h t", h=2)
            tmp = self.sb(ps_, "g_tmp", [PART, 2, TOK])
            summed = [None, None]
            for h in range(4):
                sq = p.act(lambda e: e.activation(tmp[:, h % 2, :], ycat[:, 4 + h, :], ACTF.Square), after=summed[h % 2])
                summed[h % 2] = self.token_sums(tmp[:, h % 2, :], self.ones[:, 0:2], 16 * h, sq)
            m = self.rsqrt_small(64, summed, ALU.mult, 1.0 / PART, ALU.add, 1e-6)
            for h in range(4):
                y = ycat[:, 4 + h, :]
                heads = self.st[:, 1, 16 * h:16 * h + 16].rearrange("p (b two) -> p b two", two=2)[:, :, 0:1]
                spread = self.over_channels(heads, tmp[:, h % 2, :], m)
                p.dve(lambda e: e.scalar_tensor_tensor(out=two(y), in0=two(y), scalar=self.col("gla_norm"), in1=ps[:, 6:8, :],
                                                       op0=ALU.mult, op1=ALU.mult), after=spread)
                p.dve(lambda e: e.tensor_tensor(y, y, gate[:, h, :], ALU.mult))
            p.meet()
        st.close()

    def rwkv(self, xn, ycat):
        p, i, nc = self.p, self.i, self.nc
        w_in = i["w_in"].rearrange("a k n -> (a k) n")
        sg_dram = nc.dram_tensor("sg_dram", (2, NBLK + 1, PART, RW), F32, kind="Internal").ap()
        lo_dram = nc.dram_tensor("lo_dram", (3, PART, TOK), F32, kind="Internal").ap()
        st = ExitStack()
        rkv = self.sb(st, "r_rkv", [PART, 12, TOK])
        p.meet()
        with ExitStack() as gs:
            self.weight_slots(gs)
            zp = [self.sb(gs, f"r_zp{s}", [PART, TOK + 2]) for s in range(2)]
            sh = [self.sb(gs, f"r_sh{s}", [PART, TOK]) for s in range(2)]
            wlo = self.sb(gs, "r_wlo", [PART, TOK])
            alo = self.sb(gs, "r_alo", [CH, TOK])
            sglo = self.sb(gs, "r_sglo", [PART, TOK])
            for z in zp:
                p.dve(lambda e: e.memset(z[:, 0:1], 0.0))
                p.dve(lambda e: e.memset(z[:, TOK + 1:TOK + 2], 0.0))

            def shifted(par, bank, done, mu, dst, rows=PART):
                z, s = zp[par], sh[par]
                free = p.act(lambda e: e.activation(z[0:rows, 1:TOK + 1].rearrange("p (h t) -> p h t", h=2), bank[0:rows], ACTF.Copy),
                             after=[done, p.dve.counter.here()])
                p.dve(lambda e: e.tensor_tensor(s[0:rows], z[0:rows, 0:TOK], z[0:rows, 2:TOK + 2], ALU.add), after=free)
                p.dve(lambda e: e.scalar_tensor_tensor(out=s[0:rows], in0=s[0:rows], scalar=0.5, in1=z[0:rows, 1:TOK + 1],
                                                       op0=ALU.mult, op1=ALU.subtract))
                end = p.dve(lambda e: e.scalar_tensor_tensor(out=dst, in0=s[0:rows], scalar=mu, in1=z[0:rows, 1:TOK + 1],
                                                             op0=ALU.mult, op1=ALU.add))
                return free, end

            rhs = lambda k, h: xn[:, k, h * HALF:(h + 1) * HALF]
            parity = [0]

            def rkv_evac(n, bank, done):
                parity[0] ^= 1
                return [shifted(parity[0], bank, done, self.col("mu", n), rkv[:, n, :])[0]]

            self.gemm(lambda g: w_in[:, bass.ds(g * 256, 256)], DC, 6, 2, rhs, rkv_evac, None)

            def w_evac(n, bank, done):
                f, end = shifted(0, bank, done, self.col("mu", 12), wlo[:])
                p.act(lambda e: e.activation(wlo[:], wlo[:], ACTF.Tanh), after=end)
                return [f]

            self.gemm(lambda g: w_in[:, 1536:1664], DC, 1, 1, rhs, w_evac, None)
            self.gemm(lambda g: w_in[:, 1664:1728], DC, 1, 1, rhs,
                      lambda n, bank, done: [shifted(1, bank, done, self.col("mu_a", 0, CH), alo[:], CH)[0]], None, m=CH)

            def g_evac(n, bank, done):
                f, end = shifted(0, bank, done, self.col("mu_g"), sglo[:])
                p.act(lambda e: e.activation(sglo[:], sglo[:], ACTF.Sigmoid), after=end)
                return [f]

            self.gemm(lambda g: w_in[:, 1728:1856], DC, 1, 1, rhs, g_evac, None)
            p.meet()
            self.t_st.start(p.sp, lo_dram[0], wlo[:])
            self.t_st.start(p.sp, lo_dram[1, 0:CH], alo[:])
            p.meet(self.t_st.start(p.sp, lo_dram[2], sglo[:]))
        kb = xn
        self.dump("d_rkv", rkv[:])
        with ExitStack() as gs:
            wlo = self.sb(gs, "r_wlo2", [PART, TOK])
            alo = self.sb(gs, "r_alo2", [CH, TOK])
            wup = self.sb(gs, "r_wup", [PART, 2, RW])
            w0 = self.sb(gs, "r_w0", [PART, 2, RW])
            aup = self.sb(gs, "r_aup", [CH, RW])
            sg = self.sb(gs, "r_sg", [PART, 2, 2, RW])
            hsel = self.sb(gs, "r_hsel", [PART, 2])
            omka = self.sb(gs, "r_omka", [PART, 4])
            a = self.sb(gs, "r_a", [PART, TOK])
            t1 = self.sb(gs, "r_t1", [PART, TOK])
            t2 = self.sb(gs, "r_t2", [PART, TOK])
            z = p.dve(lambda e: e.memset(wup[:], 0.0))
            self.t_misc.start(p.sp, wlo[:], lo_dram[0])
            self.t_misc.start(p.sp, alo[:], lo_dram[1, 0:CH])
            self.t_misc.start(p.sp, hsel[:], i["k_head_sel"])
            self.t_misc.start(p.sp, aup[:], i["rwkv_a_up"][0])
            for d in range(2):
                self.t_misc.start(p.sp, wup[CH * d:CH * d + CH, d, :], i["rwkv_w_up"][0, d], after=z)
                self.t_misc.start(p.sp, w0[:, d, :], i["rwkv_w0"][0, d:d + 1, :].to_broadcast([PART, RW]))
            p.meet(self.t_misc.here())
            stored = None
            for n in range(NBLK):
                b = n % 2
                for d in range(2):
                    done = p.pe(lambda e: e.matmul(self.ps[:, 2 * b + d, :], wlo[:, n * PART:(n + 1) * PART], wup[:, d, :],
                                                   start=True, stop=True), after=p.act.counter.here() if d == 0 else None, mark=(d == 1))
                m = p.dve(lambda e: e.tensor_tensor(sg[:, b], self.ps[:, 2 * b:2 * b + 2, :], w0[:], ALU.add),
                          after=[done, self.t_st.here()])
                s = p.act(lambda e: e.activation(sg[:, b], sg[:, b], ACTF.Sigmoid), after=m)
                stored = self.t_st.start(p.sp, sg_dram[0, n], sg[:, b, 0], after=s)
                self.t_st.start(p.sp, sg_dram[1, NBLK - 1 - n], sg[:, b, 1])
                if n == 0:
                    self.t_st.start(p.sp, sg_dram[:, NBLK].rearrange("d p c -> p d c"), sg[:, b])
            p.dve(lambda e: e.tensor_scalar(omka[:], self.cols[:, self.cols_at["rwkv_k_a"]:self.cols_at["rwkv_k_a"] + 4], -1.0, 1.0,
                                            ALU.mult, ALU.add))
            t12, freed = (t1, t2), [None, None]
            for c in range(4):
                kk, k = kb[:, c, :], rkv[:, 4 + c, :]
                p.dve(lambda e: e.tensor_scalar(kk, k, self.col("rwkv_k_k", c), None, ALU.mult))
                sq = p.dve(lambda e: e.tensor_tensor(t12[c % 2][:], kk, kk, ALU.mult), after=freed[c % 2])
                freed[c % 2] = sums = self.token_sums(t12[c % 2], hsel[:], 16 * c, sq)
            m = self.rsqrt_small(64, sums, ALU.max, 1e-24)
            for c in range(4):
                kk, bb, k = kb[:, c, :], kb[:, 4 + c, :], rkv[:, 4 + c, :]
                spread = self.over_channels(self.st[:, 1, 16 * c:16 * c + 16].rearrange("p (b h) -> p b h", h=2), t2, m)
                p.pe.wait(p.act.counter.here())
                for h in range(2):
                    done = p.pe(lambda e: e.matmul(self.ps[:, h, :], aup[:, c * PART:(c + 1) * PART], alo[:, h * HALF:(h + 1) * HALF],
                                                   start=True, stop=True), mark=(h == 1))
                av = p.act(lambda e: e.activation(a[:].rearrange("p (h t) -> p h t", h=2), self.ps[:, 0:2, :], ACTF.Sigmoid,
                                                  bias=self.col("rwkv_a0", c)), after=[done, p.dve.counter.here()])
                p.dve(lambda e: e.tensor_tensor(kk.rearrange("p (h t) -> p h t", h=2), kk.rearrange("p (h t) -> p h t", h=2),
                                                self.ps[:, 6:8, :], ALU.mult), after=spread)
                p.dve(lambda e: e.tensor_tensor(bb, kk, a[:], ALU.mult), after=av)
                p.dve(lambda e: e.tensor_scalar(t1[:], a[:], self.col("rwkv_k_a", c), omka[:, c:c + 1], ALU.mult, ALU.add))
                p.dve(lambda e: e.tensor_tensor(k, k, t1[:], ALU.mult))
            p.meet(self.t_st.here())
        self.dump("d_kkb", kb[:])
        self.rwkv_scan(rkv, kb, ycat, sg_dram)
        self.dump("d_ry", ycat[:, 0:4, :])
        with ExitStack() as gs:
            hones = self.sb(gs, "r_hones2", [PART, PART])
            hsel = self.sb(gs, "r_hsel2", [PART, 2])
            gup = self.sb(gs, "r_gup", [PART, RW])
            sglo = self.sb(gs, "r_sglo2", [PART, TOK])
            mu = self.sb(gs, "r_mu", [PART, TOK])
            t1 = self.sb(gs, "r_u1", [PART, TOK])
            t2 = self.sb(gs, "r_u2", [PART, TOK])
            t3 = self.sb(gs, "r_u3", [PART, TOK])
            self.t_misc.start(p.sp, hones[:], i["k_head_ones"])
            self.t_misc.start(p.sp, hsel[:], i["k_head_sel"])
            self.t_misc.start(p.sp, gup[:], i["rwkv_g_up"][0])
            self.t_misc.start(p.sp, sglo[:], lo_dram[2])
            p.meet(self.t_misc.here())
            two = lambda x: x.rearrange("p (h t) -> p h t", h=2)

            def head_sum(src, base, after):
                for h in range(2):
                    done = p.pe(lambda e: e.matmul(self.ps[:, base + h, :], hones[:], src[:, h * HALF:(h + 1) * HALF], start=True, stop=True),
                                after=after, mark=(h == 1))
                return done

            t12, freed = (t1, t3), [None, None]
            for c in range(4):
                y = ycat[:, c, :]
                done = head_sum(y, 2 * (c % 2), p.dve.counter.here())
                p.dve(lambda e: e.scalar_tensor_tensor(out=two(y), in0=self.ps[:, 2 * (c % 2):2 * (c % 2) + 2, :], scalar=-1.0 / 64, in1=two(y),
                                                       op0=ALU.mult, op1=ALU.add), after=done)
                sq = p.dve(lambda e: e.tensor_tensor(t12[c % 2][:], y, y, ALU.mult), after=freed[c % 2])
                freed[c % 2] = sums = self.token_sums(t12[c % 2], hsel[:], 16 * c, sq)
            m = self.rsqrt_small(64, sums, ALU.mult, 1.0 / 64, ALU.add, 64e-5)
            for c in range(4):
                y, r, k, v = ycat[:, c, :], rkv[:, c, :], rkv[:, 4 + c, :], rkv[:, 8 + c, :]
                spread = self.over_channels(self.st[:, 1, 16 * c:16 * c + 16].rearrange("p (b h) -> p b h", h=2), t3, m)
                p.dve(lambda e: e.tensor_tensor(two(y), two(y), self.ps[:, 6:8, :], ALU.mult), after=spread)
                p.dve(lambda e: e.tensor_scalar(y, y, self.col("rwkv_ln_w", c), self.col("rwkv_ln_b", c), ALU.mult, ALU.add))
                m_ = p.dve(lambda e: e.scalar_tensor_tensor(out=t1[:], in0=r, scalar=self.col("rwkv_r_k", c), in1=k, op0=ALU.mult, op1=ALU.mult))
                done = head_sum(t1, 2, m_)
                p.dve(lambda e: e.tensor_tensor(two(t2[:]), self.ps[:, 2:4, :], two(v), ALU.mult), after=done)
                p.dve(lambda e: e.tensor_tensor(y, y, t2[:], ALU.add))
                for h in range(2):
                    done = p.pe(lambda e: e.matmul(self.ps[:, 0 + h, :], gup[:, c * PART:(c + 1) * PART], sglo[:, h * HALF:(h + 1) * HALF],
                                                   start=True, stop=True), after=p.dve.counter.here(), mark=(h == 1))
                p.dve(lambda e: e.tensor_tensor(two(y), two(y), self.ps[:, 0:2, :], ALU.mult), after=done)
            p.meet()
        st.close()

    def rwkv_scan(self, rkv, kb, ycat, sg_dram):
        p, i, ps = self.p, self.i, self.ps
        pe, act, dve = p.pe, p.act, p.dve
        DIRS = range(2)
        with ExitStack() as ls:
            tri = self.sb(ls, "tri", [PART, 2, 2 * PART])
            gmask = self.sb(ls, "gram_mask", [PART, 2, 2, CH])
            lmask = self.sb(ls, "lev_mask", [PART, LEVELS, 2, CH])
            eye = self.sb(ls, "eye", [PART, CH])
            sig = self.sb(ls, "sig", [PART, 2, RW])
            Ei, En, Ex = (self.sb(ls, f"s_{n}", [PART, LANES, PART]) for n in ("Ei", "En", "Ex"))
            AR = self.sb(ls, "s_AR", [PART, LANES, 2, CH])
            bd = {n: self.sb(ls, f"s_{n}", [PART, LANES, PART])
                  for n in ("Vb", "Ab", "Bb", "Kb", "Nb", "Mk", "XTb", "Tb", "Sb", "BT", "KT", "VT")}
            Vb, Ab, Bb, Kb, Nb, Mk, XTb, Tb, Sb, BT, KT, VT = bd.values()
            cm = {n: self.sb(ls, f"s_{n}", [PART, LANES, CH]) for n in ("Vc", "Mrb", "Mrk", "X", "XT", "T", "Rn", "S")}
            Vc, Mrb, Mrk, X, XT, T, Rn, S = cm.values()
            fac = self.sb(ls, "s_fac", [PART, LANES, 1])
            for t, n in ((tri[:].rearrange("p a b -> p (a b)"), "k_tri"), (gmask[:].rearrange("p a b c -> p (a b c)"), "k_gram_mask"),
                         (lmask[:].rearrange("p a b c -> p (a b c)"), "k_lev_mask"), (eye[:], "k_stack_eye")):
                self.t_misc.start(p.sp, t, i[n])
            for t in (Vb[:], Ab[:], Bb[:], Kb[:], Nb[:], Mk[:], XTb[:], Tb[:]):
                dve(lambda e: e.memset(t, 0.0), chain=False)
            for t in (S[:], Sb[:], ycat[:, 0:4, :]):
                p.pool(lambda e: e.memset(t, 0.0), chain=False)
            dve(lambda e: e.memset(fac[:], 1.0), chain=False)
            p.meet(self.t_misc.here())
            HS = [slice(0, 64), slice(64, 128)]
            L = [slice(0, 4), slice(4, 8)]
            lanes = [range(0, 4), range(4, 8)]
            half_bank = lambda d, b: ps[:, 4 * d + b, 0:256].rearrange("p (l t) -> p l t", t=CH)
            full_bank = lambda d, b: ps[:, 4 * d + b, :].rearrange("p (l t) -> p l t", t=PART)

            def each(d, b, width, lhsT, rhs, after, start=True, stop=True):
                pe.wait(after)
                for l in lanes[d]:
                    at = (l - 4 * d) * width
                    for H in (HS if width == CH else [slice(0, PART)]):
                        done = pe(lambda e: e.matmul(ps[H, 4 * d + b, at:at + width], lhsT(l)[:, H], rhs(l), start=start, stop=stop),
                                  mark=(l == lanes[d][-1] and H.stop == PART))
                return done

            def sums(d, b, terms, after):
                pe.wait(after)
                for l in lanes[d]:
                    at = (l - 4 * d) * CH
                    for H in HS:
                        for n, (lhsT, rhs) in enumerate(terms):
                            done = pe(lambda e: e.matmul(ps[H, 4 * d + b, at:at + CH], lhsT(l)[:, H], rhs(l), start=(n == 0),
                                                         stop=(n == len(terms) - 1)),
                                      mark=(l == lanes[d][-1] and H is HS[1] and n == len(terms) - 1))
                return done

            def turned(d, b, src, after):
                pe.wait(after)
                for l in lanes[d]:
                    at = (l - 4 * d) * PART
                    done = pe(lambda e: e.transpose(ps[:, 4 * d + b, at:at + PART], src[:, l, :], self.ident[:]), mark=(l == lanes[d][-1]))
                return done

            def spread(dst, d, src, after):
                for H in HS:
                    done = act(lambda e: e.activation(dst[H, L[d], H], src(H), ACTF.Copy), after=after, chain=False)
                return done

            def turn(t, last):
                before = p.all_done()
                made = [None, None]
                pe.wait([self.t_in.here(), before])
                for d in DIRS:
                    for l in lanes[d]:
                        x = l - 4 * d
                        done = pe(lambda e: e.matmul(ps[:, 4 * d + x // 2, (x % 2) * 256:(x % 2) * 256 + 256],
                                                     sig[:, d, x * PART:(x + 1) * PART], tri[:, d, :], start=True, stop=True), mark=(x == 3))
                    cum = ps[:, 4 * d:4 * d + 2, :].rearrange("p b (l x t) -> p (b l) x t", l=2, x=2)
                    act(lambda e: e.activation(Ex[:, L[d]], cum[:, :, 1, :], ACTF.Exp), after=[done, before], chain=False)
                    act(lambda e: e.activation(En[:, L[d]], cum[:, :, 0, :], ACTF.Exp, scale=-1.0), chain=False)
                    made[d] = act(lambda e: e.activation(Ei[:, L[d]], cum[:, :, 0, :], ACTF.Exp), chain=False)
                self.t_in.start(p.sp, sig[:], sg_dram[:, bass.ds(t + 1, 1)].rearrange("d a p c -> p (d a) c"), after=done)
                end = [before, before]
                for sub in range(2):
                    where = [(t * PART + sub * CH, sub), (t * -PART + (7 * PART + (1 - sub) * CH), 1 - sub)]
                    ab, kr, vb, sc, sb = ([None, None] for _ in range(5))
                    for d in DIRS:
                        tok, u = where[d]
                        tc, W = slice(u * CH, (u + 1) * CH), bass.ds(tok, CH)
                        last_tok = u * CH + (CH - 1 if d == 0 else 0)
                        vb[d] = spread(Vb, d, lambda H: rkv[H, 8:12, W], end[d])
                        dve.wait([end[d], made[d]])
                        dve(lambda e: e.tensor_tensor(AR[:, L[d], 0], kb[:, 0:4, W], Ex[:, L[d], tc], ALU.mult), chain=False)
                        for H in HS:
                            dve(lambda e: e.tensor_tensor(Bb[H, L[d], H], kb[H, 4:8, W], En[H, L[d], tc], ALU.mult), chain=False)
                        ab[d] = dve(lambda e: e.tensor_tensor(AR[:, L[d], 1], rkv[:, 0:4, W], Ei[:, L[d], tc], ALU.mult), chain=False)
                        for H in HS:
                            kr[d] = dve(lambda e: e.tensor_tensor(Kb[H, L[d], H], rkv[H, 4:8, W], En[H, L[d], tc], ALU.mult), chain=False)
                        f = dve(lambda e: e.tensor_tensor(fac[:, L[d]], fac[:, L[d]], Ei[:, L[d], last_tok:last_tok + 1], ALU.mult), chain=False)
                        sc[d] = dve(lambda e: e.tensor_tensor(S[:, L[d]], S[:, L[d]], rep_last(fac[:, L[d]], CH), ALU.mult), after=f, chain=False)
                        dve(lambda e: e.tensor_copy(fac[:, L[d]], Ei[:, L[d], last_tok:last_tok + 1]), after=sc[d], chain=False)
                    gb, gk, tv, tb, tk = ([None, None] for _ in range(5))
                    for d in DIRS:
                        gb[d] = each(d, 0, PART, lambda l: Bb[:, l, :], lambda l: AR[:, l].rearrange("p a b -> p (a b)"), [ab[d], end[d]])
                        gk[d] = each(d, 1, PART, lambda l: Kb[:, l, :], lambda l: AR[:, l].rearrange("p a b -> p (a b)"), kr[d])
                        tv[d] = turned(d, 2, Vb, vb[d])
                        tb[d] = turned(d, 3, Bb, None)
                    nb, mk, mr, vt, vc, bt, kt, af = ([None, None] for _ in range(8))
                    for d in DIRS:
                        for H in HS:
                            nb[d] = dve(lambda e: e.tensor_tensor(Nb[H, L[d], H], full_bank(d, 0)[H, :, 0:CH], bass_rep(gmask[H, d, 0], 4), ALU.mult),
                                        after=gb[d], chain=False)
                        af[d] = spread(Ab, d, lambda H: AR[H, L[d], 0], ab[d])
                    for d in DIRS:
                        for H in HS:
                            mk[d] = dve(lambda e: e.tensor_tensor(Mk[H, L[d], H], full_bank(d, 1)[H, :, 0:CH], bass_rep(gmask[H, d, 0], 4), ALU.mult),
                                        after=gk[d], chain=False)
                        act(lambda e: e.activation(VT[:, L[d]], full_bank(d, 2), ACTF.Copy), after=tv[d], chain=False)
                        for H in HS:
                            vc[d] = act(lambda e: e.activation(Vc[H, L[d]], full_bank(d, 2)[H, :, H], ACTF.Copy), chain=False)
                        tk[d] = turned(d, 2, Kb, vc[d])
                        sb[d] = spread(Sb, d, lambda H: S[H, L[d]], sc[d])
                    for d in DIRS:
                        dve(lambda e: e.tensor_tensor(Mrb[:, L[d]], full_bank(d, 0)[:, :, CH:], bass_rep(gmask[:, d, 1], 4), ALU.mult),
                            after=gb[d], chain=False)
                        mr[d] = dve(lambda e: e.tensor_tensor(Mrk[:, L[d]], full_bank(d, 1)[:, :, CH:], bass_rep(gmask[:, d, 1], 4), ALU.mult),
                                    chain=False)
                        bt[d] = act(lambda e: e.activation(BT[:, L[d]], full_bank(d, 3), ACTF.Copy), after=tb[d], chain=False)
                    rh, rn = [None, None], [None, None]
                    for d in DIRS:
                        rh[d] = sums(d, 3, ((lambda l: Ab[:, l, :], lambda l: S[:, l, :]), (lambda l: Mk[:, l, :], lambda l: Vc[:, l, :])),
                                     [af[d], sc[d], mk[d], bt[d]])
                        kt[d] = act(lambda e: e.activation(KT[:, L[d]], full_bank(d, 2), ACTF.Copy), after=tk[d], chain=False)
                    for d in DIRS:
                        rn[d] = dve(lambda e: e.tensor_scalar(Rn[:, L[d]], half_bank(d, 3), -1.0, None, ALU.mult), after=rh[d], chain=False)
                    x, xt, xb, xy = ([None, None] for _ in range(4))
                    for lev in range(LEVELS):
                        first, final = lev == 0, lev == LEVELS - 1
                        cur_x = (lambda l: eye[:]) if first else (lambda l: X[:, l, :])
                        cur_xt = (lambda l: eye[:]) if first else (lambda l: XT[:, l, :])
                        cur_xb = (lambda l: self.ident[:]) if first else (lambda l: XTb[:, l, :])
                        lx, tm, t2, xx = ([None, None] for _ in range(4))
                        for d in DIRS:
                            lx[d] = each(d, 0, CH, lambda l: Nb[:, l, :], cur_x, [nb[d], mr[d], x[d]])
                        for d in DIRS:
                            tm[d] = dve(lambda e: e.tensor_tensor(T[:, L[d]], half_bank(d, 0), bass_rep(lmask[:, lev, d], 4), ALU.mult),
                                        after=[lx[d], xy[d]], chain=False)
                            t2[d] = spread(Tb, d, lambda H: T[H, L[d]], [tm[d], xy[d]])
                        if not final:
                            for d in DIRS:
                                xx[d] = each(d, 1, CH, cur_xb, lambda l: T[:, l, :], [tm[d], xb[d]])
                        for d in DIRS:
                            xy[d] = each(d, 2, CH, lambda l: Tb[:, l, :], cur_xt, [t2[d], kt[d], xt[d]])
                        for d in DIRS:
                            if not final:
                                old = bass_rep(eye[:], 4) if first else X[:, L[d]]
                                x[d] = dve(lambda e: e.tensor_tensor(X[:, L[d]], old, half_bank(d, 1), ALU.subtract), after=[xx[d], x[d]], chain=False)
                            old = bass_rep(eye[:], 4) if first else XT[:, L[d]]
                            xt[d] = dve(lambda e: e.tensor_tensor(XT[:, L[d]], old, half_bank(d, 2), ALU.subtract), after=[xy[d], xt[d]], chain=False)
                            xb[d] = spread(XTb, d, lambda H: XT[H, L[d]], xt[d])
                    uu, uc, ub = ([None, None] for _ in range(3))
                    for d in DIRS:
                        uu[d] = each(d, 0, CH, lambda l: XTb[:, l, :], lambda l: Rn[:, l, :], [rn[d], xb[d]])
                    for d in DIRS:
                        uc[d] = dve(lambda e: e.tensor_copy(T[:, L[d]], half_bank(d, 0)), after=uu[d], chain=False)
                        ub[d] = spread(Tb, d, lambda H: T[H, L[d]], uc[d])
                    yy, ss = [None, None], [None, None]
                    for d in DIRS:
                        ss[d] = sums(d, 3, ((lambda l: BT[:, l, :], lambda l: T[:, l, :]), (lambda l: KT[:, l, :], lambda l: Vc[:, l, :])),
                                     [uc[d], bt[d], kt[d]])
                        yy[d] = sums(d, 1, ((lambda l: Sb[:, l, :], lambda l: AR[:, l, 1]), (lambda l: Tb[:, l, :], lambda l: Mrb[:, l, :]),
                                            (lambda l: VT[:, l, :], lambda l: Mrk[:, l, :])), [ub[d], sb[d]])
                    for d in DIRS:
                        s1 = dve(lambda e: e.tensor_tensor(S[:, L[d]], S[:, L[d]], half_bank(d, 3), ALU.add), after=ss[d], chain=False)
                    for d in DIRS:
                        yv = ycat[:, 0:4, bass.ds(where[d][0], CH)]
                        e1 = dve(lambda e: e.tensor_tensor(yv, yv, half_bank(d, 1), ALU.add), after=yy[d])
                        end[d] = [e1, yy[d]]

            p.pe.wait(self.t_in.start(p.sp, sig[:], sg_dram[:, 0].rearrange("d p c -> p d c")))
            p.loop(NBLK, turn)
            p.meet(self.t_in.here())

    def block1_tail(self, A, B, A_room):
        p, i = self.p, self.i
        two = lambda x: x.rearrange("p (h t) -> p h t", h=2)
        wide = lambda w, at=0: (lambda g: w[:, bass.ds(g * 256 + at, 256)])
        rhs = lambda x: (lambda k, h: x[:, k, h * HALF:(h + 1) * HALF])

        def keep(dst):
            return lambda n, bank, done: [p.act(lambda e: e.activation(two(dst[:, n, :]), bank, ACTF.Copy), after=done)]

        with ExitStack() as s:
            self.weight_slots(s)
            self.gemm(wide(i["w_out"][0]), DC, 4, 2, rhs(B), keep(A))
            p.meet()
            self.t_h.start(p.sp, B[:], self.h_dram)
            self.add_normed(A, "norm_mix_post", B, s)
            self.dump("d_h1", B[:])
        A_room.close()
        with ExitStack() as s:
            kept = self.t_h.start(p.sp, self.h_dram, B[:], after=p.dve.counter.here())
            xh, xl = (self.sb(s, n, [PART, DC, TOK], F32R) for n in ("hn_h", "hn_l"))

            def norm():
                with ExitStack() as s2:
                    inv = self.sb(s2, "f_inv", [PART, TOK])
                    tmp = self.sb(s2, "f_tmp", [PART, 2, TOK])
                    self.rms_inverse(lambda c: B[:, c, :], DC, D, inv[:], tmp)
                    parted = [None, None]
                    for c in range(DC):
                        t = tmp[:, c % 2, :]
                        m = p.dve(lambda e: e.scalar_tensor_tensor(out=t, in0=B[:, c, :], scalar=self.col("norm_ffn_pre", c), in1=inv[:],
                                                                   op0=ALU.mult, op1=ALU.mult), after=parted[c % 2])
                        parted[c % 2] = self.in_two_parts(xh[:, c, :], xl[:, c, :], t, m)
                    p.meet()
                    p.dve.wait(kept)
                    for c in range(DC):
                        p.dve(lambda e: e.memset(B[:, c, :], 0.0), chain=False)

            gate, up, down = i["ffn_gate"][0], i["ffn_up"][0], i["ffn_down"][0]
            act_g, act_h = (self.sb(s, n, [PART, TOK]) for n in ("act_g", "act_h"))
            gated = [None]

            def swiglu(b, bank, done, reader):
                if b == 0:
                    gated[0] = p.act(lambda e: e.activation(two(act_g[:]), bank, ACTF.Silu), after=[done, *reader])
                    return None, None, gated[0]
                m = p.dve(lambda e: e.tensor_tensor(two(act_h[:]), two(act_g[:]), bank, ALU.mult), after=[done, gated[0]])
                return act_h[:], m, m

            self.fused_mlp(s, DFF // PART, lambda g: [w[:, bass.ds(g * PART, PART)] for w in (gate, up)],
                           lambda g: down[bass.ds(g * PART, PART), :], norm, (xh, xl), swiglu,
                           lambda n, bank, done: p.dve(lambda e: e.tensor_tensor(two(B[:, n, :]), two(B[:, n, :]), bank, ALU.add), after=done))
            p.meet()
        A, B = B, self.sb(A_room, "B1_again", [PART, DC, TOK])
        self.t_h.start(p.sp, B[:], self.h_dram)
        with ExitStack() as s:
            self.weight_slots(s)
            with ExitStack() as s2:
                self.add_normed(A, "norm_ffn_post", B, s2)
            self.dump("d_h2", B[:])
            E = self.sb(s, "ple_e", [PART, DC, TOK])
            pT = self.sb(s, "pT", [PART, 2, TOK])
            prow = self.sb(s, "p_row", [PART, NBLK, 256])
            tmp = [self.sb(s, f"ple_t{n}", [PART, TOK]) for n in range(2)]
            got = self.t_misc.start(p.sp, prow[:], i["p"].rearrange("a b (n p) c -> p (a b n) c", p=PART), after=p.all_done())
            for c in range(2):
                for t in range(NBLK):
                    done = p.pe(lambda e: e.transpose(self.ps[:, 4 + 2 * c + t // 4, (t % 4) * PART:(t % 4 + 1) * PART],
                                                      prow[:, t, c * PART:(c + 1) * PART], self.ident[:]), after=[got, p.dve.counter.here()],
                                mark=(t == NBLK - 1))
                p.act(lambda e: e.activation(two(pT[:, c, :]), self.ps[:, 4 + 2 * c:6 + 2 * c, :], ACTF.Copy), after=done)
            p.meet()
            self.gemm(wide(i["ple_proj"][0]), 2, 4, 2, rhs(pT), keep(E))
            par = [0]

            def ple(n, bank, done):
                par[0] ^= 1
                t = tmp[par[0]]
                f = p.act(lambda e: e.activation(two(t[:]), bank, ACTF.Sigmoid, bias=self.col("ple_gate_b", n)),
                          after=[done, p.dve.counter.here()])
                p.dve(lambda e: e.tensor_tensor(A[:, n, :], t[:], E[:, n, :], ALU.mult), after=f)
                return [f]

            self.gemm(wide(i["ple_gate"][0]), DC, 4, 2, rhs(B), ple)
            p.meet()
        with ExitStack() as s2:
            self.add_normed(A, "norm_ple", B, s2)
        self.dump("d_h3", B[:])
        p.meet(self.t_h.start(p.sp, self.h_dram, B[:], after=p.dve.counter.here()))
        A_room.close()

    def ada(self, stack):
        p, i = self.p, self.i
        self.mod = self.sb(stack, "mod", [PART, 48, 2])
        self.gain = self.sb(stack, "gain", [PART, 3, DC])
        at = self.cols_at
        cols = lambda n: self.cols[:, at[n]:at[n] + DC]
        with ExitStack() as s:
            self.weight_slots(s, 4096)
            cc = self.sb(s, "cc", [PART, DC, 2])
            p.meet()
            p.act(lambda e: e.activation(cc[:, :, 0], cols("c_2"), ACTF.Silu))
            a = p.act(lambda e: e.activation(cc[:, :, 1], cols("c_ctx"), ACTF.Silu))
            w = i["w_ada_2"][0]
            self.gemm(lambda g: w[:, bass.ds(g * 512, 512)], DC, 12, 4, lambda k, h: cc[:, k, :],
                      lambda n, bank, done: [p.dve(lambda e: e.tensor_scalar(self.mod[:, n, :] if isinstance(n, int) else
                                                                             self.mod[:, bass.ds(n, 1), :].rearrange("p a b -> p (a b)"),
                                                                             bank[:, 0, 0:2], self.col("b_ada_2", n), None, ALU.add),
                                                   after=done)], a, tokens=2)
            for k, (g, sc, who) in enumerate((("norm1_g_2", 8, 0), ("norm1_g_2", 8, 1), ("norm2_g_2", 32, 0))):
                p.dve(lambda e: e.scalar_tensor_tensor(out=self.gain[:, k, :], in0=self.mod[:, sc:sc + DC, who], scalar=1.0, in1=cols(g),
                                                       op0=ALU.add, op1=ALU.mult))
            p.meet()

    def modulated(self, dst, x, inv, gain, shift, who):
        p = self.p
        for c in range(DC):
            p.dve(lambda e: e.scalar_tensor_tensor(out=dst(c), in0=x(c), scalar=self.gain[:, gain, c:c + 1], in1=inv, op0=ALU.mult, op1=ALU.mult))
            p.act(lambda e: e.activation(dst(c), dst(c), ACTF.Identity, bias=self.mod[:, shift + c, who:who + 1]), after=p.dve.counter.here())

    def block2_mixers(self, hxA, Y):
        p, i, nc, ps = self.p, self.i, self.nc, self.ps
        two = lambda x: x.rearrange("p (h t) -> p h t", h=2)
        rhs = lambda k, h: hxA[:, k, h * HALF:(h + 1) * HALF]
        w_in = i["w_in_2"][0]
        st = ExitStack()
        q = self.sb(st, "b_q", [PART, 4, TOK])
        qr = self.sb(st, "b_qr", [PART, 4, TOK])
        kr = self.sb(st, "b_kr", [PART, 4, TOK])
        VV = self.sb(st, "b_VV", [PART, ROWS - 1, RW])
        kc = self.sb(st, "b_kc", [PART, 4, CTX])
        vc = self.sb(st, "b_vc", [PART, 2, RW])
        bias = self.sb(st, "a_bias", [PART, 4, RPB_R, GRID])

        def values_from(x, blocks_, dst, free, halfway=None):
            wq = [self.w[n][:, 0:2048].rearrange("p (c n) -> p c n", c=DC) for n in range(2)]
            start = free + [p.pe.counter.here(), p.act.counter.here()]
            for s_ in range(2):
                self.t_w[s_].start(p.sp, wq[s_], w_in[:, 1024 + 256 * s_:1280 + 256 * s_].rearrange("(c p) n -> p c n", p=PART), after=start)
            p.pe.wait([self.t_w[0].here(), self.t_w[1].here(), start])
            read = [None, None]
            for n in range(blocks_):
                if halfway and n == blocks_ // 2:
                    halfway()
                for s_ in range(2):
                    for k in range(DC):
                        done = p.pe(lambda e: e.matmul(ps[:, n % 2, 256 * s_:256 * s_ + 256], x[:, k, n * PART:(n + 1) * PART], wq[s_][:, k, :],
                                                       start=(k == 0), stop=(k == DC - 1)),
                                    after=read[n % 2] if k == 0 and s_ == 0 else None, mark=(k == DC - 1))
                read[n % 2] = p.act(lambda e: e.activation(dst(n), ps[:, n % 2, :], ACTF.Copy), after=done)

        rpb_dram = nc.dram_tensor("rpb_dram", (HEADS, RPB_R, GRID, PART), F32, kind="Internal").ap()
        with ExitStack() as s:
            self.weight_slots(s)
            hc = self.sb(s, "b_hc", [PART, DC, CTX])
            crow = self.sb(s, "b_crow", [PART, 2, D])
            inv = self.sb(s, "b_cinv", [PART, CTX])
            tmp = self.sb(s, "b_ctmp", [PART, 2, CTX])
            rp = self.sb(s, "b_rp", [HEADS * RPB_R, PART])
            z = p.dve(lambda e: e.memset(rp[:], 0.0))
            got = self.t_misc.start(p.sp, crow[:], i["ctx_2"].rearrange("a (n p) c -> p (a n) c", p=PART))
            for c in range(DC):
                for n in range(2):
                    done = p.pe(lambda e: e.transpose(ps[:, c // 2, (c % 2) * 256 + n * PART:(c % 2) * 256 + (n + 1) * PART],
                                                      crow[:, n, c * PART:(c + 1) * PART], self.ident[:]), after=got,
                                mark=(c == DC - 1 and n == 1))
            p.act(lambda e: e.activation(hc[:].rearrange("p (b c) t -> p b (c t)", b=4), ps[:, 0:4, :], ACTF.Copy), after=done)
            a = self.t_st.start(p.sp, rp[:, 48:48 + RPB_C], i["rpb_2"].rearrange("a h r c -> (a h r) c"), after=z)
            self.t_st.start(p.sp, rpb_dram.rearrange("h r q c -> (h r) q c"), bass_rep(rp[:], GRID), after=a)
            self.rms_inverse(lambda c: hc[:, c, :], DC, D, inv[:], tmp, tokens=CTX)
            self.modulated(lambda c: hc[:, c, :], lambda c: hc[:, c, :], inv[:], 1, 0, 1)
            p.meet()
            self.gemm(lambda g: w_in[:, bass.ds(g * 256 + 512, 256)], DC, 2, 2, lambda k, h: hc[:, k, :],
                      lambda n, bank, done: [p.act(lambda e: e.activation(kc[:, n, :], bank[:, 0, 0:CTX], ACTF.Copy), after=done)],
                      tokens=CTX)
            p.meet()
            values_from(hc, CTX // PART, lambda n: vc[:, n, :], [])
            p.meet(self.t_st.here())
        self.dump("d_kc", kc[:])
        conv_dram = nc.dram_tensor("conv_dram", (PART, 4, TOK), F32, kind="Internal").ap()
        with ExitStack() as s:
            self.weight_slots(s)
            swap = self.sb(s, "b_swap", [PART, PART])
            cp = self.sb(s, "b_cp", [PART, 4, TOK + TAPS - 1])
            sg, t1, cos, sin = (Y[:, n, :] for n in range(4))
            rope_read = [None, None]
            for t, n in ((swap[:], "k_swap"), (cos, "k_rope_cos"), (sin, "k_rope_sin")):
                self.t_misc.start(p.sp, t, i[n], after=p.all_done())

            pad = TAPS // 2
            p.dve(lambda e: e.memset(cp[:, :, 0:pad], 0.0))
            p.dve(lambda e: e.memset(cp[:, :, pad + TOK:], 0.0))

            def glu(g, b, bank, done):
                if b == 0:
                    return [p.act(lambda e: e.activation(two(sg), bank, ACTF.Sigmoid), after=[done, p.dve.counter.here()])]
                return [p.dve(lambda e: e.tensor_tensor(two(cp[:, g, pad:pad + TOK]), two(sg), bank, ALU.mult),
                              after=[done, p.act.counter.here()])]

            free = self.gemm(lambda g: [w_in[:, bass.ds(g * PART + 2048, PART)], w_in[:, bass.ds(g * PART + 1536, PART)]], DC, 4, 2, rhs,
                             glu, split=True)

            def conv(n, last):
                o = Y[:, bass.ds(n + 4, 1), :].rearrange("p a t -> p (a t)")
                x = cp[:, bass.ds(n, 1), :].rearrange("p a t -> p (a t)")
                p.dve(lambda e: e.tensor_scalar(o, x[:, 0:TOK], self.col("dw", n), self.col("dw_bias_2", n), ALU.mult, ALU.add))
                for w in range(1, TAPS):
                    p.dve(lambda e: e.scalar_tensor_tensor(out=o, in0=x[:, w:w + TOK], scalar=self.col("dw", n + 4 * w), in1=o,
                                                           op0=ALU.mult, op1=ALU.add))

            p.loop(4, conv)

            def qk(n, bank, done):
                dst = q[:, n, :] if self.which == 0 else kr[:, n, :]
                return [p.act(lambda e: e.activation(two(dst), bank, ACTF.Copy), after=done)]

            for self.which in range(2):
                self.gemm(lambda g: w_in[:, bass.ds(g * 256 + 512 * self.which, 256)], DC, 2, 2, rhs, qk,
                          start=free + [p.pe.counter.here(), p.act.counter.here()])
            mean, inv, tmp = qr[:, 0, :], qr[:, 1, :], qr[:, 2:4, :]
            added = [None, None]

            def squares():
                for h in range(HEADS):
                    src = bass.AP(tensor=rpb_dram.tensor, offset=h * RPB_R * GRID * PART + GRID - 1,
                                  ap=[[PART - 1, GRID], [GRID * PART, RPB_R], [1, GRID]])
                    H = (h % 2) * 64
                    self.t_st.start(p.sp, bias[H:H + 64, h // 2, :, :], src)
                p.dve(lambda e: e.tensor_tensor(mean, Y[:, 4, :], Y[:, 5, :], ALU.add))
                p.dve(lambda e: e.tensor_tensor(mean, mean, Y[:, 6, :], ALU.add))
                m = p.dve(lambda e: e.tensor_tensor(mean, mean, Y[:, 7, :], ALU.add))
                for h in range(2):
                    done = p.pe(lambda e: e.matmul(ps[:, 6 + h, :], self.ones[:], mean[:, h * HALF:(h + 1) * HALF], start=True, stop=True), after=m,
                                mark=(h == 1))
                for c in range(4):
                    y, sq = Y[:, 4 + c, :], inv if c == 0 else tmp[:, c % 2, :]
                    m = p.dve(lambda e: e.scalar_tensor_tensor(out=two(y), in0=ps[:, 6:8, :], scalar=-1.0 / RW, in1=two(y), op0=ALU.mult, op1=ALU.add),
                              after=done)
                    squared = p.act(lambda e: e.activation(sq, y, ACTF.Square), after=[m, added[c % 2]])
                    if c:
                        added[c % 2] = p.dve(lambda e: e.tensor_tensor(inv, inv, sq, ALU.add), after=squared)

            def layer_norm():
                sums = self.token_sums(inv, self.ones[:, 0:2], 0, added)
                m = self.rsqrt_small(2 * NBLK, sums, ALU.mult, 1.0 / RW, ALU.add, 1e-6)
                over = self.over_channels(self.st[:, 1, 0:2 * NBLK].rearrange("p (b two) -> p b two", two=2)[:, :, 0:1], tmp[:, 0, :], m)
                for c in range(4):
                    y = Y[:, 4 + c, :]
                    p.dve(lambda e: e.tensor_tensor(two(y), two(y), ps[:, 6:8, :], ALU.mult), after=over)
                    m = p.dve(lambda e: e.tensor_scalar(y, y, self.col("conv_ln_g_2", c), self.col("conv_ln_b_2", c), ALU.mult, ALU.add))
                    p.act(lambda e: e.activation(y, y, ACTF.Silu), after=m)

            values_from(hxA, NBLK, lambda n: VV[:, 2 * n, :], free, squares)
            layer_norm()
            self.t_misc.start(p.sp, VV[0:64, 1:ROWS - 1:2, :], VV[64:128, 0:ROWS - 2:2, :], after=p.act.counter.here())
            self.t_misc.start(p.sp, VV[64:128, 1:ROWS - 1:2, :], VV[0:64, 2:ROWS - 1:2, :])
            p.pe.wait([self.t_misc.here(), p.act.counter.here()])
            for c in range(8):
                src, dst = (q[:, c, :], qr[:, c, :]) if c < 4 else (kr[:, c - 4, :], kr[:, c - 4, :])
                base = 4 + 2 * (c % 2)
                for h in range(2):
                    done = p.pe(lambda e: e.matmul(ps[:, base + h, :], swap[:], src[:, h * HALF:(h + 1) * HALF], start=True, stop=True),
                                after=rope_read[c % 2], mark=(h == 1))
                p.dve(lambda e: e.tensor_tensor(two(t1), ps[:, base:base + 2, :], two(sin), ALU.mult), after=[done, self.t_misc.here()])
                p.dve(lambda e: e.tensor_tensor(dst, src, cos, ALU.mult))
                rope_read[c % 2] = p.dve(lambda e: e.tensor_tensor(dst, dst, t1, ALU.add))
            p.meet()
        self.dump("d_conv", Y[:, 4:8, :])
        self.dump("d_qr", qr[:])
        self.dump("d_kr", kr[:])
        self.attention(q, qr, kr, VV, kc, vc, Y, bias)
        st.close()

    def attention(self, q, qr, kr, VV, kc, vc, Y, bias):
        p, i, nc, ps = self.p, self.i, self.nc, self.ps
        SC = 64 ** -0.5
        K8 = WIN_R * GRID
        with ExitStack() as s:
            cmask = self.sb(s, "a_cmask", [PART, GRID])
            eye = self.sb(s, "a_eye", [PART, CH])
            Qb = self.sb(s, "a_Qb", [PART, 8, PART])
            Qc = self.sb(s, "a_Qc", [PART, 8, PART])
            sc = [self.sb(s, f"a_sc{n}", [PART, K8 + CTX]) for n in range(2)]
            P_ = [self.sb(s, f"a_P{n}", [PART, K8 + CTX]) for n in range(2)]
            PT = [self.sb(s, f"a_PT{n}", [PART, K8 + CTX]) for n in range(2)]
            ob = self.sb(s, "a_ob", [PART, 8, PART])
            mx = self.sb(s, "a_mx", [PART, 8])
            sm = self.sb(s, "a_sm", [PART, 8])
            self.t_misc.start(p.sp, cmask[:], i["k_col_mask"])
            self.t_misc.start(p.sp, eye[:], i["k_stack_eye"])
            for t in (Qb, Qc, ob):
                p.dve(lambda e: e.memset(t[:], 0.0), chain=False)
            p.meet(self.t_misc.here(), self.t_st.here())
            for pr in range(4):
                p.dve(lambda e: e.tensor_tensor(bias[:, pr], bias[:, pr], bass_rep(cmask[:], RPB_R), ALU.add))
            p.meet()
            HS = [slice(0, 64), slice(64, 128)]

            def rows(r, windows):
                pe, act, dve = p.pe, p.act, p.dve
                T = [bass.ds(r * GRID + n * GRID, GRID) for n in range(2)]
                before = p.all_done()
                dve.wait(before)
                act.wait(before)
                pe.wait(before)
                qd, qa = [None, None], [None, None]
                for n in range(2):
                    for H in HS:
                        qd[n] = dve(lambda e: e.tensor_copy(Qb[H, 4 * n:4 * n + 4, H], qr[H, :, T[n]]), chain=False)
                        qa[n] = act(lambda e: e.activation(Qc[H, 4 * n:4 * n + 4, H], q[H, :, T[n]], ACTF.Copy), chain=False)
                got, read, high, exped, turned, moved, out, spread = ({} for _ in range(8))

                def scores(u):
                    b = 2 * (u % 2)
                    key = windows[u // 4][0] * GRID
                    pe.wait([qd[u // 4], qa[u // 4], read.get(u - 2)])
                    pe(lambda e: e.matmul(ps[:, b, :], Qb[:, u, :], kr[:, u % 4, bass.ds(key, K8)], start=True, stop=True))
                    got[u] = pe(lambda e: e.matmul(ps[:, b + 1, 0:CTX], Qc[:, u, :], kc[:, u % 4, :], start=True, stop=True), mark=True)

                def softmax(u):
                    b, x = 2 * (u % 2), u % 2
                    off = windows[u // 4][1]
                    c = act(lambda e: e.activation(sc[x][:, K8:], ps[:, b + 1, 0:CTX], ACTF.Copy, scale=SC), after=[got[u], exped.get(u - 2)], chain=False)
                    w = dve(lambda e: e.scalar_tensor_tensor(
                        out=sc[x][:, 0:K8].rearrange("p (r c) -> p r c", c=GRID), in0=ps[:, b, :].rearrange("p (r c) -> p r c", c=GRID), scalar=SC,
                        in1=bias[:, u % 4, bass.ds(off, WIN_R), :], op0=ALU.mult, op1=ALU.add), after=[got[u], exped.get(u - 2)], chain=False)
                    read[u] = [c, w]
                    high[u] = dve(lambda e: e.tensor_reduce(mx[:, u:u + 1], sc[x][:], AX.X, ALU.max, negate=True), after=[w, c], chain=False)

                def exps(u):
                    x = u % 2
                    exped[u] = act(lambda e: e.activation(P_[x][:], sc[x][:], ACTF.Exp, bias=mx[:, u:u + 1], accum_out=sm[:, u:u + 1]),
                                   after=[high[u], turned.get(u - 2)], chain=False)

                def turn_probs(u):
                    x = u % 2
                    pe.wait([exped[u], moved.get(u - 1)])
                    for j in range(6):
                        turned[u] = pe(lambda e: e.transpose(ps[:, 4 + j // 4, (j % 4) * PART:(j % 4 + 1) * PART], P_[x][:, j * PART:(j + 1) * PART],
                                                             self.ident[:]), mark=(j == 5))
                    a = act(lambda e: e.activation(PT[x][:, 0:512], ps[:, 4, :], ACTF.Copy), after=[turned[u], out.get(u - 2)], chain=False)
                    d = dve(lambda e: e.tensor_copy(PT[x][:, 512:], ps[:, 5, 0:256]), after=[turned[u], out.get(u - 2)], chain=False)
                    moved[u] = [a, d]

                def values(u):
                    x, pr = u % 2, u % 4
                    rs = windows[u // 4][0]
                    pe.wait([moved[u], spread.get(0) if u == 4 else None])
                    for j in range(6):
                        v = VV[:, bass.ds(rs + 2 * j, 1), pr * PART:(pr + 1) * PART].rearrange("p a b -> p (a b)") if j < 4 \
                            else vc[:, j - 4, pr * PART:(pr + 1) * PART]
                        out[u] = pe(lambda e: e.matmul(ps[:, 6, pr * PART:(pr + 1) * PART], PT[x][:, j * PART:(j + 1) * PART], v,
                                                       start=(j == 0), stop=(j == 5)), mark=(j == 5))

                def normalise(n):
                    m = dve(lambda e: e.reciprocal(sm[:, 4 * n:4 * n + 4], sm[:, 4 * n:4 * n + 4]), after=exped[4 * n + 3], chain=False)
                    o6 = ps[:, 6, :].rearrange("p (u c) -> p u c", u=4)
                    for H in HS:
                        spread[n] = dve(lambda e: e.tensor_tensor(ob[H, 4 * n:4 * n + 4, H], o6[H, :, H],
                                                                  sm[H, 4 * n:4 * n + 4].unsqueeze(2).to_broadcast([64, 4, 64]), ALU.mult),
                                        after=[m, out[4 * n + 3]], chain=False)

                def fold(n):
                    pe.wait(spread[n])
                    for u in range(4):
                        f = pe(lambda e: e.matmul(ps[:, 7, (4 * n + u) * GRID:(4 * n + u + 1) * GRID], ob[:, 4 * n + u, :], eye[:],
                                                  start=True, stop=True), mark=(u == 3))
                    act(lambda e: e.activation(Y[:, 0:4, T[n]], ps[:, 7, 256 * n:256 * n + 256].rearrange("p (u c) -> p u c", u=4), ACTF.Copy),
                        after=f, chain=False)

                scores(0)
                scores(1)
                softmax(0)
                exps(0)
                for u in range(8):
                    if u < 7:
                        softmax(u + 1)
                    if u < 6:
                        scores(u + 2)
                    if u:
                        values(u - 1)
                    if u == 4:
                        normalise(0)
                    turn_probs(u)
                    if u < 7:
                        exps(u + 1)
                    if u == 5:
                        fold(0)
                values(7)
                normalise(1)
                fold(1)

            lo, hi = WIN_R // 2, ROWS - WIN_R // 2
            top = WIN_R - 1
            p.loop(lo // 2, lambda t, last: rows(t * 2, [(0, t * -2 + top), (0, t * -2 + (top - 1))]))
            p.loop((hi - lo) // 2, lambda t, last: rows(t * 2 + lo, [(t * 2, top - lo), (t * 2 + 1, top - lo)]))
            p.loop((ROWS - hi) // 2, lambda t, last: rows(t * 2 + hi, [(ROWS - WIN_R, t * -2 + (top - lo)), (ROWS - WIN_R, t * -2 + (top - lo - 1))]))
            p.meet()
        self.dump("d_attn", Y[:, 0:4, :])

    def block2(self):
        p, i, ps = self.p, self.i, self.ps
        two = lambda x: x.rearrange("p (h t) -> p h t", h=2)
        st = ExitStack()
        self.ada(st)
        A = self.sb(st, "A2", [PART, DC, TOK])
        with ExitStack() as s:
            Y = self.sb(s, "Y2", [PART, DC, TOK])
            with ExitStack() as s2:
                inv = self.sb(s2, "b2_inv", [PART, TOK])
                tmp = self.sb(s2, "b2_tmp", [PART, 2, TOK])
                h = Y
                p.dve.wait(self.t_h.start(p.sp, h[:], self.h_dram, after=p.all_done()))
                p.act.wait(self.t_h.here())
                self.rms_inverse(lambda c: h[:, c, :], DC, D, inv[:], tmp)
                self.modulated(lambda c: A[:, c, :], lambda c: h[:, c, :], inv[:], 0, 0, 0)
                p.meet()
            self.dump("d_hx", A[:])
            self.block2_mixers(A, Y)
            self.weight_slots(s)
            h = A
            loaded = self.t_h.start(p.sp, h[:], self.h_dram, after=p.all_done())
            p.dve.wait(loaded)
            w = i["w_out_2"][0]

            def mix_out(n, bank, done):
                g1 = self.mod[:, 16 + n, 0:1] if isinstance(n, int) else self.mod[:, bass.ds(n + 16, 1), 0]
                return [p.dve(lambda e: e.scalar_tensor_tensor(out=two(h[:, n, :]), in0=bank, scalar=g1, in1=two(h[:, n, :]),
                                                               op0=ALU.mult, op1=ALU.add), after=done)]

            self.gemm(lambda g: w[:, bass.ds(g * 256, 256)], DC, 4, 2, lambda k, hh: Y[:, k, hh * HALF:(hh + 1) * HALF], mix_out)
            p.meet()
        self.dump("d_h4", A[:])
        with ExitStack() as s:
            xh, xl = (self.sb(s, n, [PART, DC, TOK], F32R) for n in ("hx2_h", "hx2_l"))

            def norm():
                with ExitStack() as s2:
                    inv = self.sb(s2, "m_inv", [PART, TOK])
                    tmp = self.sb(s2, "m_tmp", [PART, 2, TOK])
                    self.rms_inverse(lambda c: A[:, c, :], DC, D, inv[:], tmp)
                    parted = [None, None]
                    for c in range(DC):
                        t = tmp[:, c % 2, :]
                        m = p.dve(lambda e: e.scalar_tensor_tensor(out=t, in0=A[:, c, :], scalar=self.gain[:, 2, c:c + 1], in1=inv[:],
                                                                   op0=ALU.mult, op1=ALU.mult), after=parted[c % 2])
                        m = p.act(lambda e: e.activation(t, t, ACTF.Identity, bias=self.mod[:, 24 + c, 0:1]), after=m)
                        parted[c % 2] = self.in_two_parts(xh[:, c, :], xl[:, c, :], t, m)
                    p.meet()

            w1, w2 = i["w_mlp1_2"][0], i["w_mlp2_2"][0]
            act_g, act_h = (self.sb(s, n, [PART, TOK]) for n in ("relu", "relu2"))

            def relu2(b, bank, done, reader):
                f = p.act(lambda e: e.activation(two(act_g[:]), bank, ACTF.Relu), after=[done, *reader])
                m = p.dve(lambda e: e.tensor_tensor(act_h[:], act_g[:], act_g[:], ALU.mult), after=f)
                return act_h[:], m, f

            def add_gated(n, bank, done):
                return p.dve(lambda e: e.scalar_tensor_tensor(out=two(A[:, n, :]), in0=bank, scalar=self.mod[:, 40 + n, 0:1],
                                                              in1=two(A[:, n, :]), op0=ALU.mult, op1=ALU.add), after=done)

            self.fused_mlp(s, DFF2 // PART, lambda g: [w1[:, bass.ds(g * PART, PART)]],
                           lambda g: w2[bass.ds(g * PART, PART), :], norm, (xh, xl), relu2, add_gated)
            p.meet()
        with ExitStack() as s:
            h = A
            inv = self.sb(s, "l_inv", [PART, TOK])
            tmp = self.sb(s, "l_tmp", [PART, 2, TOK])
            row = [self.sb(s, f"o_row{n}", [PART, D]) for n in range(2)]
            self.rms_inverse(lambda c: h[:, c, :], DC, D, inv[:], tmp)
            self.normed(lambda c: h[:, c, :], lambda c: h[:, c, :], inv[:], "final_g")
            out = self.out.rearrange("b (n p) c -> n p (b c)", p=PART)
            p.meet()
            t_out = [Transfer(p, "t_out0"), Transfer(p, "t_out1")]
            copied = [None, None]
            for t in range(NBLK):
                x = t % 2
                for c in range(DC):
                    done = p.pe(lambda e: e.transpose(ps[:, 2 * x + c // 4, (c % 4) * PART:(c % 4 + 1) * PART], h[:, c, t * PART:(t + 1) * PART],
                                                      self.ident[:]), after=copied[x] if c == 0 else None, mark=(c == DC - 1))
                copied[x] = p.act(lambda e: e.activation(two(row[x][:]), ps[:, 2 * x:2 * x + 2, :], ACTF.Copy), after=[done, t_out[x].here()])
                t_out[x].start(p.sp, out[t], row[x][:], after=copied[x])
            p.meet(t_out[0].here(), t_out[1].here())
        st.close()

    def block1(self):
        with ExitStack() as s:
            B = self.sb(s, "B1", [PART, DC, TOK])
            A_room = ExitStack()
            A = self.sb(A_room, "A1", [PART, DC, TOK])
            with ExitStack() as s2:
                self.load_x(A, s2)
            self.gla(A, B)
            self.rwkv(A, B)
            self.block1_tail(A, B, A_room)


def flat_list(x):
    return [x] if isinstance(x, Done) else [d for y in x for d in flat_list(y)]


def bass_rep(ap, n):
    return ap.unsqueeze(1).to_broadcast([ap.shape[0], n] + list(ap.shape[1:]))


def rep_mid(ap, n):
    return ap.unsqueeze(2).to_broadcast([ap.shape[0], ap.shape[1], n, ap.shape[2]])


def rep_last(ap, n):
    return ap.to_broadcast([ap.shape[0], ap.shape[1], n])


def kernel(**inputs):
    import concourse.bacc as bacc
    from concourse.bass_utils import run_bass_kernel_spmd

    nc = bacc.Bacc("TRN2", target_bir_lowering=False, num_devices=1)
    given = {name: np.ascontiguousarray(a) for name, a in inputs.items()}
    given.update({f"k_{name}": a for name, a in constants().items()})
    ins, arrays = {}, {}
    for name, a in given.items():
        arrays[f"in_{name}_dram"] = a
        ins[name] = nc.dram_tensor(f"in_{name}_dram", a.shape, F32, kind="ExternalInput").ap()
    out = nc.dram_tensor("out_dram", (1, TOK, D), F32, kind="ExternalOutput").ap()
    k = Kernel(nc, ins, out)
    with ExitStack() as stack:
        k.setup(stack)
        k.block1()
        k.block2()
    r = run_bass_kernel_spmd(nc, [arrays], core_ids=[0])
    return r.results[0]["out_dram"]
```
